# Optimizing a Trainium2 kernel written in Bass

```python
import math
import jax, jax.numpy as jnp
from jax import lax
import numpy as np

D_MODEL = 1024
BATCH = 1
SEQ = 512
DEPTH = 1

CTX_LEN = 256
GRID_W = 64
CHUNK = 128
ROWS_PER_CHUNK = CHUNK // GRID_W
EPS = 1e-6

SSD_HEAD_DIM = 64
SSD_HEADS = D_MODEL // SSD_HEAD_DIM
SSD_WIDTH = SSD_HEADS * SSD_HEAD_DIM
SSD_GROUPS = 4
SSD_STATE = 128
SSD_CONV = 3
DT_MIN = 0.001
DT_MAX = 0.1
GN = SSD_GROUPS * SSD_STATE
N_XBC = SSD_WIDTH + 2 * GN
N_SCAN = N_XBC + 2 * SSD_HEADS

MLP_WIDTH = D_MODEL
MLP_GROUP_DIM = 128
MLP_GROUPS = MLP_WIDTH // MLP_GROUP_DIM

N_IN = N_SCAN + SSD_WIDTH + 2 * MLP_WIDTH + 2 * D_MODEL

N_EXPERTS = 16
EXPERT_FF = D_MODEL
CAPACITY_FACTOR = 2


def split_cols(p, sizes):
    idx = np.cumsum(sizes)[:-1].tolist()
    return jnp.split(p, idx, axis=-1)

def rmsnorm(x, w):
    xf = x.astype(jnp.float32)
    y = xf * lax.rsqrt(jnp.mean(xf * xf, axis=-1, keepdims=True) + EPS)
    return (y * w.astype(jnp.float32)).astype(x.dtype)

def layernorm(x, w, b):
    xf = x.astype(jnp.float32)
    mu = jnp.mean(xf, axis=-1, keepdims=True)
    var = jnp.mean(jnp.square(xf - mu), axis=-1, keepdims=True)
    y = (xf - mu) * lax.rsqrt(var + EPS)
    return (y * w.astype(jnp.float32) + b.astype(jnp.float32)).astype(x.dtype)

def dwconv_centred(x, w, b):
    ch = x.shape[-1]
    k = w.shape[0]
    y = lax.conv_general_dilated(x, w[:, None, :].astype(x.dtype), window_strides=(1,),
                                 padding=[(k // 2, k // 2)],
                                 dimension_numbers=('NWC', 'WIO', 'NWC'),
                                 feature_group_count=ch)
    return y + b.astype(x.dtype)

def ssd_chunked(xh, dt, A, bm, cm, h0):
    b, l, H, P = xh.shape
    G, N = bm.shape[2], bm.shape[3]
    R = H // G
    nc = l // CHUNK
    x = xh.reshape(b, nc, CHUNK, G, R, P)
    dt_c = dt.reshape(b, nc, CHUNK, G, R)
    a_cum = jnp.cumsum(dt_c * A.reshape(G, R), axis=2)
    Bc = bm.reshape(b, nc, CHUNK, G, N)
    Cc = cm.reshape(b, nc, CHUNK, G, N)
    xdt = x * dt_c[..., None].astype(x.dtype)
    lower = jnp.tril(jnp.ones((CHUNK, CHUNK), dtype=bool))[None, None, :, :, None, None]
    seg = a_cum[:, :, :, None] - a_cum[:, :, None, :]
    decay = jnp.exp(jnp.where(lower, seg, -jnp.inf))
    cb = jnp.einsum('bcign,bcjgn->bcijg', Cc, Bc)
    y_diag = jnp.einsum('bcijg,bcijgr,bcjgrp->bcigrp', cb, decay, xdt)
    decay_to_end = jnp.exp(a_cum[:, :, -1:] - a_cum)
    states = jnp.einsum('bcjgn,bcjgr,bcjgrp->bcgrpn', Bc, decay_to_end, xdt)
    chunk_decay = jnp.exp(a_cum[:, :, -1])

    def step(h, inp):
        st, dcy = inp
        return h * dcy[..., None, None] + st, h

    h_final, h_in = lax.scan(step, h0, (jnp.moveaxis(states, 1, 0).astype(jnp.float32),
                                        jnp.moveaxis(chunk_decay, 1, 0)))
    y_off = jnp.einsum('bcign,bcigr,cbgrpn->bcigrp', Cc, jnp.exp(a_cum), h_in)
    y = (y_diag + y_off).reshape(b, l, H, P).astype(xh.dtype)
    return y, h_final

def ssd_scan_bidir(p_scan, conv_w, conv_b, dt_bias, a_log, h0_f, h0_b):
    xbc, dt_raw = p_scan[..., :N_XBC], p_scan[..., N_XBC:]
    xbc = jax.nn.silu(dwconv_centred(xbc, conv_w, conv_b))
    xs, bm, cm = split_cols(xbc, [SSD_WIDTH, GN, GN])
    b, l, _ = xs.shape
    xh = xs.reshape(b, l, SSD_HEADS, SSD_HEAD_DIM)
    bm = bm.reshape(b, l, SSD_GROUPS, SSD_STATE)
    cm = cm.reshape(b, l, SSD_GROUPS, SSD_STATE)
    dt = jax.nn.softplus(dt_raw.astype(jnp.float32).reshape(b, l, 2, SSD_HEADS)
                         + dt_bias.astype(jnp.float32))
    A = -jnp.exp(a_log.astype(jnp.float32))
    y_f, st_f = ssd_chunked(xh, dt[:, :, 0], A[0], bm, cm, h0_f)
    rev = lambda t: jnp.flip(t, axis=1)
    y_b, st_b = ssd_chunked(rev(xh), rev(dt[:, :, 1]), A[1], rev(bm), rev(cm), h0_b)
    return y_f + rev(y_b), xh, st_f, st_b

def ssd_output(y, xh, z, d_skip, norm_w):
    b, l, H, P = xh.shape
    y = y + d_skip.astype(xh.dtype)[:, None] * xh
    g = y.reshape(b, l, SSD_WIDTH) * jax.nn.silu(z)
    g = rmsnorm(g.reshape(b, l, SSD_GROUPS, SSD_WIDTH // SSD_GROUPS),
                norm_w.reshape(SSD_GROUPS, SSD_WIDTH // SSD_GROUPS))
    return g.reshape(b, l, SSD_WIDTH)

def spatial_gating(u, v, n_chunks, ln_w, ln_b, w_s, b_s):
    b, l, _ = v.shape
    v = layernorm(v, ln_w, ln_b)
    vc = v.reshape(b, n_chunks, CHUNK, MLP_GROUPS, MLP_GROUP_DIM)
    mixed = jnp.einsum('gij,bcjgd->bcigd', w_s, vc) + b_s.T[None, None, :, :, None]
    return u * mixed.reshape(b, l, MLP_WIDTH)

def mixer_out(y, xh, p_rest, n_chunks, d_skip, ssd_norm_w, ln_w, ln_b, w_s, b_s, w_pa, w_pb, w_o):
    z, uv, gate_a, gate_b = split_cols(p_rest, [SSD_WIDTH, 2 * MLP_WIDTH, D_MODEL, D_MODEL])
    ssd = ssd_output(y, xh, z, d_skip, ssd_norm_w)
    u, v = jnp.split(jax.nn.gelu(uv), 2, axis=-1)
    sgu = spatial_gating(u, v, n_chunks, ln_w, ln_b, w_s, b_s)
    merged = jax.nn.sigmoid(gate_a) * (ssd @ w_pa) + jax.nn.sigmoid(gate_b) * (sgu @ w_pb)
    return merged @ w_o

def expert_choice_ffn(xn, router_w, w_gate, w_up, w_down):
    b, n, d = xn.shape
    cap = CAPACITY_FACTOR * n // N_EXPERTS
    logits = jnp.einsum('bnd,de->ben', xn, router_w).astype(jnp.float32)
    aff = jax.nn.softmax(logits, axis=1)
    gate, idx = lax.top_k(aff, cap)
    xg = jax.vmap(lambda xs, ix: xs[ix])(xn, idx)
    hid = jax.nn.silu(jnp.einsum('becd,edf->becf', xg, w_gate)) * jnp.einsum('becd,edf->becf', xg, w_up)
    y = jnp.einsum('becf,efd->becd', hid, w_down) * gate[..., None].astype(xn.dtype)
    scatter = lambda ix, ys: jnp.zeros((n, d), ys.dtype).at[ix.reshape(-1)].add(ys.reshape(-1, d))
    return jax.vmap(scatter)(idx, y)

def first_inputs(seed: int = 0) -> dict:
    key = jax.random.key(seed)
    ks = jax.random.split(key, 32)
    f32 = jnp.float32
    L = DEPTH
    nrm = lambda k, shape, s: jax.random.normal(k, shape, f32) * s
    gain = lambda k, shape: 1.0 + 0.01 * jax.random.normal(k, shape, f32)
    dt0 = jnp.exp(jax.random.uniform(ks[12], (L, 2, SSD_HEADS), f32, math.log(DT_MIN), math.log(DT_MAX)))
    return {
        'x': nrm(ks[0], (BATCH, SEQ, D_MODEL), 1.0),
        'c': nrm(ks[1], (BATCH, D_MODEL), 1.0),
        'ctx': nrm(ks[2], (BATCH, CTX_LEN, D_MODEL), 1.0),
        'c_ctx': nrm(ks[3], (D_MODEL,), 1.0),
        'ada_w': nrm(ks[4], (L, D_MODEL, 6 * D_MODEL), 0.5 * D_MODEL ** -0.5),
        'ada_b': nrm(ks[5], (L, 6 * D_MODEL), 0.01),
        'norm1_w': gain(ks[6], (L, D_MODEL)),
        'norm2_w': gain(ks[7], (L, D_MODEL)),
        'w_in': nrm(ks[8], (L, D_MODEL, N_IN), D_MODEL ** -0.5),
        'conv_w': nrm(ks[9], (L, SSD_CONV, N_XBC), SSD_CONV ** -0.5),
        'conv_b': nrm(ks[10], (L, N_XBC), 0.01),
        'dt_bias': dt0 + jnp.log(-jnp.expm1(-dt0)),
        'a_log': jnp.log(jax.random.uniform(ks[13], (L, 2, SSD_HEADS), f32, 1.0, 16.0)),
        'd_skip': gain(ks[14], (L, SSD_HEADS)),
        'ssd_norm_w': gain(ks[15], (L, SSD_WIDTH)),
        'sgu_ln_w': gain(ks[16], (L, MLP_WIDTH)),
        'sgu_ln_b': nrm(ks[17], (L, MLP_WIDTH), 0.01),
        'w_s': nrm(ks[18], (L, MLP_GROUPS, CHUNK, CHUNK), CHUNK ** -0.5),
        'b_s': gain(ks[19], (L, MLP_GROUPS, CHUNK)),
        'w_pa': nrm(ks[20], (L, SSD_WIDTH, D_MODEL), SSD_WIDTH ** -0.5),
        'w_pb': nrm(ks[21], (L, MLP_WIDTH, D_MODEL), MLP_WIDTH ** -0.5),
        'w_o': nrm(ks[22], (L, D_MODEL, D_MODEL), D_MODEL ** -0.5),
        'router_w': nrm(ks[23], (L, D_MODEL, N_EXPERTS), D_MODEL ** -0.5),
        'w_gate': nrm(ks[24], (L, N_EXPERTS, D_MODEL, EXPERT_FF), D_MODEL ** -0.5),
        'w_up': nrm(ks[25], (L, N_EXPERTS, D_MODEL, EXPERT_FF), D_MODEL ** -0.5),
        'w_down': nrm(ks[26], (L, N_EXPERTS, EXPERT_FF, D_MODEL), EXPERT_FF ** -0.5),
        'final_norm_w': gain(ks[27], (D_MODEL,)),
    }

def first_block(x, c, ctx, c_ctx, ada_w, ada_b, norm1_w, norm2_w, w_in, conv_w, conv_b, dt_bias, a_log,
              d_skip, ssd_norm_w, sgu_ln_w, sgu_ln_b, w_s, b_s, w_pa, w_pb, w_o, router_w,
              w_gate, w_up, w_down, final_norm_w):
    bsz, n_lat, _ = x.shape
    rows = n_lat // GRID_W
    lat_chunks = rows // ROWS_PER_CHUNK
    ctx_chunks = ctx.shape[1] // CHUNK
    h0 = jnp.zeros((bsz, SSD_GROUPS, SSD_HEADS // SSD_GROUPS, SSD_HEAD_DIM, SSD_STATE), jnp.float32)
    h, hc = x, ctx
    for layer in range(DEPTH):
        last = layer == DEPTH - 1
        mod_l = (jax.nn.silu(c) @ ada_w[layer] + ada_b[layer])[:, None, :]
        mod_c = (jax.nn.silu(c_ctx) @ ada_w[layer] + ada_b[layer])[None, None, :]
        sh1_l, sc1_l, g1_l, sh2_l, sc2_l, g2_l = jnp.split(mod_l, 6, axis=-1)
        sh1_c, sc1_c, g1_c, sh2_c, sc2_c, g2_c = jnp.split(mod_c, 6, axis=-1)
        w_in_l = w_in[layer]
        mix_args = (d_skip[layer], ssd_norm_w[layer], sgu_ln_w[layer], sgu_ln_b[layer],
                    w_s[layer], b_s[layer], w_pa[layer], w_pb[layer], w_o[layer])
        xm_c = rmsnorm(hc, norm1_w[layer]) * (1 + sc1_c) + sh1_c
        xm_l = rmsnorm(h, norm1_w[layer]) * (1 + sc1_l) + sh1_l
        y_c, xh_c, st_f, st_b = ssd_scan_bidir(xm_c @ w_in_l[:, :N_SCAN], conv_w[layer], conv_b[layer],
                                               dt_bias[layer], a_log[layer], h0, h0)
        p_l = xm_l @ w_in_l
        y_l, xh_l, _, _ = ssd_scan_bidir(p_l[..., :N_SCAN], conv_w[layer], conv_b[layer],
                                         dt_bias[layer], a_log[layer], st_f, st_b)
        h = h + g1_l * mixer_out(y_l, xh_l, p_l[..., N_SCAN:], lat_chunks, *mix_args)
        if not last:
            hc = hc + g1_c * mixer_out(y_c, xh_c, xm_c @ w_in_l[:, N_SCAN:], ctx_chunks, *mix_args)
        moe_args = (router_w[layer], w_gate[layer], w_up[layer], w_down[layer])
        xf_l = rmsnorm(h, norm2_w[layer]) * (1 + sc2_l) + sh2_l
        h = h + g2_l * expert_choice_ffn(xf_l, *moe_args)
        if not last:
            xf_c = rmsnorm(hc, norm2_w[layer]) * (1 + sc2_c) + sh2_c
            hc = hc + g2_c * expert_choice_ffn(xf_c, *moe_args)
    return rmsnorm(h, final_norm_w)


_first_inputs = first_inputs


def first_inputs(seed=0):
    import zlib

    import numpy as np

    out = dict(_first_inputs(seed))
    spreads = {}
    factors = {'ctx': 6.61,
     'c_ctx': 6.049,
     'ada_b': 5.101,
     'norm1_w': 8.0,
     'norm2_w': 8.0,
     'conv_b': 8.0,
     'd_skip': 8.0,
     'ssd_norm_w': 8.0,
     'sgu_ln_w': 8.0,
     'sgu_ln_b': 8.0,
     'b_s': 8.0,
     'final_norm_w': 6.227}
    for name, (base, spread) in spreads.items():
        noise = np.random.default_rng([zlib.crc32(name.encode()), seed]).standard_normal(out[name].shape)
        drawn = base * np.exp(spread * noise) if base else spread * noise
        out[name] = __import__('jax').numpy.asarray(drawn.astype(out[name].dtype))
    for name, factor in factors.items():
        out[name] = (out[name] * factor).astype(out[name].dtype)
    return out


_narrow_inputs = first_inputs


def first_inputs(seed=0):

    out = dict(_narrow_inputs(seed))
    wider = {'conv_b': 12.0,
     'd_skip': 12.0,
     'ssd_norm_w': 12.0,
     'sgu_ln_w': 3.15,
     'b_s': 3.06,
     'final_norm_w': 7.1}
    for name, times in wider.items():
        mean = out[name].mean()
        out[name] = (mean + times * (out[name] - mean)).astype(out[name].dtype)
    return out


DEPTH_2 = 2

NA_HEADS = 8
NA_HEAD_DIM = 64
NA_WIDTH = NA_HEADS * NA_HEAD_DIM
NA_WIN_ROWS = 8
NA_WIN_COLS = 16
NA_COL_BLOCK = NA_WIN_COLS
NA_KEY_COL_BLOCK = 2 * NA_WIN_COLS
DIFF_HEADS = 4
DIFF_HEAD_DIM = 64
DIFF_QK_WIDTH = DIFF_HEADS * 2 * DIFF_HEAD_DIM
DIFF_V_WIDTH = DIFF_HEADS * 2 * DIFF_HEAD_DIM
MLA_HEADS = 8
MLA_NOPE_DIM = 64
MLA_ROPE_DIM = 32
MLA_V_DIM = 64
MLA_Q_RANK = 384
MLA_KV_RANK = 256
MLA_WIDTH = MLA_HEADS * MLA_V_DIM
N_BRANCH = 3
BRANCH_WIDTH = 512
D_IN = 3 * NA_WIDTH + 2 * DIFF_QK_WIDTH + DIFF_V_WIDTH + MLA_Q_RANK + MLA_KV_RANK + MLA_ROPE_DIM + N_BRANCH * D_MODEL
D_FF = -(-8 * D_MODEL // (3 * 256)) * 256
ROPE_THETA = 500000.0
DIFF_ROT_DIM = DIFF_HEAD_DIM // 4
Q_BLOCK = 128
DN_ALPHA = (2 * DEPTH_2) ** 0.25
DN_BETA = (8 * DEPTH_2) ** -0.25
LN_EPS = 1e-5
RMS_EPS = 1e-6


def layer_norm(x, g, b):
    xf = x.astype(jnp.float32)
    mu = jnp.mean(xf, -1, keepdims=True)
    var = jnp.mean(jnp.square(xf - mu), -1, keepdims=True)
    return ((xf - mu) * lax.rsqrt(var + LN_EPS) * g.astype(jnp.float32) + b.astype(jnp.float32)).astype(x.dtype)

def rms_norm(x, g):
    xf = x.astype(jnp.float32)
    return (xf * lax.rsqrt(jnp.mean(xf * xf, -1, keepdims=True) + RMS_EPS) * g.astype(jnp.float32)).astype(x.dtype)

def rope(x, rot_dim):
    s = x.shape[1]
    half = rot_dim // 2
    inv_freq = jnp.exp(-math.log(ROPE_THETA) * jnp.arange(half, dtype=jnp.float32) / half)
    ang = jnp.arange(s, dtype=jnp.float32)[:, None] * inv_freq[None, :]
    cos = jnp.cos(ang)[None, :, None, :]
    sin = jnp.sin(ang)[None, :, None, :]
    xr = x[..., :rot_dim].astype(jnp.float32)
    x1, x2 = xr[..., :half], xr[..., half:]
    rot = jnp.concatenate([x1 * cos - x2 * sin, x2 * cos + x1 * sin], -1).astype(x.dtype)
    return jnp.concatenate([rot, x[..., rot_dim:]], -1)

def blocked_attention(q, k, v, scale):
    b, s, h, dq = q.shape
    nb = s // Q_BLOCK
    qb = q.reshape(b, nb, Q_BLOCK, h, dq).transpose(1, 0, 2, 3, 4)

    def one_block(qi):
        sc = jnp.einsum('bqhd,bkhd->bhqk', qi, k, preferred_element_type=jnp.float32) * scale
        p = jax.nn.softmax(sc, axis=-1).astype(v.dtype)
        return jnp.einsum('bhqk,bkhd->bqhd', p, v)

    out = lax.map(one_block, qb)
    return out.transpose(1, 0, 2, 3, 4).reshape(b, s, h, v.shape[-1])

def neighbourhood_attention(q, k, v, rpb):
    b, s, h, d = q.shape
    rows = s // GRID_W
    kr = min(NA_WIN_ROWS, rows)
    kc = NA_WIN_COLS
    ncb = GRID_W // NA_COL_BLOCK
    qg = q.reshape(b, rows, GRID_W, h, d)
    kg = k.reshape(b, rows, GRID_W, h, d)
    vg = v.reshape(b, rows, GRID_W, h, d)
    qcol = jnp.arange(GRID_W).reshape(ncb, NA_COL_BLOCK)
    kstart = jnp.clip(jnp.arange(ncb) * NA_COL_BLOCK - kc // 2, 0, GRID_W - NA_KEY_COL_BLOCK)
    kcol = kstart[:, None] + jnp.arange(NA_KEY_COL_BLOCK)[None, :]
    wstart = jnp.clip(qcol - kc // 2, 0, GRID_W - kc)
    col_valid = (kcol[:, None, :] >= wstart[:, :, None]) & (kcol[:, None, :] < wstart[:, :, None] + kc)
    dcol_idx = jnp.clip(kcol[:, None, :] - qcol[:, :, None], -(kc - 1), kc - 1) + (kc - 1)
    row_center = NA_WIN_ROWS - 1
    scale = d ** -0.5

    def one_row(r):
        rs = jnp.clip(r - kr // 2, 0, rows - kr)
        qr = lax.dynamic_index_in_dim(qg, r, axis=1, keepdims=False)
        k_rows = lax.dynamic_slice_in_dim(kg, rs, kr, axis=1)
        v_rows = lax.dynamic_slice_in_dim(vg, rs, kr, axis=1)
        kb = jnp.take(k_rows, kcol, axis=2)
        vb = jnp.take(v_rows, kcol, axis=2)
        qb = qr.reshape(b, ncb, NA_COL_BLOCK, h, d)
        sc = jnp.einsum('bnqhd,banchd->bhnqac', qb, kb, preferred_element_type=jnp.float32) * scale
        drow = rs + jnp.arange(kr) - r + row_center
        bias = rpb[:, drow][:, :, dcol_idx].transpose(0, 2, 3, 1, 4)
        sc = sc + bias[None].astype(jnp.float32)
        sc = jnp.where(col_valid[None, None, :, :, None, :], sc, -jnp.inf)
        p = jax.nn.softmax(sc, axis=(-2, -1)).astype(v.dtype)
        o = jnp.einsum('bhnqac,banchd->bnqhd', p, vb)
        return o.reshape(b, GRID_W, h, d)

    out = lax.map(one_row, jnp.arange(rows))
    return out.transpose(1, 0, 2, 3, 4).reshape(b, s, h * d)

def diff_attention(q, k, v, lam_vecs, subln_g, lam_init):
    b, s, _ = q.shape
    q = q.reshape(b, s, DIFF_HEADS, 2, DIFF_HEAD_DIM)
    k = k.reshape(b, s, DIFF_HEADS, 2, DIFF_HEAD_DIM)
    v = v.reshape(b, s, DIFF_HEADS, 2 * DIFF_HEAD_DIM)
    q1, q2 = rope(q[:, :, :, 0], DIFF_ROT_DIM), rope(q[:, :, :, 1], DIFF_ROT_DIM)
    k1, k2 = rope(k[:, :, :, 0], DIFF_ROT_DIM), rope(k[:, :, :, 1], DIFF_ROT_DIM)
    lv = lam_vecs.astype(jnp.float32)
    lam = jnp.exp(jnp.sum(lv[0] * lv[1])) - jnp.exp(jnp.sum(lv[2] * lv[3])) + lam_init
    scale = DIFF_HEAD_DIM ** -0.5
    a1 = blocked_attention(q1, k1, v, scale)
    a2 = blocked_attention(q2, k2, v, scale)
    o = a1 - lam.astype(a1.dtype) * a2
    o = rms_norm(o, subln_g) * (1.0 - lam_init)
    return o.reshape(b, s, DIFF_V_WIDTH)

def latent_attention(c_q, c_kv, k_rope, w_qb, w_kvb, q_norm_g, kv_norm_g):
    b, s, _ = c_q.shape
    q = jnp.einsum('bsr,re->bse', rms_norm(c_q, q_norm_g), w_qb).reshape(b, s, MLA_HEADS, MLA_NOPE_DIM + MLA_ROPE_DIM)
    q = jnp.concatenate([q[..., :MLA_NOPE_DIM], rope(q[..., MLA_NOPE_DIM:], MLA_ROPE_DIM)], -1)
    kv = jnp.einsum('bsr,re->bse', rms_norm(c_kv, kv_norm_g), w_kvb).reshape(b, s, MLA_HEADS, MLA_NOPE_DIM + MLA_V_DIM)
    k_nope, v = kv[..., :MLA_NOPE_DIM], kv[..., MLA_NOPE_DIM:]
    k_r = rope(k_rope[:, :, None, :], MLA_ROPE_DIM)
    k = jnp.concatenate([k_nope, jnp.broadcast_to(k_r, (b, s, MLA_HEADS, MLA_ROPE_DIM))], -1)
    o = blocked_attention(q, k, v, (MLA_NOPE_DIM + MLA_ROPE_DIM) ** -0.5)
    return o.reshape(b, s, MLA_WIDTH)

def second_inputs(seed: int = 0) -> dict:
    key = jax.random.key(seed)
    ks = jax.random.split(key, 20)

    def nrm(k, shape, s):
        return jax.random.normal(k, shape, jnp.float32) * s

    return {
        "x": nrm(ks[0], (BATCH, SEQ, D_MODEL), 1.0),
        "ln_in_g": 1.0 + nrm(ks[1], (D_MODEL,), 0.02),
        "ln_in_b": nrm(ks[2], (D_MODEL,), 0.02),
        "w_in": nrm(ks[3], (DEPTH_2, D_MODEL, D_IN), D_MODEL ** -0.5),
        "b_gate": nrm(ks[4], (DEPTH_2, N_BRANCH * D_MODEL), 0.02),
        "na_rpb": nrm(ks[5], (DEPTH_2, NA_HEADS, 2 * NA_WIN_ROWS - 1, 2 * NA_WIN_COLS - 1), 0.02),
        "diff_lambda": nrm(ks[6], (DEPTH_2, 4, DIFF_HEAD_DIM), 0.1),
        "diff_subln_g": 1.0 + nrm(ks[7], (DEPTH_2, 2 * DIFF_HEAD_DIM), 0.02),
        "mla_q_norm_g": 1.0 + nrm(ks[8], (DEPTH_2, MLA_Q_RANK), 0.02),
        "mla_kv_norm_g": 1.0 + nrm(ks[9], (DEPTH_2, MLA_KV_RANK), 0.02),
        "w_mla_qb": nrm(ks[10], (DEPTH_2, MLA_Q_RANK, MLA_HEADS * (MLA_NOPE_DIM + MLA_ROPE_DIM)), MLA_Q_RANK ** -0.5),
        "w_mla_kvb": nrm(ks[11], (DEPTH_2, MLA_KV_RANK, MLA_HEADS * (MLA_NOPE_DIM + MLA_V_DIM)), MLA_KV_RANK ** -0.5),
        "w_branch": nrm(ks[12], (DEPTH_2, N_BRANCH, BRANCH_WIDTH, D_MODEL), BRANCH_WIDTH ** -0.5 * DN_BETA),
        "w_out": nrm(ks[13], (DEPTH_2, D_MODEL, D_MODEL), D_MODEL ** -0.5 * DN_BETA),
        "ln1_g": 1.0 + nrm(ks[14], (DEPTH_2, D_MODEL), 0.02),
        "ln1_b": nrm(ks[15], (DEPTH_2, D_MODEL), 0.02),
        "w_ffn_in": nrm(ks[16], (DEPTH_2, D_MODEL, 2 * D_FF), D_MODEL ** -0.5),
        "w_ffn_out": nrm(ks[17], (DEPTH_2, D_FF, D_MODEL), D_FF ** -0.5 * DN_BETA),
        "ln2_g": 1.0 + nrm(ks[18], (DEPTH_2, D_MODEL), 0.02),
        "ln2_b": nrm(ks[19], (DEPTH_2, D_MODEL), 0.02),
    }

def second_block(x, ln_in_g, ln_in_b, w_in, b_gate, na_rpb, diff_lambda, diff_subln_g,
              mla_q_norm_g, mla_kv_norm_g, w_mla_qb, w_mla_kvb, w_branch, w_out,
              ln1_g, ln1_b, w_ffn_in, w_ffn_out, ln2_g, ln2_b):
    b, s, _ = x.shape
    sizes = (NA_WIDTH, NA_WIDTH, NA_WIDTH, DIFF_QK_WIDTH, DIFF_QK_WIDTH, DIFF_V_WIDTH,
             MLA_Q_RANK, MLA_KV_RANK, MLA_ROPE_DIM, N_BRANCH * D_MODEL)
    split_points = np.cumsum(sizes)[:-1].tolist()

    x = layer_norm(x, ln_in_g, ln_in_b)
    for l in range(DEPTH_2):
        lam_init = 0.8 - 0.6 * math.exp(-0.3 * l)
        proj = jnp.einsum('bsd,de->bse', x, w_in[l])
        (na_q, na_k, na_v, df_q, df_k, df_v, m_cq, m_ckv, m_kr, gate_pre) = jnp.split(proj, split_points, axis=-1)

        na_out = neighbourhood_attention(
            na_q.reshape(b, s, NA_HEADS, NA_HEAD_DIM), na_k.reshape(b, s, NA_HEADS, NA_HEAD_DIM),
            na_v.reshape(b, s, NA_HEADS, NA_HEAD_DIM), na_rpb[l])
        df_out = diff_attention(df_q, df_k, df_v, diff_lambda[l], diff_subln_g[l], lam_init)
        mla_out = latent_attention(m_cq, m_ckv, m_kr, w_mla_qb[l], w_mla_kvb[l],
                                   mla_q_norm_g[l], mla_kv_norm_g[l])

        gates = jax.nn.sigmoid((gate_pre + b_gate[l]).astype(jnp.float32)).astype(x.dtype)
        gates = gates.reshape(b, s, N_BRANCH, D_MODEL)
        merged = (gates[:, :, 0] * jnp.einsum('bse,ed->bsd', na_out, w_branch[l, 0])
                  + gates[:, :, 1] * jnp.einsum('bse,ed->bsd', df_out, w_branch[l, 1])
                  + gates[:, :, 2] * jnp.einsum('bse,ed->bsd', mla_out, w_branch[l, 2]))
        mix = jnp.einsum('bsd,de->bse', merged, w_out[l])
        x = layer_norm(DN_ALPHA * x + mix, ln1_g[l], ln1_b[l])

        gu = jnp.einsum('bsd,df->bsf', x, w_ffn_in[l])
        hidden = jax.nn.silu(gu[..., :D_FF]) * gu[..., D_FF:]
        ffn = jnp.einsum('bsf,fd->bsd', hidden, w_ffn_out[l])
        x = layer_norm(DN_ALPHA * x + ffn, ln2_g[l], ln2_b[l])
    return x


def setup_inputs(seed=0):
    out = dict(first_inputs(seed))
    for name, value in second_inputs(seed + 1).items():
        if name != "x":
            out[name + "_2"] = value
    return out


def reference(
    x, c, ctx, c_ctx, ada_w, ada_b, norm1_w, norm2_w, w_in, conv_w, conv_b, dt_bias, a_log,
    d_skip, ssd_norm_w, sgu_ln_w, sgu_ln_b, w_s, b_s, w_pa, w_pb, w_o, router_w, w_gate, w_up,
    w_down, final_norm_w, ln_in_g_2, ln_in_b_2, w_in_2, b_gate_2, na_rpb_2, diff_lambda_2,
    diff_subln_g_2, mla_q_norm_g_2, mla_kv_norm_g_2, w_mla_qb_2, w_mla_kvb_2, w_branch_2,
    w_out_2, ln1_g_2, ln1_b_2, w_ffn_in_2, w_ffn_out_2, ln2_g_2, ln2_b_2,
):
    x = first_block(
        x, c, ctx, c_ctx, ada_w, ada_b, norm1_w, norm2_w, w_in, conv_w, conv_b, dt_bias, a_log,
        d_skip, ssd_norm_w, sgu_ln_w, sgu_ln_b, w_s, b_s, w_pa, w_pb, w_o, router_w, w_gate,
        w_up, w_down, final_norm_w,
    )
    return second_block(
        x, ln_in_g_2, ln_in_b_2, w_in_2, b_gate_2, na_rpb_2, diff_lambda_2, diff_subln_g_2,
        mla_q_norm_g_2, mla_kv_norm_g_2, w_mla_qb_2, w_mla_kvb_2, w_branch_2, w_out_2, ln1_g_2,
        ln1_b_2, w_ffn_in_2, w_ffn_out_2, ln2_g_2, ln2_b_2,
    )


_drawn_inputs = setup_inputs


def setup_inputs(seed=0):
    import zlib

    import numpy as np

    out = dict(_drawn_inputs(seed))
    spreads = {}
    factors = {'d_skip': 8.0,
     'b_gate_2': 8.0,
     'na_rpb_2': 25.328,
     'diff_lambda_2': 8.0,
     'diff_subln_g_2': 8.0,
     'mla_q_norm_g_2': 8.0,
     'mla_kv_norm_g_2': 8.0,
     'w_mla_qb_2': 4.893}
    for name, (base, spread) in spreads.items():
        noise = np.random.default_rng([zlib.crc32(name.encode()), seed]).standard_normal(out[name].shape)
        drawn = base * np.exp(spread * noise) if base else spread * noise
        out[name] = __import__('jax').numpy.asarray(drawn.astype(out[name].dtype))
    for name, factor in factors.items():
        out[name] = (out[name] * factor).astype(out[name].dtype)
    return out
```

```python
from contextlib import ExitStack

import numpy as np

import concourse.bass as bass
from concourse import mybir

F32 = mybir.dt.float32
ALU = mybir.AluOpType
ACT = mybir.ActivationFunctionType
AX = mybir.AxisListType

P = 128
D = 1024
KD = D // P
T = 512
TT = T // P
CTX = 256
CT = CTX // P
SLAB = 4352
SLOTS = 3
BANKS = 8
NEG = -1.0e30

HEADS, HDIM, GROUPS, STATE = 16, 64, 4, 128
HPG = HEADS // GROUPS
XBC = D + 2 * GROUPS * STATE
NSCAN = XBC + 2 * HEADS
EPS = 1e-6
EXPERTS, CAP = 16, 64

LAYERS = 2
GRID = 64
ROWS = T // GRID
QB = 16
NBLK = GRID // QB
WIN = 16
RPB_W = 2 * WIN - 1
RPB_H = 15
RUN = (ROWS - 1) * RPB_W + 3 * QB
RPB_PAD = 16
NA_HEADS, DF_HEADS, MLA_HEADS = 8, 4, 8
BR = 512
FF = 2816
KF = FF // P
QRANK, KVRANK, ROPE_D = 384, 256, 32
ALPHA = 4.0 ** 0.25
SCALE = {"df": 64 ** -0.5, "ml": 96 ** -0.5}
LN_EPS = 1e-5


class Ring:

    def __init__(self, full, free, step):
        self.full, self.free, self.step, self.n = full, free, step, len(full)
        self.base, self.pos = [0] * self.n, 0
        self.reps = 0

    def begin(self, keys, reps=1):
        if self.reps:
            self.base = [b + self.reps * c for b, c in zip(self.base, self.count)]
            self.pos = (self.pos + len(self.use)) % self.n
        self.reps, self.count, self.use = reps, [0] * self.n, {}
        for k, key in enumerate(keys):
            slot = (self.pos + k) % self.n
            assert key not in self.use, key
            self.use[key] = (slot, self.base[slot] + self.count[slot])
            self.count[slot] += 1

    def slot(self, key):
        return self.use[key][0]

    def filled(self, eng, key, i=0):
        slot, before = self.use[key]
        eng.wait_ge(self.full[slot], i * (self.step * self.count[slot]) + self.step * (before + 1))

    def filled_too(self, eng, key, later, i=0):
        if self.use[key][0] != self.use[later][0]:
            self.filled(eng, key, i)

    def vacant(self, eng, key, i=0):
        slot, before = self.use[key]
        if before:
            eng.wait_ge(self.free[slot], i * self.count[slot] + before)

    def put(self, key):
        return self.full[self.use[key][0]]

    def done(self, key):
        return self.free[self.use[key][0]]


def bcast_rows(v, n):
    return v.rearrange("(a n) -> a n", a=1).broadcast_to([P, n])


def w_tiles(w, r0, rows, c0, cols):
    return w[r0:r0 + rows, c0:c0 + cols].rearrange("(k p) n -> p k n", p=P)


class Core:

    def __init__(self, nc, ctx, ins):
        self.nc, self.ctx, self.ins = nc, ctx, ins
        self.stage = ""
        self.ring = self.sb("ring", [P, SLOTS, SLAB])
        self.slabs = Ring([self.sem(f"slab_full{i}") for i in range(SLOTS)],
                          [self.sem(f"slab_read{i}") for i in range(SLOTS)], 16)
        self.bank = [ctx.enter_context(nc.psum_tensor(f"bank{i}", [P, 512], F32)) for i in range(BANKS)]
        self.banks = Ring([self.sem(f"bank_full{i}") for i in range(BANKS)],
                          [self.sem(f"bank_read{i}") for i in range(BANKS)], 1)
        self.vec = self.sb("vec", [P, NVEC])
        self.con = self.sb("con", [P, NCON])
        self.x = self.sb("x", [P, KD, T])
        self.mod = self.sb("mod", [P, 48, 2])

    def sb(self, name, shape, ctx=None):
        return (ctx or self.ctx).enter_context(self.nc.sbuf_tensor(self.stage + name, shape, F32))

    def sem(self, name, ctx=None):
        return (ctx or self.ctx).enter_context(self.nc.semaphore(self.stage + name))

    def v(self, name, i=0, n=1):
        a = VEC[name][0] + i
        return self.vec[:, a:a + n]

    def c(self, name, rows=P):
        a, n = CON[name][:2]
        return self.con[0:rows, a:a + n]

    def ps(self, key):
        return self.bank[self.banks.slot(key)]

    def slab(self, key, k, n):
        return self.ring[:, self.slabs.slot(key), 0:k * n].rearrange("p (k n) -> p k n", k=k)


def load_slab(core, sp, key, src, i=0, at=0):
    _, k, n = src.shape
    core.slabs.vacant(sp, key, i)
    dst = core.ring[:, core.slabs.slot(key), at:at + k * n].rearrange("p (k n) -> p k n", k=k)
    sp.dma_start(dst, src).then_inc(core.slabs.put(key), 16)


def product(pe, out, lhs, rhs, read=None):
    n = len(lhs)
    for k in range(n):
        last = pe.matmul(out, lhs[k], rhs[k], start=k == 0, stop=k == n - 1)
        if k == 0 and read is not None:
            last.then_inc(read, 1)
    return last


def front(core, ctx, a):
    core.stage = "front_"
    nc, I = core.nc, core.ins
    TA = T + CTX
    NM = XBC // P
    sem = lambda n: core.sem(n, ctx)
    pad = core.sb("pad", [P, 2, TA + 3], ctx)
    conv = core.sb("conv", [P, 2, TA + 1], ctx)
    act_x = core.sb("act_x", [P, 2, TA], ctx)
    sq = core.sb("sq", [P, 2, TA], ctx)
    rstd = core.sb("rstd", [P, TA], ctx)
    scale1 = core.sb("scale1", [P, KD, 2], ctx)
    dtw = core.sb("dtw", [P, 6, CT + TT, 2 * HEADS], ctx)
    raw, mag, ex, one_ex, ln_ex, rest = (dtw[:, k] for k in range(6))
    rows = core.sb("rowsA", [P, 5 * HEADS], ctx)
    dt_bias, a_neg = rows[:, 0:2 * HEADS], rows[:, 2 * HEADS:4 * HEADS]
    const_in, x_in, pad_zero = sem("const_in"), sem("x_in"), sem("pad_zero")
    c_silu = sem("c_silu")
    sq_done, sq_used, root_done = sem("sq_done"), sem("sq_used"), sem("root_done")
    scaled, xm_done = sem("scaled"), sem("xm_done")
    dt_dve, dt_act = sem("dt_dve"), sem("dt_act")
    pad_done, conv_done, act_done = sem("pad_done"), sem("conv_done"), sem("act_done")

    ada = [("ada", s) for s in range(4)]
    xbc = [("xbc", s) for s in range(4)]
    core.slabs.begin(ada + ["dtw"] + xbc)
    keys = ["rms_l", "rms_c"] + ada + ["dt"]
    for m in range(NM):
        keys += [("xl", m)] + ([("xc", m)] if m < 12 else [])
        if m >= 1 and m - 1 < 12:
            keys += [("tl", m - 1), ("tc", m - 1)]
    core.banks.begin(keys)

    with nc.Block() as block:
        @block.sync
        def _(sp):
            sp.dma_start(core.con[:, :], I["con"]).then_inc(const_in, 16)
            sp.dma_start(core.vec[:, :], I["vec"]).then_inc(const_in, 16)
            sp.dma_start(a.c[:, :, :], I["cT"].rearrange("(k p) n -> p k n", p=P)).then_inc(const_in, 16)
            sp.dma_start(a.xm[:, :, 0:T], I["xT"].rearrange("(k p) n -> p k n", p=P)).then_inc(x_in, 16)
            sp.dma_start(a.xm[:, :, T:TA], I["ctxT"].rearrange("(k p) n -> p k n", p=P)).then_inc(x_in, 16)
            sp.dma_start(rows[:, :], bcast_rows(I["rowsA"], 5 * HEADS)).then_inc(const_in, 16)
            for s in range(4):
                load_slab(core, sp, ("ada", s), w_tiles(I["ada_w"], 0, D, 512 * s, 512))
            load_slab(core, sp, "dtw", w_tiles(I["w_in"], 0, D, XBC, 2 * HEADS))
            for s in range(4):
                load_slab(core, sp, ("xbc", s), w_tiles(I["w_in"], 0, D, 512 * s, 512))

        @block.tensor
        def _(pe):
            pe.wait_ge(const_in, 64)
            core.banks.vacant(pe, "rms_l")
            core.banks.vacant(pe, "rms_c")
            for k in range(KD):
                pe.wait_ge(sq_done, k + 1)
                last = pe.matmul(core.ps("rms_l")[:, :], core.c("mean_d"), sq[:, k % 2, 0:T],
                                 start=k == 0, stop=k == KD - 1)
                if k == KD - 1:
                    last.then_inc(core.banks.put("rms_l"), 1)
                last = pe.matmul(core.ps("rms_c")[:, 0:CTX], core.c("mean_d"), sq[:, k % 2, T:TA],
                                 start=k == 0, stop=k == KD - 1)
                if k < KD - 1:
                    last.then_inc(sq_used, 1)
            last.then_inc(core.banks.put("rms_c"), 1)
            pe.wait_ge(c_silu, 1)
            for s in range(4):
                core.slabs.filled(pe, ("ada", s))
                core.banks.vacant(pe, ("ada", s))
                w = core.slab(("ada", s), KD, 512)
                for m in range(4):
                    last = product(pe, core.ps(("ada", s))[:, 2 * m:2 * m + 2],
                                   [w[:, k, m * P:(m + 1) * P] for k in range(KD)],
                                   [a.c[:, k, :] for k in range(KD)],
                                   core.slabs.done(("ada", s - 1)) if s and m == 0 else None)
                last.then_inc(core.banks.put(("ada", s)), 1)
            pe.wait_ge(xm_done, 2 * KD)
            core.slabs.filled(pe, "dtw")
            core.banks.vacant(pe, "dt")
            w = core.slab("dtw", KD, 2 * HEADS)
            for t in range(TT + CT):
                last = product(pe, core.ps("dt")[:, t * 32:t * 32 + 32],
                               [a.xm[:, k, t * P:(t + 1) * P] for k in range(KD)],
                               [w[:, k, :] for k in range(KD)],
                               core.slabs.done(("ada", 3)) if t == 0 else None)
            last.then_inc(core.banks.put("dt"), 1)

            def turn(m):
                pe.wait_ge(act_done, m + 1)
                src = act_x[:, m % 2]
                for name, t0, n in (("tl", 0, TT), ("tc", TT, CT)):
                    core.banks.vacant(pe, (name, m))
                    for t in range(n):
                        last = pe.transpose(core.ps((name, m))[:, t * P:(t + 1) * P],
                                            src[:, (t0 + t) * P:(t0 + t + 1) * P], core.c("ident"))
                    last.then_inc(core.banks.put((name, m)), 1)

            for m in range(NM):
                read = None
                if m % 4 == 0:
                    core.slabs.filled(pe, ("xbc", m // 4))
                    read = core.slabs.done(("xbc", m // 4 - 1) if m else "dtw")
                w = core.slab(("xbc", m // 4), KD, 512)
                cut = [w[:, k, (m % 4) * P:(m % 4 + 1) * P] for k in range(KD)]
                core.banks.vacant(pe, ("xl", m))
                last = product(pe, core.ps(("xl", m))[:, :], cut, [a.xm[:, k, 0:T] for k in range(KD)], read)
                last.then_inc(core.banks.put(("xl", m)), 1)
                if m < 12:
                    core.banks.vacant(pe, ("xc", m))
                    last = product(pe, core.ps(("xc", m))[:, 0:CTX], cut, [a.xm[:, k, T:TA] for k in range(KD)])
                    last.then_inc(core.banks.put(("xc", m)), 1)
                if m >= 1 and m - 1 < 12:
                    turn(m - 1)
            pe.drain().then_inc(core.slabs.done(("xbc", 3)), 1)

        @block.scalar
        def _(act):
            act.wait_ge(x_in, 32)
            for k in range(KD):
                if k >= 2:
                    act.wait_ge(sq_used, k - 1)
                act.activation(sq[:, k % 2, :], a.xm[:, k, :], ACT.Square).then_inc(sq_done, 1)
            act.wait_ge(const_in, 64)
            core.banks.filled(act, "rms_l")
            core.banks.filled(act, "rms_c")
            act.activation(rstd[:, 0:T], core.ps("rms_l")[:, :], ACT.Sqrt,
                           bias=core.c("eps6")).then_inc(core.banks.done("rms_l"), 1)
            act.activation(rstd[:, T:TA], core.ps("rms_c")[:, 0:CTX], ACT.Sqrt,
                           bias=core.c("eps6")).then_inc(core.banks.done("rms_c"), 1)
            act.drain().then_inc(root_done, 1)
            act.activation(a.c[:, :, :], a.c[:, :, :], ACT.Silu).then_inc(c_silu, 1)
            for k in range(KD):
                for j, (lo, hi) in enumerate(((0, T), (T, TA))):
                    act.wait_ge(scaled, 2 * k + j + 1)
                    act.activation(a.xm[:, k, lo:hi], a.xm[:, k, lo:hi], ACT.Identity,
                                   bias=core.mod[:, k, j:j + 1]).then_inc(xm_done, 1)
            act.wait_ge(dt_dve, 1)
            act.activation(mag, raw, ACT.Abs).then_inc(dt_act, 1)
            act.wait_ge(dt_act, 1)
            act.activation(ex, mag, ACT.Exp, scale=-1.0)
            act.activation(a_neg, a_neg, ACT.Exp).then_inc(dt_act, 1)
            act.wait_ge(dt_dve, 2)
            act.activation(ln_ex, one_ex, ACT.Ln).then_inc(dt_act, 1)

            def silu(m):
                act.wait_ge(conv_done, m + 1)
                if m >= 12:
                    act.activation(a.bc[:, m - 8, :], conv[:, m % 2, 0:T], ACT.Silu, bias=core.v("conv_b", m))\
                       .then_inc(act_done, 1)
                    return
                if m >= 2:
                    core.banks.filled(act, ("tc", m - 2))
                act.activation(act_x[:, m % 2, 0:T], conv[:, m % 2, 0:T], ACT.Silu, bias=core.v("conv_b", m))
                act.activation(act_x[:, m % 2, T:TA], conv[:, m % 2, T + 1:TA + 1], ACT.Silu,
                               bias=core.v("conv_b", m))
                act.drain().then_inc(act_done, 1)
                if m >= 8:
                    act.activation(a.bc[:, m - 8, :], act_x[:, m % 2, 0:T], ACT.Identity)

            act.wait_ge(pad_zero, 1)
            for m in range(NM):
                core.banks.filled(act, ("xl", m))
                if m >= 2:
                    act.wait_ge(conv_done, m - 1)
                act.activation(pad[:, m % 2, 1:T + 1], core.ps(("xl", m))[:, :], ACT.Identity)\
                   .then_inc(core.banks.done(("xl", m)), 1)
                if m < 12:
                    core.banks.filled(act, ("xc", m))
                    act.activation(pad[:, m % 2, T + 2:TA + 2], core.ps(("xc", m))[:, 0:CTX], ACT.Identity)\
                       .then_inc(core.banks.done(("xc", m)), 1)
                act.drain().then_inc(pad_done, 1)
                if m >= 1:
                    silu(m - 1)
            silu(NM - 1)

        @block.vector
        def _(dve):
            dve.wait_ge(const_in, 64)
            for s in range(4):
                core.banks.filled(dve, ("ada", s))
                bias = core.v("ada_b", 4 * s, 4).unsqueeze(2).broadcast_to([P, 4, 2])
                dve.tensor_tensor(core.mod[:, 4 * s:4 * s + 4, :],
                                  core.ps(("ada", s))[:, 0:8].rearrange("p (m j) -> p m j", j=2), bias,
                                  ALU.add).then_inc(core.banks.done(("ada", s)), 1)
            dve.drain()
            dve.tensor_scalar(scale1[:, :, :], core.mod[:, KD:2 * KD, :], 1.0, None, ALU.add)
            dve.drain()
            dve.tensor_tensor(scale1[:, :, :], scale1[:, :, :],
                              core.v("norm1_w", 0, KD).unsqueeze(2).broadcast_to([P, KD, 2]), ALU.mult)
            dve.wait_ge(root_done, 1)
            dve.reciprocal(rstd[:, :], rstd[:, :])
            dve.drain()
            for k in range(KD):
                for j, (lo, hi) in enumerate(((0, T), (T, TA))):
                    dve.scalar_tensor_tensor(out=a.xm[:, k, lo:hi], in0=a.xm[:, k, lo:hi],
                                             scalar=scale1[:, k, j:j + 1], in1=rstd[:, lo:hi],
                                             op0=ALU.mult, op1=ALU.mult).then_inc(scaled, 1)
            core.banks.filled(dve, "dt")
            bias = dt_bias.unsqueeze(1).broadcast_to([P, CT + TT, 2 * HEADS])
            dve.tensor_tensor(raw, core.ps("dt")[:, 0:192].rearrange("p (t h) -> p t h", h=2 * HEADS), bias,
                              ALU.add).then_inc(core.banks.done("dt"), 1)
            dve.drain().then_inc(dt_dve, 1)
            dve.wait_ge(dt_act, 2)
            dve.tensor_scalar(one_ex, ex, 1.0, None, ALU.add)
            dve.drain().then_inc(dt_dve, 1)
            dve.tensor_scalar(rest, one_ex, -1.0, None, ALU.add)
            dve.drain()
            dve.tensor_tensor(rest, ex, rest, ALU.subtract)
            dve.reciprocal(mag, one_ex)
            dve.drain()
            dve.tensor_tensor(rest, rest, mag, ALU.mult)
            dve.wait_ge(dt_act, 3)
            dve.drain()
            dve.tensor_tensor(rest, rest, ln_ex, ALU.add)
            dve.drain()
            dve.scalar_tensor_tensor(out=a.dt[:, :, :], in0=raw, scalar=0.0, in1=rest, op0=ALU.max, op1=ALU.add)
            dve.drain()
            dve.scalar_tensor_tensor(out=a.dta[:, :, :], in0=a.dt[:, :, :], scalar=-1.0,
                                     in1=a_neg.unsqueeze(1).broadcast_to([P, CT + TT, 2 * HEADS]),
                                     op0=ALU.mult, op1=ALU.mult)

            def tokens(m):
                dst, col = (a.xtok, m) if m < 8 else (a.btok, m - 8)
                for name, t0, n in (("tl", 0, TT), ("tc", TT, CT)):
                    core.banks.filled(dve, (name, m))
                    last = dve.tensor_copy(dst[:, t0:t0 + n, col * P:(col + 1) * P],
                                           core.ps((name, m))[:, 0:n * P].rearrange("p (t f) -> p t f", f=P))
                    last.then_inc(core.banks.done((name, m)), 1)

            for m in range(NM):
                dve.wait_ge(pad_done, m + 1)
                if m >= 2:
                    dve.wait_ge(act_done, m - 1)
                n = TA + 1 if m < 12 else T
                src, dst = pad[:, m % 2], conv[:, m % 2, 0:n]
                dve.tensor_scalar(dst, src[:, 0:n], core.v("conv_w", m), None, ALU.mult)
                dve.drain()
                for tap in (1, 2):
                    dve.scalar_tensor_tensor(out=dst, in0=src[:, tap:n + tap], scalar=core.v("conv_w", NM * tap + m),
                                             in1=dst, op0=ALU.mult, op1=ALU.add)
                    if tap == 1:
                        dve.drain()
                dve.drain().then_inc(conv_done, 1)
                if m >= 2 and m - 2 < 12:
                    tokens(m - 2)

        @block.gpsimd
        def _(pool):
            pool.memset(pad[:, :, :], 0.0).then_inc(pad_zero, 1)
            pool.wait_ge(const_in, 64)
            pool.tensor_copy(a.skip[:, :], rows[:, 4 * HEADS:5 * HEADS])


def scan(core, ctx, a):
    core.stage = "scan_"
    nc = core.nc
    sem = lambda n: core.sem(n, ctx)
    NT, H2 = TT + CT, 2 * HEADS
    acum = core.sb("acum", [P, NT, H2], ctx)
    grow = core.sb("grow", [P, NT, H2], ctx)
    total = core.sb("total", [P, NT, H2], ctx)
    toend = core.sb("toend", [P, NT, H2], ctx)
    spare = core.x[:, :, :].rearrange("p m t -> p (m t)")
    cb = spare[:, 0:TT * GROUPS * P].rearrange("p (t n) -> p t n", t=TT)
    xdt, xend = spare[:, 2 * D:3 * D], spare[:, 3 * D:4 * D]
    h = core.sb("h", [P, 2, D], ctx)
    NSEG = 6
    seg = core.sb("seg", [P, NSEG, HPG * P], ctx)
    part = core.sb("part", [P, D], ctx)
    acum_done, exp_done, cb_done, toend_done = sem("acum_done"), sem("exp_done"), sem("cb_done"), sem("toend_done")
    seg_done, decay_done, mt_done, mt_used = sem("seg_done"), sem("decay_done"), sem("mt_done"), sem("mt_used")
    xdt_done, xdt_used, xend_done, xend_used = sem("xdt_done"), sem("xdt_used"), sem("xend_done"), sem("xend_used")
    h_done, part_done, part_used = sem("h_done"), sem("part_done"), sem("part_used")

    ctx_steps = [(d, TT + (k if d == 0 else CT - 1 - k), False) for k in range(CT) for d in (0, 1)]
    lat_steps = [(d, k if d == 0 else TT - 1 - k, True) for k in range(TT) for d in (0, 1)]
    steps = ctx_steps + lat_steps
    outs = [u for u, s in enumerate(steps) if s[2]]
    feeds = [u for u, s in enumerate(steps) if u < len(steps) - 2]
    G = range(GROUPS)
    keys = ["sums"] + [("cb", t) for t in range(TT)]
    first = outs[0]

    def seg_keys(u):
        return [("seg", u, g) for g in G]

    keys += [k for u in range(first) for k in (("st", u, 0), ("st", u, 1))] + seg_keys(first)
    for u in outs:
        if u + 1 in outs:
            keys += seg_keys(u + 1)
        keys += [("off", u, 0), ("off", u, 1)]
        if u in feeds:
            keys += [("st", u, 0), ("st", u, 1)]
        keys += [("diag", u, 0), ("diag", u, 1)]
    core.slabs.begin([])
    core.banks.begin(keys)
    order = {u: n for n, u in enumerate(outs)}
    feed_no = {u: n for n, u in enumerate(feeds)}
    per_head = lambda ap: ap.unsqueeze(2).broadcast_to([P, HEADS, HDIM])
    by_head = lambda ap: ap.rearrange("p (h f) -> p h f", f=HDIM)

    with nc.Block() as block:
        @block.tensor
        def _(pe):
            core.banks.vacant(pe, "sums")
            sums = core.ps("sums")
            for d, tri in enumerate(("tri_f", "tri_b")):
                pe.matmul(sums[:, d * 96:d * 96 + 96], core.c(tri), a.dta[:, :, d * HEADS:(d + 1) * HEADS],
                          start=True, stop=True)
            pe.matmul(sums[:, 192:384], core.c("ones"), a.dta[:, :, :], start=True, stop=True)\
              .then_inc(core.banks.put("sums"), 1)
            for t in range(TT):
                core.banks.vacant(pe, ("cb", t))
                for g in G:
                    last = pe.matmul(core.ps(("cb", t))[:, g * P:(g + 1) * P], a.bc[:, g, t * P:(t + 1) * P],
                                     a.bc[:, GROUPS + g, t * P:(t + 1) * P], start=True, stop=True)
                last.then_inc(core.banks.put(("cb", t)), 1)

            def state(u):
                t = steps[u][1]
                pe.wait_ge(xend_done, feed_no[u] + 1)
                for half in (0, 1):
                    core.banks.vacant(pe, ("st", u, half))
                    for g in (2 * half, 2 * half + 1):
                        last = pe.matmul(core.ps(("st", u, half))[:, (g % 2) * 256:(g % 2) * 256 + 256],
                                         a.btok[:, t, g * P:(g + 1) * P], xend[:, g * 256:(g + 1) * 256],
                                         start=True, stop=True)
                    last.then_inc(core.banks.put(("st", u, half)), 1)

            def sums_of(u):
                d, t, _ = steps[u]
                for g in G:
                    core.banks.vacant(pe, ("seg", u, g))
                    for r in range(HPG):
                        col = d * HEADS + g * HPG + r
                        last = pe.matmul(core.ps(("seg", u, g))[:, r * P:(r + 1) * P],
                                         a.dta[:, t, col:col + 1].broadcast_to([P, P]),
                                         core.c("tri_b" if d else "tri_f"), start=True, stop=True)
                    last.then_inc(core.banks.put(("seg", u, g)), 1)

            for u in range(first):
                state(u)
            sums_of(first)
            for u in outs:
                d, t, _ = steps[u]
                if u + 1 in outs:
                    sums_of(u + 1)
                pe.wait_ge(h_done, u - 1)
                for half in (0, 1):
                    core.banks.vacant(pe, ("off", u, half))
                    for g in (2 * half, 2 * half + 1):
                        last = pe.matmul(core.ps(("off", u, half))[:, (g % 2) * 256:(g % 2) * 256 + 256],
                                         a.bc[:, GROUPS + g, t * P:(t + 1) * P], h[:, d, g * 256:(g + 1) * 256],
                                         start=True, stop=True)
                    last.then_inc(core.banks.put(("off", u, half)), 1)
                if u in feeds:
                    state(u)
                pe.wait_ge(xdt_done, order[u] + 1)
                for half in (0, 1):
                    core.banks.vacant(pe, ("diag", u, half))
                    for g in (2 * half, 2 * half + 1):
                        n = order[u] * GROUPS + g
                        pe.wait_ge(mt_done, n + 1)
                        for r in range(HPG):
                            hd = g * HPG + r
                            last = pe.matmul(core.ps(("diag", u, half))[:, (hd % 8) * HDIM:(hd % 8 + 1) * HDIM],
                                             seg[:, n % NSEG, r * P:(r + 1) * P], xdt[:, hd * HDIM:(hd + 1) * HDIM],
                                             start=True, stop=True)
                            if r == HPG - 1 and g % 2 == 0:
                                last.then_inc(mt_used, 1)
                    last.then_inc(core.banks.put(("diag", u, half)), 1)

        @block.scalar
        def _(act):
            act.wait_ge(acum_done, 1)
            act.activation(grow[:, :, :], acum[:, :, :], ACT.Exp)
            act.activation(total[:, :, :], total[:, :, :], ACT.Exp)
            act.activation(toend[:, :, :], toend[:, :, :], ACT.Exp)
            act.drain().then_inc(exp_done, 1)
            for t in range(TT):
                core.banks.filled(act, ("cb", t))
                act.activation(cb[:, t, :], core.ps(("cb", t))[:, :], ACT.Identity)\
                   .then_inc(core.banks.done(("cb", t)), 1)
            act.drain().then_inc(cb_done, 1)
            for n in range(len(outs) * GROUPS):
                act.wait_ge(seg_done, n + 1)
                act.activation(seg[:, n % NSEG, :], seg[:, n % NSEG, :], ACT.Exp).then_inc(decay_done, 1)

        @block.vector
        def _(dve):
            core.banks.filled(dve, "sums")
            sums = core.ps("sums")
            for d in (0, 1):
                dve.tensor_copy(acum[:, :, d * HEADS:(d + 1) * HEADS],
                                sums[:, d * 96:d * 96 + 96].rearrange("p (t h) -> p t h", h=HEADS))
            dve.tensor_copy(total[:, :, :], sums[:, 192:384].rearrange("p (t h) -> p t h", h=H2))\
               .then_inc(core.banks.done("sums"), 1)
            dve.drain()
            dve.tensor_tensor(toend[:, :, :], total[:, :, :], acum[:, :, :], ALU.subtract)
            dve.drain().then_inc(acum_done, 1)
            dve.wait_ge(exp_done, 1)
            dve.tensor_tensor(toend[:, :, :], toend[:, :, :], a.dt[:, :, :], ALU.mult)
            dve.drain().then_inc(toend_done, 1)

            def carry(u):
                d, t, _ = steps[u]
                if u >= 2:
                    if u in outs:
                        core.banks.filled(dve, ("off", u, 1))
                    dve.tensor_tensor(by_head(h[:, d, :]), by_head(h[:, d, :]),
                                      per_head(total[:, t, d * HEADS:(d + 1) * HEADS]), ALU.mult)
                    dve.drain()
                for half in (0, 1):
                    core.banks.filled(dve, ("st", u, half))
                    dst, src = h[:, d, half * 512:half * 512 + 512], core.ps(("st", u, half))[:, :]
                    last = dve.tensor_tensor(dst, dst, src, ALU.add) if u >= 2 else dve.tensor_copy(dst, src)
                    last.then_inc(core.banks.done(("st", u, half)), 1)
                dve.drain().then_inc(h_done, 1)

            def segments(u):
                d, t, _ = steps[u]
                for g in G:
                    n = order[u] * GROUPS + g
                    core.banks.filled(dve, ("seg", u, g))
                    if n >= NSEG:
                        old = n - NSEG
                        if old % 2 == 0:
                            dve.wait_ge(mt_used, old // 2 + 1)
                        else:
                            core.banks.filled(dve, ("diag", outs[old // GROUPS], (old % GROUPS) // 2))
                    for r in range(HPG):
                        col = d * HEADS + g * HPG + r
                        last = dve.scalar_tensor_tensor(
                            out=seg[:, n % NSEG, r * P:(r + 1) * P], in0=core.ps(("seg", u, g))[:, r * P:(r + 1) * P],
                            scalar=acum[:, t, col:col + 1], in1=core.c("mask_b" if d else "mask_f"),
                            op0=ALU.subtract, op1=ALU.add)
                    last.then_inc(core.banks.done(("seg", u, g)), 1)
                    dve.drain().then_inc(seg_done, 1)

            def scaled_x(u):
                d, t, _ = steps[u]
                if order[u]:
                    core.banks.filled(dve, ("diag", u - 1, 1))
                dve.tensor_tensor(by_head(xdt[:, :]), by_head(a.xtok[:, t, :]),
                                  per_head(a.dt[:, t, d * HEADS:(d + 1) * HEADS]), ALU.mult).then_inc(xdt_done, 1)

            for u in range(first):
                carry(u)
            segments(first)
            for u in outs:
                d, t, _ = steps[u]
                scaled_x(u)
                if u in feeds:
                    carry(u)
                if u + 1 in outs:
                    segments(u + 1)
                if order[u]:
                    dve.wait_ge(part_used, order[u])
                for half in (0, 1):
                    lo = half * 512
                    core.banks.filled(dve, ("off", u, half))
                    dve.tensor_tensor(by_head(part[:, :])[:, 8 * half:8 * half + 8],
                                      by_head(core.ps(("off", u, half))[:, :]),
                                      per_head(grow[:, t, d * HEADS:(d + 1) * HEADS])[:, 8 * half:8 * half + 8],
                                      ALU.mult).then_inc(core.banks.done(("off", u, half)), 1)
                    core.banks.filled(dve, ("diag", u, half))
                    dve.drain()
                    dve.tensor_tensor(part[:, lo:lo + 512], part[:, lo:lo + 512], core.ps(("diag", u, half))[:, :],
                                      ALU.add).then_inc(core.banks.done(("diag", u, half)), 1)
                dve.drain().then_inc(part_done, 1)

        @block.gpsimd
        def _(pool):
            def to_end(u):
                d, t, _ = steps[u]
                n = feed_no[u]
                if n:
                    core.banks.filled(pool, ("st", feeds[n - 1], 1))
                pool.tensor_tensor(by_head(xend[:, :]), by_head(a.xtok[:, t, :]),
                                   per_head(toend[:, t, d * HEADS:(d + 1) * HEADS]), ALU.mult).then_inc(xend_done, 1)

            def decays(u):
                t = steps[u][1]
                for g in G:
                    n = order[u] * GROUPS + g
                    pool.wait_ge(decay_done, n + 1)
                    cbg = cb[:, t, g * P:(g + 1) * P].unsqueeze(1).broadcast_to([P, HPG, P])
                    m = seg[:, n % NSEG, :].rearrange("p (r i) -> p r i", i=P)
                    pool.tensor_tensor(m, m, cbg, ALU.mult).then_inc(mt_done, 1)

            def add_part(u):
                t = steps[u][1]
                pool.wait_ge(part_done, order[u] + 1)
                pool.tensor_tensor(a.y[:, t, :], a.y[:, t, :], part[:, :], ALU.add).then_inc(part_used, 1)

            pool.wait_ge(toend_done, 1)
            for u in range(first):
                to_end(u)
            for t in range(TT):
                pool.tensor_tensor(by_head(a.y[:, t, :]), by_head(a.xtok[:, t, :]), per_head(a.skip[:, :]), ALU.mult)
            pool.drain()
            pool.wait_ge(cb_done, 1)
            for u in outs:
                t = steps[u][1]
                if u in feeds:
                    to_end(u)
                decays(u)
                if order[u]:
                    add_part(u - 1)
            add_part(outs[-1])


def mixer(core, ctx, a):
    core.stage = "mixer_"
    nc, I = core.nc, core.ins
    sem = lambda n: core.sem(n, ctx)
    Z0, V0, U0 = NSCAN, NSCAN + 2 * D, NSCAN + D
    GA, GB = NSCAN + 3 * D, NSCAN + 4 * D
    v = core.sb("v", [P, TT, D], ctx)
    u = core.sb("u", [P, KD, T], ctx)
    yt = core.sb("yt", [P, KD, T], ctx)
    ws = core.sb("ws", [P, KD, P], ctx)
    gate = core.sb("gate", [P, 4, T], ctx)
    rows = core.sb("rowsB", [P, 2 * D + KD * P], ctx)
    ln_w, ln_b, b_s = rows[:, 0:D], rows[:, D:2 * D], rows[:, 2 * D:]
    zs = core.sb("zs", [P, 2, 512], ctx)
    tmp = core.sb("tmp", [P, 2, T], ctx)
    ssq = core.sb("ssq", [P, TT, GROUPS], ctx)
    bn = core.sb("bn", [P, TT, 2, 6], ctx)
    mv = core.sb("mv", [P, TT, 2], ctx)
    merged = v[:, :, :].rearrange("p t n -> p (t n)").rearrange("p (m t) -> p m t", t=T)
    zs_done, zs_used, ssq_done, y_done = sem("zs_done"), sem("zs_used"), sem("ssq_done"), sem("y_done")
    v_done, v_ready, u_done, root2_done, mv_done = sem("v_done"), sem("v_ready"), sem("u_done"), sem("root2_done"), sem("mv_done")
    sgu_done, yt_done, gate_done, merged_done = sem("sgu_done"), sem("yt_done"), sem("gate_done"), sem("merged_done")
    rows_in, res_in, gated, mod2_done = sem("rows_in"), sem("res_in"), sem("gated"), sem("mod2_done")
    v_norm, merged_a = sem("v_norm"), sem("merged_a")

    merge_slabs = [(n, hh) for hh in (0, 1) for n in ("ga", "pa", "gb", "pb")]
    slab_list = [("z", 0), ("z", 1), ("v", 0), ("v", 1), ("u", 0), ("u", 1)] + [("ada", s) for s in range(4, 12)] \
        + merge_slabs + [("wo", 0), ("wo", 1)]
    core.slabs.begin(slab_list)
    tok = [(t, hh) for hh in (0, 1) for t in range(TT)]
    merge_tiles = [(n, m) for n, hh in merge_slabs for m in range(4 * hh, 4 * hh + 4)]
    core.banks.begin([("z", *k) for k in tok] + [("v", *k) for k in tok] + [("u", m) for m in range(KD)]
                     + [("ada", s) for s in range(4, 12)]
                     + [("yt", m) for m in range(KD)] + [("mx", g) for g in range(KD)]
                     + merge_tiles + [("wo", m) for m in range(KD)])
    tile_no = {k: n for n, k in enumerate(merge_tiles)}
    source = {("z", s): w_tiles(I["w_in"], 0, D, Z0 + 512 * s, 512) for s in (0, 1)}
    source |= {("v", s): w_tiles(I["w_in"], 0, D, V0 + 512 * s, 512) for s in (0, 1)}
    source |= {("u", s): w_tiles(I["w_in"], 0, D, U0 + 512 * s, 512) for s in (0, 1)}
    source |= {("ada", s): w_tiles(I["ada_w"], 0, D, 512 * s, 512) for s in range(4, 12)}
    source |= {("ga", s): w_tiles(I["w_in"], 0, D, GA + 512 * s, 512) for s in (0, 1)}
    source |= {("gb", s): w_tiles(I["w_in"], 0, D, GB + 512 * s, 512) for s in (0, 1)}
    source |= {("pa", s): w_tiles(I["w_pa"], 0, D, 512 * s, 512) for s in (0, 1)}
    source |= {("pb", s): w_tiles(I["w_pb"], 0, D, 512 * s, 512) for s in (0, 1)}
    source |= {("wo", s): w_tiles(I["w_o"], 0, D, 512 * s, 512) for s in (0, 1)}

    with nc.Block() as block:
        @block.sync
        def _(sp):
            sp.dma_start(ws[:, :, :], I["wsT"].rearrange("g j i -> j g i")).then_inc(rows_in, 16)
            sp.dma_start(rows[:, :], bcast_rows(I["rowsB"], 2 * D + KD * P)).then_inc(rows_in, 16)
            for n, key in enumerate(slab_list):
                load_slab(core, sp, key, source[key])
                if n == 2:
                    sp.dma_start(core.x[:, :, :], I["xT"].rearrange("(k p) n -> p k n", p=P)).then_inc(res_in, 16)

        @block.tensor
        def _(pe):
            prev = None

            def begin(key):
                nonlocal prev
                core.slabs.filled(pe, key)
                read, prev = (core.slabs.done(prev) if prev else None), key
                return read

            def by_feature(name, s, src, m0=0):
                read = begin((name, s))
                w = core.slab((name, s), KD, 512)
                for m in range(4):
                    key = (name, 4 * s + m)
                    core.banks.vacant(pe, key)
                    product(pe, core.ps(key)[:, :], [w[:, k, m * P:(m + 1) * P] for k in range(KD)],
                            [src[:, k, 0:T] for k in range(KD)], read if m == 0 else None)\
                        .then_inc(core.banks.put(key), 1)

            for name in ("z", "v"):
                for s in (0, 1):
                    read = begin((name, s))
                    w = core.slab((name, s), KD, 512)
                    for t in range(TT):
                        key = (name, t, s)
                        core.banks.vacant(pe, key)
                        product(pe, core.ps(key)[:, :], [a.xm[:, k, t * P:(t + 1) * P] for k in range(KD)],
                                [w[:, k, :] for k in range(KD)], read if t == 0 else None)\
                            .then_inc(core.banks.put(key), 1)
            for s in (0, 1):
                by_feature("u", s, a.xm)
            for s in range(4, 12):
                read = begin(("ada", s))
                core.banks.vacant(pe, ("ada", s))
                w = core.slab(("ada", s), KD, 512)
                for m in range(4):
                    last = product(pe, core.ps(("ada", s))[:, 2 * m:2 * m + 2],
                                   [w[:, k, m * P:(m + 1) * P] for k in range(KD)],
                                   [a.c[:, k, :] for k in range(KD)], read if m == 0 else None)
                last.then_inc(core.banks.put(("ada", s)), 1)
            pe.wait_ge(y_done, 1)
            for m in range(KD):
                core.banks.vacant(pe, ("yt", m))
                for t in range(TT):
                    last = pe.transpose(core.ps(("yt", m))[:, t * P:(t + 1) * P], a.y[:, t, m * P:(m + 1) * P],
                                        core.c("ident"))
                last.then_inc(core.banks.put(("yt", m)), 1)
            pe.wait_ge(rows_in, 32)
            pe.wait_ge(v_ready, TT)
            for g in range(KD):
                core.banks.vacant(pe, ("mx", g))
                for c in range(TT):
                    last = pe.matmul(core.ps(("mx", g))[:, c * P:(c + 1) * P], v[:, c, g * P:(g + 1) * P],
                                     ws[:, g, :], start=True, stop=True)
                last.then_inc(core.banks.put(("mx", g)), 1)
            for hh in (0, 1):
                by_feature("ga", hh, a.xm)
                pe.wait_ge(yt_done, KD)
                by_feature("pa", hh, yt)
                by_feature("gb", hh, a.xm)
                pe.wait_ge(sgu_done, KD)
                by_feature("pb", hh, u)
            pe.wait_ge(merged_done, KD)
            for s in (0, 1):
                by_feature("wo", s, merged)
            pe.drain().then_inc(core.slabs.done(("wo", 1)), 1)

        @block.scalar
        def _(act):
            for n, (t, hh) in enumerate(tok):
                core.banks.filled(act, ("z", t, hh))
                if n >= 2:
                    act.wait_ge(zs_used, n - 1)
                act.activation(zs[:, n % 2, :], core.ps(("z", t, hh))[:, :], ACT.Silu)\
                   .then_inc(core.banks.done(("z", t, hh)), 1)
                act.drain().then_inc(zs_done, 1)
            for n, (t, hh) in enumerate(tok):
                core.banks.filled(act, ("v", t, hh))
                act.activation(v[:, t, hh * 512:hh * 512 + 512], core.ps(("v", t, hh))[:, :], ACT.Gelu_apprx_tanh)\
                   .then_inc(core.banks.done(("v", t, hh)), 1)
                act.drain().then_inc(v_done, 1)
            for m in range(KD):
                core.banks.filled(act, ("u", m))
                act.activation(u[:, m, :], core.ps(("u", m))[:, :], ACT.Gelu_apprx_tanh)\
                   .then_inc(core.banks.done(("u", m)), 1)
            act.drain().then_inc(u_done, 1)
            act.wait_ge(gated, 2 * TT)
            for t in range(TT):
                for g in range(GROUPS):
                    act.activation(tmp[:, 0, 0:256], a.y[:, t, g * 256:(g + 1) * 256], ACT.Square,
                                   accum_out=ssq[:, t, g:g + 1])
                    act.drain()
            act.activation(ssq[:, :, :], ssq[:, :, :], ACT.Sqrt, scale=1.0 / 256, bias=core.c("eps6"))
            act.wait_ge(mv_done, 1)
            act.activation(mv[:, :, 1:2], mv[:, :, 1:2], ACT.Sqrt, bias=core.c("eps6"))
            act.drain().then_inc(root2_done, 1)
            for m in range(KD):
                core.banks.filled(act, ("yt", m))
                act.activation(yt[:, m, :], core.ps(("yt", m))[:, :], ACT.Identity,
                               scale=core.v("ssd_norm_w", m)).then_inc(core.banks.done(("yt", m)), 1)
                act.drain().then_inc(yt_done, 1)
            k = 0
            for hh in (0, 1):
                for name in ("ga", "gb"):
                    if k:
                        act.wait_ge(merged_a, 4 * k)
                    for m in range(4 * hh, 4 * hh + 4):
                        core.banks.filled(act, (name, m))
                        act.activation(gate[:, m % 4, :], core.ps((name, m))[:, :], ACT.Sigmoid)\
                           .then_inc(core.banks.done((name, m)), 1)
                        act.drain().then_inc(gate_done, 1)
                    k += 1

        @block.vector
        def _(dve):
            for n, (t, hh) in enumerate(tok):
                dve.wait_ge(zs_done, n + 1)
                dst = a.y[:, t, hh * 512:hh * 512 + 512]
                dve.tensor_tensor(dst, dst, zs[:, n % 2, :], ALU.mult).then_inc(zs_used, 1)
                dve.drain().then_inc(gated, 1)
            for n, (t, hh) in enumerate(tok):
                dve.wait_ge(v_done, n + 1)
                dve.bn_stats(bn[:, t, hh, :], v[:, t, hh * 512:hh * 512 + 512])
            dve.drain()
            for t in range(TT):
                dve.bn_aggr(mv[:, t, :], bn[:, t, :, :].rearrange("p a b -> p (a b)"))
            dve.drain().then_inc(mv_done, 1)
            for s in range(4, 12):
                core.banks.filled(dve, ("ada", s))
                bias = core.v("ada_b", 4 * s, 4).unsqueeze(2).broadcast_to([P, 4, 2])
                dve.tensor_tensor(core.mod[:, 4 * s:4 * s + 4, :],
                                  core.ps(("ada", s))[:, 0:8].rearrange("p (m j) -> p m j", j=2), bias,
                                  ALU.add).then_inc(core.banks.done(("ada", s)), 1)
            dve.wait_ge(root2_done, 1)
            dve.reciprocal(ssq[:, :, :], ssq[:, :, :])
            dve.reciprocal(mv[:, :, 1:2], mv[:, :, 1:2])
            dve.drain()
            for t in range(TT):
                dst = a.y[:, t, :].rearrange("p (g f) -> p g f", g=GROUPS)
                dve.tensor_tensor(dst, dst, ssq[:, t, :].unsqueeze(2).broadcast_to([P, GROUPS, 256]), ALU.mult)
            dve.drain().then_inc(y_done, 1)
            for t in range(TT):
                dve.tensor_scalar(v[:, t, :], v[:, t, :], mv[:, t, 0:1], mv[:, t, 1:2], ALU.subtract, ALU.mult)
                dve.drain().then_inc(v_norm, 1)
            dve.wait_ge(u_done, 1)
            for g in range(KD):
                core.banks.filled(dve, ("mx", g))
                mixed = tmp[:, 1, :]
                dve.tensor_tensor(mixed.rearrange("p (c i) -> p c i", i=P),
                                  core.ps(("mx", g))[:, :].rearrange("p (c i) -> p c i", i=P),
                                  b_s[:, g * P:(g + 1) * P].unsqueeze(1).broadcast_to([P, TT, P]), ALU.add)\
                   .then_inc(core.banks.done(("mx", g)), 1)
                dve.drain()
                dve.tensor_tensor(u[:, g, :], u[:, g, :], mixed, ALU.mult)
                dve.drain().then_inc(sgu_done, 1)
            k = 0
            for hh in (0, 1):
                for name in ("pa", "pb"):
                    for m in range(4 * hh, 4 * hh + 4):
                        dve.wait_ge(gate_done, k + 1)
                        core.banks.filled(dve, (name, m))
                        k += 1
                        if name == "pa":
                            dve.tensor_tensor(merged[:, m, :], core.ps((name, m))[:, :], gate[:, m % 4, :], ALU.mult)\
                               .then_inc(core.banks.done((name, m)), 1)
                            dve.drain().then_inc(merged_a, 1)
                        else:
                            dve.tensor_tensor(tmp[:, 1, :], core.ps((name, m))[:, :], gate[:, m % 4, :], ALU.mult)\
                               .then_inc(core.banks.done((name, m)), 1)
                            dve.drain().then_inc(merged_a, 1)
                            dve.tensor_tensor(merged[:, m, :], merged[:, m, :], tmp[:, 1, :], ALU.add)
                            dve.drain().then_inc(merged_done, 1)
            dve.wait_ge(res_in, 16)
            for m in range(KD):
                core.banks.filled(dve, ("wo", m))
                dve.scalar_tensor_tensor(out=core.x[:, m, :], in0=core.ps(("wo", m))[:, :],
                                         scalar=core.mod[:, 2 * KD + m, 0:1], in1=core.x[:, m, :],
                                         op0=ALU.mult, op1=ALU.add).then_inc(core.banks.done(("wo", m)), 1)

        @block.gpsimd
        def _(pool):
            pool.wait_ge(rows_in, 32)
            for t in range(TT):
                pool.wait_ge(v_norm, t + 1)
                pool.tensor_tensor(v[:, t, :], v[:, t, :], ln_w, ALU.mult)
                pool.drain()
                pool.tensor_tensor(v[:, t, :], v[:, t, :], ln_b, ALU.add)
                pool.drain().then_inc(v_ready, 1)


def router(core, ctx, b):
    core.stage = "router_"
    nc, I = core.nc, core.ins
    sem = lambda n: core.sem(n, ctx)
    xf = core.sb("xf", [P, KD, T], ctx)
    gates = core.sb("gates", [P, TT, EXPERTS * CAP], ctx)
    sq = core.sb("sq", [P, 2, T], ctx)
    rstd = core.sb("rstd", [P, T], ctx)
    scale2 = core.sb("scale2", [P, KD], ctx)
    rw = core.sb("rw", [P, KD, EXPERTS], ctx)
    aff = core.sb("aff", [P, TT, EXPERTS], ctx)
    top = core.sb("top", [P, TT], ctx)
    den = core.sb("den", [P, TT], ctx)
    pos = core.sb("pos", [P, TT, EXPERTS], ctx)
    mask = core.sb("mask", [P, TT, EXPERTS], ctx)
    work = core.sb("work", [EXPERTS, T], ctx)
    best = core.sb("best", [EXPERTS, 8], ctx)
    names = ["rw_in", "sq_done", "sq_used", "root_done", "scaled", "xf_done", "top_done", "exp_done", "aff_done",
             "mask_done", "masked_done", "pick_done", "gates_done"]
    rw_in, sq_done, sq_used, root_done, scaled, xf_done, top_done, exp_done, aff_done, mask_done, masked_done, \
        pick_done, gates_done = (sem(n) for n in names)
    PAIRS = EXPERTS // 2
    core.slabs.begin([])
    core.banks.begin(["rms", "logits"] + [("xt", t, hh) for t in range(TT) for hh in (0, 1)]
                     + ["aff", "mask", "pos"] + [("put", p) for p in range(PAIRS)])
    with nc.Block() as block:
        @block.sync
        def _(sp):
            sp.dma_start(rw[:, :, :], w_tiles(I["router_w"], 0, D, 0, EXPERTS)).then_inc(rw_in, 16)

        @block.tensor
        def _(pe):
            core.banks.vacant(pe, "rms")
            for k in range(KD):
                pe.wait_ge(sq_done, k + 1)
                last = pe.matmul(core.ps("rms")[:, :], core.c("mean_d"), sq[:, k % 2, :], start=k == 0, stop=k == KD - 1)
                if k < KD - 1:
                    last.then_inc(sq_used, 1)
            last.then_inc(core.banks.put("rms"), 1)
            pe.wait_ge(xf_done, KD)
            pe.wait_ge(rw_in, 16)
            core.banks.vacant(pe, "logits")
            for t in range(TT):
                last = product(pe, core.ps("logits")[:, t * EXPERTS:(t + 1) * EXPERTS],
                               [xf[:, k, t * P:(t + 1) * P] for k in range(KD)], [rw[:, k, :] for k in range(KD)])
            last.then_inc(core.banks.put("logits"), 1)
            for t in range(TT):
                for hh in (0, 1):
                    core.banks.vacant(pe, ("xt", t, hh))
                    for m in range(4):
                        last = pe.transpose(core.ps(("xt", t, hh))[:, m * P:(m + 1) * P],
                                            xf[:, 4 * hh + m, t * P:(t + 1) * P], core.c("ident"))
                    last.then_inc(core.banks.put(("xt", t, hh)), 1)
            pe.wait_ge(aff_done, 1)
            core.banks.vacant(pe, "aff")
            for t in range(TT):
                last = pe.transpose(core.ps("aff")[0:EXPERTS, t * P:(t + 1) * P], aff[:, t, :], core.c("ident"))
            last.then_inc(core.banks.put("aff"), 1)
            pe.wait_ge(mask_done, 1)
            core.banks.vacant(pe, "mask")
            for t in range(TT):
                last = pe.transpose(core.ps("mask")[:, t * EXPERTS:(t + 1) * EXPERTS], work[:, t * P:(t + 1) * P],
                                    core.c("ident")[0:EXPERTS, 0:EXPERTS])
            last.then_inc(core.banks.put("mask"), 1)
            pe.wait_ge(masked_done, 1)
            core.banks.vacant(pe, "pos")
            for t in range(TT):
                last = product(pe, core.ps("pos")[:, t * EXPERTS:(t + 1) * EXPERTS],
                               [core.c("ones")] * t + [core.c("tri_f")], [mask[:, j, :] for j in range(t + 1)])
            last.then_inc(core.banks.put("pos"), 1)
            pe.wait_ge(gates_done, TT)
            for p in range(PAIRS):
                core.banks.vacant(pe, ("put", p))
                for t in range(TT):
                    last = pe.transpose(core.ps(("put", p))[:, t * P:(t + 1) * P], gates[:, t, p * P:(p + 1) * P],
                                        core.c("ident"))
                last.then_inc(core.banks.put(("put", p)), 1)

        @block.scalar
        def _(act):
            for k in range(KD):
                if k >= 2:
                    act.wait_ge(sq_used, k - 1)
                act.activation(sq[:, k % 2, :], core.x[:, k, :], ACT.Square).then_inc(sq_done, 1)
            core.banks.filled(act, "rms")
            act.activation(rstd[:, :], core.ps("rms")[:, :], ACT.Sqrt, bias=core.c("eps6"))\
               .then_inc(core.banks.done("rms"), 1)
            act.drain().then_inc(root_done, 1)
            for k in range(KD):
                act.wait_ge(scaled, k + 1)
                act.activation(xf[:, k, :], xf[:, k, :], ACT.Identity, bias=core.mod[:, 3 * KD + k, 0:1])\
                   .then_inc(xf_done, 1)
            act.wait_ge(top_done, 1)
            for t in range(TT):
                act.activation(aff[:, t, :], aff[:, t, :], ACT.Exp, bias=top[:, t:t + 1], accum_out=den[:, t:t + 1])
            act.drain().then_inc(exp_done, 1)
            for t in range(TT):
                for hh in (0, 1):
                    core.banks.filled(act, ("xt", t, hh))
                    act.activation(b.xf_tok[:, t, hh * 512:hh * 512 + 512], core.ps(("xt", t, hh))[:, :], ACT.Identity)\
                       .then_inc(core.banks.done(("xt", t, hh)), 1)
            for p in range(PAIRS):
                core.banks.filled(act, ("put", p))
                act.activation(b.put[:, p, :], core.ps(("put", p))[:, :], ACT.Identity)\
                   .then_inc(core.banks.done(("put", p)), 1)

        @block.vector
        def _(dve):
            dve.tensor_scalar(scale2[:, :], core.mod[:, 4 * KD:5 * KD, 0], 1.0, None, ALU.add)
            dve.drain()
            dve.tensor_tensor(scale2[:, :], scale2[:, :], core.v("norm2_w", 0, KD), ALU.mult)
            dve.wait_ge(root_done, 1)
            dve.reciprocal(rstd[:, :], rstd[:, :])
            dve.drain()
            for k in range(KD):
                dve.scalar_tensor_tensor(out=xf[:, k, :], in0=core.x[:, k, :], scalar=scale2[:, k:k + 1],
                                         in1=rstd[:, :], op0=ALU.mult, op1=ALU.mult).then_inc(scaled, 1)
            core.banks.filled(dve, "logits")
            dve.tensor_copy(aff[:, :, :], core.ps("logits")[:, 0:TT * EXPERTS].rearrange("p (t e) -> p t e", e=EXPERTS))\
               .then_inc(core.banks.done("logits"), 1)
            dve.drain()
            dve.tensor_reduce(top[:, :], aff[:, :, :], AX.X, ALU.max)
            dve.drain()
            dve.tensor_scalar(top[:, :], top[:, :], -1.0, None, ALU.mult)
            dve.drain().then_inc(top_done, 1)
            dve.wait_ge(exp_done, 1)
            dve.reciprocal(den[:, :], den[:, :])
            dve.drain()
            dve.tensor_tensor(aff[:, :, :], aff[:, :, :], den[:, :].unsqueeze(2).broadcast_to([P, TT, EXPERTS]), ALU.mult)
            dve.drain().then_inc(aff_done, 1)
            core.banks.filled(dve, "aff")
            dve.tensor_copy(work[:, :], core.ps("aff")[0:EXPERTS, :]).then_inc(core.banks.done("aff"), 1)
            for _ in range(CAP // 8):
                dve.drain()
                dve.max(best[:, :], work[:, :])
                dve.drain()
                dve.match_replace(work[:, :], best[:, :], work[:, :], -1.0)
            dve.drain()
            dve.tensor_scalar(work[:, :], work[:, :], 0.0, None, ALU.is_lt)
            dve.drain().then_inc(mask_done, 1)
            core.banks.filled(dve, "mask")
            dve.tensor_copy(mask[:, :, :], core.ps("mask")[:, 0:TT * EXPERTS].rearrange("p (t e) -> p t e", e=EXPERTS))\
               .then_inc(core.banks.done("mask"), 1)
            dve.drain().then_inc(masked_done, 1)
            core.banks.filled(dve, "pos")
            dve.tensor_tensor(pos[:, :, :], core.ps("pos")[:, 0:TT * EXPERTS].rearrange("p (t e) -> p t e", e=EXPERTS),
                              mask[:, :, :], ALU.mult).then_inc(core.banks.done("pos"), 1)
            dve.drain()
            over = lambda ap: ap.unsqueeze(2).broadcast_to([P, EXPERTS, CAP])
            for t in range(TT):
                dve.tensor_tensor(b.pick[:, t, :].rearrange("p (e s) -> p e s", s=CAP),
                                  core.c("slot").unsqueeze(1).broadcast_to([P, EXPERTS, CAP]), over(pos[:, t, :]),
                                  ALU.is_equal).then_inc(pick_done, 1)

        @block.gpsimd
        def _(pool):
            pool.wait_ge(aff_done, 1)
            for t in range(TT):
                pool.wait_ge(pick_done, t + 1)
                pool.tensor_tensor(gates[:, t, :].rearrange("p (e s) -> p e s", s=CAP),
                                   b.pick[:, t, :].rearrange("p (e s) -> p e s", s=CAP),
                                   aff[:, t, :].unsqueeze(2).broadcast_to([P, EXPERTS, CAP]), ALU.mult)\
                    .then_inc(gates_done, 1)


def experts(core, ctx, b):
    core.stage = "experts_"
    nc, I = core.nc, core.ins
    sem = lambda n: core.sem(n, ctx)
    PAIRS = EXPERTS // 2
    xg = core.sb("xg", [P, KD, 2, P], ctx)
    ht = core.sb("ht", [P, KD, 2, P], ctx)
    hid = core.sb("hid", [P, D], ctx)
    y = core.sb("yslot", [P, D], ctx)
    zero_done, xg_done, silu_done, hid_done, ht_done, y_done = (
        sem(n) for n in ("zero_done", "xg_done", "silu_done", "hid_done", "ht_done", "yslot_done"))
    slab_list = [(n, hh, e) for n in ("g", "u") for hh in (0, 1) for e in (0, 1)]
    slab_list = [(n, hh, e) for hh in (0, 1) for n in ("g", "u") for e in (0, 1)] \
        + [("d", hh, e) for hh in (0, 1) for e in (0, 1)]
    core.slabs.begin(slab_list, reps=PAIRS)
    core.banks.begin([("xg", 0), ("xg", 1)] + [(n, hh) for hh in (0, 1) for n in ("g", "u")]
                     + [("ht", 0), ("ht", 1), ("d", 0), ("d", 1)] + [("sc", m) for m in range(KD)], reps=PAIRS)
    banks, slabs = core.banks, core.slabs
    weight = {"g": I["w_gate"], "u": I["w_up"], "d": I["w_down"]}

    with nc.Block() as block:
        @block.sync
        def _(sp):
            with sp.Fori(0, PAIRS) as i:
                for key in slab_list:
                    n, hh, e = key
                    at = sp.snap(2 * i + e, min_val=0, max_val=EXPERTS - 1)
                    src = weight[n][bass.ds(at, 1), :, 512 * hh:512 * hh + 512]\
                        .rearrange("a (k p) n -> p (a k) n", p=P)
                    load_slab(core, sp, key, src, i)

        @block.tensor
        def _(pe):
            pe.wait_ge(zero_done, 2)
            with pe.Fori(0, PAIRS) as i:
                col = pe.snap(i * P, min_val=0, max_val=(PAIRS - 1) * P)
                for q in (0, 1):
                    banks.vacant(pe, ("xg", q), i)
                    for m in range(4):
                        last = product(pe, core.ps(("xg", q))[:, m * P:(m + 1) * P],
                                       [b.xf_tok[:, t, (4 * q + m) * P:(4 * q + m + 1) * P] for t in range(TT)],
                                       [b.pick[:, t, bass.ds(col, P)] for t in range(TT)])
                    last.then_inc(banks.put(("xg", q)), 1)
                pe.wait_ge(xg_done, 2 * i + 2)

                prev = None

                def both(n, hh, lhs):
                    nonlocal prev
                    banks.vacant(pe, (n, hh), i)
                    for e in (0, 1):
                        slabs.filled(pe, (n, hh, e), i)
                        w = core.slab((n, hh, e), KD, 512)
                        for k in range(KD):
                            last = pe.matmul(core.ps((n, hh))[:, :], lhs[:, k, e, :], w[:, k, :],
                                             start=e == 0 and k == 0, stop=e == 1 and k == KD - 1)
                            if k == 0 and prev:
                                last.then_inc(slabs.done(prev), 1)
                        prev = (n, hh, e)
                    last.then_inc(banks.put((n, hh)), 1)

                for hh in (0, 1):
                    for n in ("g", "u"):
                        both(n, hh, xg)
                for q in (0, 1):
                    pe.wait_ge(hid_done, 2 * i + q + 1)
                    banks.vacant(pe, ("ht", q), i)
                    for m in range(4):
                        last = pe.transpose(core.ps(("ht", q))[:, m * P:(m + 1) * P],
                                            hid[:, (4 * q + m) * P:(4 * q + m + 1) * P], core.c("ident"))
                        if prev:
                            last.then_inc(slabs.done(prev), 1)
                            prev = None
                    last.then_inc(banks.put(("ht", q)), 1)
                pe.wait_ge(ht_done, 2 * i + 2)
                for hh in (0, 1):
                    both("d", hh, ht)
                pe.wait_ge(y_done, 2 * i + 2)
                for m in range(KD):
                    banks.vacant(pe, ("sc", m), i)
                    if prev:
                        pe.nop().then_inc(slabs.done(prev), 1)
                        prev = None
                    pe.matmul(core.ps(("sc", m))[:, :], y[:, m * P:(m + 1) * P], b.put[:, bass.ds(i, 1), :]
                              .rearrange("p a n -> p (a n)"), start=True, stop=True).then_inc(banks.put(("sc", m)), 1)

        @block.scalar
        def _(act):
            with act.Fori(0, PAIRS) as i:
                for hh in (0, 1):
                    banks.filled(act, ("g", hh), i)
                    act.activation(hid[:, hh * 512:hh * 512 + 512], core.ps(("g", hh))[:, :], ACT.Silu)\
                       .then_inc(banks.done(("g", hh)), 1)
                    act.drain().then_inc(silu_done, 1)
                for hh in (0, 1):
                    banks.filled(act, ("d", hh), i)
                    act.activation(y[:, hh * 512:hh * 512 + 512], core.ps(("d", hh))[:, :], ACT.Identity)\
                       .then_inc(banks.done(("d", hh)), 1)
                    act.drain().then_inc(y_done, 1)

        @block.vector
        def _(dve):
            def spread(name, dst, q, i, done):
                banks.filled(dve, (name, q), i)
                src = core.ps((name, q))[:, :].rearrange("p (m c) -> p m c", c=P)
                dve.tensor_copy(dst[:, 4 * q:4 * q + 4, 0, 0:CAP], src[:, :, 0:CAP])
                dve.tensor_copy(dst[:, 4 * q:4 * q + 4, 1, CAP:P], src[:, :, CAP:P]).then_inc(banks.done((name, q)), 1)
                dve.drain().then_inc(done, 1)

            with dve.Fori(0, PAIRS) as i:
                for q in (0, 1):
                    spread("xg", xg, q, i, xg_done)
                for hh in (0, 1):
                    dve.wait_ge(silu_done, 2 * i + hh + 1)
                    banks.filled(dve, ("u", hh), i)
                    dst = hid[:, hh * 512:hh * 512 + 512]
                    dve.tensor_tensor(dst, dst, core.ps(("u", hh))[:, :], ALU.mult).then_inc(banks.done(("u", hh)), 1)
                    dve.drain().then_inc(hid_done, 1)
                for q in (0, 1):
                    spread("ht", ht, q, i, ht_done)
                for m in range(KD):
                    banks.filled(dve, ("sc", m), i)
                    dve.scalar_tensor_tensor(out=core.x[:, m, :], in0=core.ps(("sc", m))[:, :],
                                             scalar=core.mod[:, 5 * KD + m, 0:1], in1=core.x[:, m, :],
                                             op0=ALU.mult, op1=ALU.add).then_inc(banks.done(("sc", m)), 1)

        @block.gpsimd
        def _(pool):
            pool.memset(xg[:, :, :, :], 0.0).then_inc(zero_done, 1)
            pool.memset(ht[:, :, :, :], 0.0).then_inc(zero_done, 1)


def blocked(ap):
    return ap.rearrange("p (r n c) -> p n r c", n=NBLK, c=QB)


class Norm:

    def __init__(self, core, ctx, per):
        self.core, self.per = core, per
        self.sq = core.sb("norm_sq", [P, 2, T], ctx)
        self.rstd = core.sb("norm_rstd", [P, T], ctx)
        self.summand, self.centred, self.squared, self.square_read, self.root, self.scaled, self.ready = (
            core.sem("norm_" + n, ctx)
            for n in ("summand", "centred", "squared", "square_read", "root", "scaled", "ready"))

    def at(self, i, n, k, each=KD):
        return i * (self.per * each) + n * each + k

    def tensor(self, pe, i, n, read=None):
        core, banks = self.core, self.core.banks
        banks.vacant(pe, ("mean", n), i)
        for k in range(KD):
            pe.wait_ge(self.summand, self.at(i, n, k + 1))
            last = pe.matmul(core.ps(("mean", n))[:, :], core.c("mean_d"), core.x[:, k, :],
                             start=k == 0, stop=k == KD - 1)
            if k == 0 and read is not None:
                last.then_inc(read, 1)
        last.then_inc(banks.put(("mean", n)), 1)
        banks.vacant(pe, ("var", n), i)
        for k in range(KD):
            pe.wait_ge(self.squared, self.at(i, n, k + 1))
            last = pe.matmul(core.ps(("var", n))[:, :], core.c("mean_d"), self.sq[:, k % 2, :],
                             start=k == 0, stop=k == KD - 1)
            if k < KD - 1:
                last.then_inc(self.square_read, 1)
        last.then_inc(banks.put(("var", n)), 1)

    def vector(self, dve, i, n, gain):
        core, banks = self.core, self.core.banks
        banks.filled(dve, ("mean", n), i)
        for k in range(KD):
            last = dve.tensor_tensor(core.x[:, k, :], core.x[:, k, :], core.ps(("mean", n))[:, :], ALU.subtract)
            if k == KD - 1:
                last.then_inc(banks.done(("mean", n)), 1)
                dve.drain().then_inc(self.centred, 1)
            else:
                last.then_inc(self.centred, 1)
        dve.wait_ge(self.root, self.at(i, n, 1, 1))
        dve.reciprocal(self.rstd[:, :], self.rstd[:, :])
        dve.drain()
        for k in range(KD):
            dve.scalar_tensor_tensor(out=core.x[:, k, :], in0=core.x[:, k, :], scalar=gain(k),
                                     in1=self.rstd[:, :], op0=ALU.mult, op1=ALU.mult).then_inc(self.scaled, 1)

    def scalar(self, act, i, n, shift):
        core, banks = self.core, self.core.banks
        for k in range(KD):
            act.wait_ge(self.centred, self.at(i, n, k + 1))
            if k >= 2:
                act.wait_ge(self.square_read, self.at(i, n, k - 1, KD - 1))
            act.activation(self.sq[:, k % 2, :], core.x[:, k, :], ACT.Square).then_inc(self.squared, 1)
        banks.filled(act, ("var", n), i)
        act.activation(self.rstd[:, :], core.ps(("var", n))[:, :], ACT.Sqrt, bias=core.c("eps5"))\
           .then_inc(banks.done(("var", n)), 1)
        act.drain().then_inc(self.root, 1)
        for k in range(KD):
            act.wait_ge(self.scaled, self.at(i, n, k + 1))
            act.activation(core.x[:, k, :], core.x[:, k, :], ACT.Identity, bias=shift(k)).then_inc(self.ready, 1)


def entry(core, ctx):
    core.stage = "entry_"
    nc = core.nc
    sem = lambda n: core.sem(n, ctx)
    norm = Norm(core, ctx, 1)
    old = core.sb("old", [P, KD, T], ctx)
    sq_done, sq_used, root_done = sem("sq_done"), sem("sq_used"), sem("root_done")
    core.slabs.begin([])
    core.banks.begin(["rms", ("mean", 0), ("var", 0)])
    with nc.Block() as block:
        @block.tensor
        def _(pe):
            core.banks.vacant(pe, "rms")
            for k in range(KD):
                pe.wait_ge(sq_done, k + 1)
                last = pe.matmul(core.ps("rms")[:, :], core.c("mean_d"), norm.sq[:, k % 2, :], start=k == 0, stop=k == KD - 1)
                if k < KD - 1:
                    last.then_inc(sq_used, 1)
            last.then_inc(core.banks.put("rms"), 1)
            norm.tensor(pe, 0, 0)

        @block.scalar
        def _(act):
            for k in range(KD):
                if k >= 2:
                    act.wait_ge(sq_used, k - 1)
                act.activation(norm.sq[:, k % 2, :], core.x[:, k, :], ACT.Square).then_inc(sq_done, 1)
            core.banks.filled(act, "rms")
            act.activation(norm.rstd[:, :], core.ps("rms")[:, :], ACT.Sqrt, bias=core.c("eps6"))\
               .then_inc(core.banks.done("rms"), 1)
            act.drain().then_inc(root_done, 1)
            norm.scalar(act, 0, 0, lambda k: core.v("ln_in_b_2", k))

        @block.vector
        def _(dve):
            dve.wait_ge(root_done, 1)
            dve.reciprocal(norm.rstd[:, :], norm.rstd[:, :])
            dve.drain()
            for k in range(KD):
                dve.scalar_tensor_tensor(out=old[:, k, :], in0=core.x[:, k, :], scalar=core.v("final_norm_w", k),
                                         in1=norm.rstd[:, :], op0=ALU.mult, op1=ALU.mult)
            dve.drain()
            for k in range(KD):
                dve.tensor_copy(core.x[:, k, :].rearrange("p (n r c) -> p n r c", n=NBLK, c=QB), blocked(old[:, k, :]))\
                   .then_inc(norm.summand, 1)
            norm.vector(dve, 0, 0, lambda k: core.v("ln_in_g_2", k))


def layer_plan():

    def attention(kind, heads, lag, before=None):
        units = [(kind, h, n) for h in range(heads) for n in range(TT)]
        out = []
        for x in range(len(units) + lag + 1):
            if before and x < len(units) and x % TT == 0:
                out += before(x // TT)
            if x < len(units):
                out.append(("scores", *units[x]))
            if lag <= x < len(units) + lag:
                out.append(("turn", *units[x - lag]))
            if x > lag and (x - lag) % TT == 0:
                h = (x - lag) // TT - 1
                if kind == "df" and h:
                    out.append(("msq", "df", h - 1))
                out.append(("values", kind, h))
        return out + [("msq", "df", heads - 1)] * (kind == "df")

    plan = [("feat", "naq", m) for m in range(4)] + [("feat", "nak", m) for m in range(4)]
    plan += [("tok", "nav", t) for t in range(TT)]
    plan += attention("na", NA_HEADS, 2)
    for w in ("dfq", "dfk"):
        for m in range(5):
            plan += [("feat", w, m)] * (m < 4) + [("swap", w, m - 1)] * (m > 0)
    plan += [("tok", "dfv", t) for t in range(TT)]
    plan += attention("df", DF_HEADS, 3)
    plan += [("feat", "cq", m) for m in range(3)] + [("feat", "ckv", m) for m in range(2)] + [("kr",)]
    plan += [("msq", "q"), ("msq", "kv"), ("swap", "kr", 0)]
    plan += [("mv", t) for t in range(TT)]
    plan += attention("ml", MLA_HEADS, 2, lambda h: [("mq", h), ("mk", h), ("swap", "mq", h)])
    for b in range(3):
        plan += [("gate", b, m) for m in range(KD)] + [("branch", b, m) for m in range(KD)]
    plan += [("wo", m) for m in range(KD)] + [("norm", 0)]
    plan += [e for f in range(KF) for e in (("fg", f), ("fu", f))]
    return plan + [("fo", m) for m in range(KD)] + [("norm", 1)]


def numbered(events, wanted):
    chosen = [e for e in events if wanted(e)]
    return {e: n for n, e in enumerate(chosen)}, len(chosen)


def layers(core, ctx, out):
    core.stage = "layers_"
    nc, I = core.nc, core.ins
    norm = Norm(core, ctx, 2)
    sem = lambda n: core.sem(n, ctx)
    con2 = core.sb("con2", [P, NCON2], ctx)
    c2 = lambda n: con2[:, CON2[n][0]:CON2[n][0] + CON2[n][1]]
    x, banks, slabs = core.x, core.banks, core.slabs
    lv = core.sb("lv", [P, NLAYER], ctx)
    vec = lambda n, k=0: lv[:, LAYER[n][0] + k:LAYER[n][0] + k + 1]
    work = core.sb("work", [P, 24 * T], ctx)
    tiles = lambda a, n: work[:, a * T:(a + n) * T].rearrange("p (m t) -> p m t", t=T)
    proj = {n: tiles(4 * k, 4) for k, n in enumerate(("naq", "nak", "nav", "dfq", "dfk", "dfv"))}
    proj |= {"cq": tiles(0, 3), "ckv": tiles(3, 2), "kr": tiles(5, 1), "mv": tiles(8, 4), "mq": tiles(12, 2), "mk": tiles(14, 2)}
    merged, hidden = tiles(0, 8), tiles(0, KF)
    heads_out = core.sb("heads_out", [P, 3, 4, T], ctx)
    NP = 8
    p = core.sb("p", [P, NP, T], ctx)
    pt = core.sb("pt", [P, 2, TT, T], ctx)
    gates = pt[:, :, :, :].rearrange("p a b t -> p (a b) t")
    table = core.sb("table", [P, NA_HEADS, RUN], ctx)
    lamv = core.sb("lamv", [P, 2, 2, 64], ctx)
    lam = core.sb("lam", [P, 8], ctx)
    side = table[:, :, :].rearrange("p h n -> p (h n)")[:, 0:2 * T].rearrange("p (a t) -> p a t", a=2)
    rot = norm.rstd

    plan = layer_plan()
    soft = [(*e[1:], j) for e in plan if e[0] == "scores" for j in range(1 + (e[1] == "df"))]
    NS = len(soft)
    soft_no = {s: n for n, s in enumerate(soft)}
    of_unit = lambda u: [soft_no[(*u, j)] for j in range(1 + (u[0] == "df"))]
    unit_no, UNITS = numbered(plan, lambda e: e[0] == "turn")
    head_no, HEADS_ALL = numbered(plan, lambda e: e[0] == "values")
    copy_no, COPIES = numbered(plan, lambda e: e[0] in ("feat", "tok", "kr", "mv", "mq", "mk"))
    swap_no, SWAPS = numbered(plan, lambda e: e[0] == "swap")
    scaled_no, SCALED = numbered(soft, lambda s: s[3] == 0)
    assert NS % NP == 0 and HEADS_ALL % 2 == 0
    SQUARES, LATENT = DF_HEADS + 5, 5
    negmax = core.sb("negmax", [P, NS], ctx)
    sums = core.sb("sums", [P, NS], ctx)
    recip = core.sb("recip", [P, NS], ctx)
    keys = []
    for e in plan:
        if e[0] == "scores":
            keys += [("scores", *e[1:], j) for j in range(1 + (e[1] == "df"))]
        else:
            keys += [("mean", e[1]), ("var", e[1])] if e[0] == "norm" else [e]
    banks.begin(keys, reps=LAYERS)

    def near(n):
        lo, hi = max(n - 1, 0), min(n + 1, NBLK - 1)
        return lo, hi - lo + 1

    W, G0 = "w_in_2", 3072 + QRANK + KVRANK + ROPE_D
    source = {n: (W, 0, D, 512 * k, 512) for k, n in enumerate(("naq", "nak", "nav", "dfq", "dfk", "dfv"))}
    source |= {"cq": (W, 0, D, 3072, QRANK), "ckv": (W, 0, D, 3072 + QRANK, KVRANK + ROPE_D), "mla": None}
    for b in range(3):
        source |= {("gate", b, hh): (W, 0, D, G0 + b * D + 512 * hh, 512) for hh in (0, 1)}
        source[("branch", b)] = ("w_branch_2", BR * b, BR, 0, D)
    source |= {("wo", hh): ("w_out_2", 0, D, 512 * hh, 512) for hh in (0, 1)}
    source |= {("ffn", f): ("w_ffn_in_2", 0, D, 4 * P * f, 4 * P) for f in range(KF // 2)}
    source |= {("fo", m): ("w_ffn_out_2", 0, FF, P * m, P) for m in range(KD)}
    slabs.begin(list(source), reps=LAYERS)

    const_in, layer_done, params_in, table_in = sem("const_in"), sem("layer_done"), sem("params_in"), sem("table_in")
    lam_sums, lam_exps, lam_done = sem("lam_sums"), sem("lam_exps"), sem("lam_done")
    copied, rotated, max_done, exp_done, recip_done, scaled, combined, turned, head_done = (
        sem(n) for n in ("copied", "rotated", "max_done", "exp_done", "recip_done", "scaled", "combined", "turned", "head_done"))
    squared, root_done, latent_done, gate_done, branch_done, silu_done, hidden_done, out_done = (
        sem(n) for n in ("squared", "root_done", "latent_done", "gate_done", "branch_done", "silu_done", "hidden_done", "out_done"))

    def free_slot(eng, s, i):
        if s >= NP:
            banks.filled_too(eng, ("turn", *soft[s - NP][:3]), ("scores", *soft[s]), i)

    with nc.Block() as block:
        @block.sync
        def _(sp):
            sp.dma_start(con2[:, :], I["con2"]).then_inc(const_in, 16)
            with sp.Fori(0, LAYERS) as i:
                at = sp.snap(i, min_val=0, max_val=LAYERS - 1)
                sp.wait_ge(layer_done, i + 1)
                sp.dma_start(lv[:, :], I["layer_vec"][bass.ds(at, 1)].rearrange("a p n -> (a p) n")).then_inc(params_in, 16)
                sp.dma_start(lamv[:, :, :, :].rearrange("p a b n -> p (a b n)"),
                             I["lam"][bass.ds(at, 1), :].broadcast_to([P, 256])).then_inc(params_in, 16)
                for r in range(ROWS):
                    lead = I["rpb"][bass.ds(at, 1), r * RPB_W:r * RPB_W + 1]
                    src = bass.AP(tensor=lead.tensor, offset=lead.offset, ap=[[1, QB], [RPB_H * RPB_W, NA_HEADS], [1, RUN]])
                    sp.dma_start(table[r * QB:(r + 1) * QB, :, :], src).then_inc(table_in, 16)
                for key, what in source.items():
                    if key == "mla":
                        load_slab(core, sp, key, I["w_mla_2"][bass.ds(at, 1)].rearrange("a p (k n) -> p (a k) n", k=1), i)
                        continue
                    name, r0, rows, c0, cols = what
                    load_slab(core, sp, key, I[name][bass.ds(at, 1), r0:r0 + rows, c0:c0 + cols]
                              .rearrange("a (k p) n -> p (a k) n", p=P), i)
            sp.wait_ge(norm.ready, LAYERS * 2 * KD)
            sp.dma_start(out.rearrange("(k p) n -> p k n", p=P), x[:, :, :]).then_inc(out_done, 16)
            sp.wait_ge(out_done, 16)

        @block.tensor
        def _(pe):
            pe.wait_ge(const_in, 16)
            xs = [x[:, k, :] for k in range(KD)]

            def layer(i):
                held = [None, None]

                def need(key):
                    if held[0] != key:
                        held[:] = [key, held[0]]
                        slabs.filled(pe, key, i)

                def emit(key, lhs, rhs, rows=P):
                    banks.vacant(pe, key, i)
                    read = slabs.done(held[1]) if held[1] is not None and len(lhs) > 1 else None
                    if read is not None:
                        held[1] = None
                    product(pe, core.ps(key)[0:rows, :], lhs, rhs, read).then_inc(banks.put(key), 1)

                def scores(kind, h, n):
                    q = slice(n * P, (n + 1) * P)
                    if kind == "na":
                        if (h, n) == (0, 0):
                            pe.wait_ge(copied, i * COPIES + copy_no[("feat", "nak", 3)] + 1)
                        lo, nb = near(n)
                        r = slice((h % 2) * 64, (h % 2) * 64 + 64)
                        key = ("scores", kind, h, n, 0)
                        banks.vacant(pe, key, i)
                        pe.matmul(core.ps(key)[:, 0:nb * P], proj["naq"][r, h // 2, q],
                                  proj["nak"][r, h // 2, lo * P:(lo + nb) * P], start=True, stop=True)\
                            .then_inc(banks.put(key), 1)
                    elif kind == "df":
                        if (h, n) == (0, 0):
                            pe.wait_ge(rotated, i * SWAPS + swap_no[("swap", "dfk", 3)] + 1)
                        for j in (0, 1):
                            r = slice(j * 64, j * 64 + 64)
                            emit(("scores", kind, h, n, j), [proj["dfq"][r, h, q]], [proj["dfk"][r, h, :]])
                    else:
                        if n == 0:
                            pe.wait_ge(copied, i * COPIES + copy_no[("mk", h)] + 1)
                            pe.wait_ge(rotated, i * SWAPS + swap_no[("swap", "mq", h)] + 1)
                        emit(("scores", kind, h, n, 0), [proj["mq"][0:96, h % 2, q]], [proj["mk"][0:96, h % 2, :]])

                def turn(kind, h, n):
                    key, s = ("turn", kind, h, n), soft_no[(kind, h, n, 0)]
                    if kind == "df":
                        pe.wait_ge(combined, i * (DF_HEADS * TT) + h * TT + n + 1)
                    else:
                        pe.wait_ge(scaled, i * SCALED + scaled_no[(kind, h, n, 0)] + 1)
                    banks.vacant(pe, key, i)
                    for b in range(near(n)[1] if kind == "na" else TT):
                        last = pe.transpose(core.ps(key)[:, b * P:(b + 1) * P], p[:, s % NP, b * P:(b + 1) * P], core.c("ident"))
                    last.then_inc(banks.put(key), 1)

                def values(kind, h):
                    key = ("values", kind, h)
                    turned_pt = pt[:, head_no[key] % 2]
                    v = proj[{"na": "nav", "df": "dfv", "ml": "mv"}[kind]]
                    if h == 0:
                        pe.wait_ge(copied, i * COPIES + copy_no[{"na": ("tok", "nav", 3), "df": ("tok", "dfv", 3),
                                                                 "ml": ("mv", 3)}[kind]] + 1)
                    pe.wait_ge(turned, i * UNITS + unit_no[("turn", kind, h, TT - 1)] + 1)
                    if kind == "na":
                        banks.vacant(pe, key, i)
                        for n in range(NBLK):
                            lo, nb = near(n)
                            last = product(pe, core.ps(key)[0:64, n * P:(n + 1) * P],
                                           [v[:, j, h * 64:h * 64 + 64] for j in range(lo, lo + nb)],
                                           [turned_pt[:, j, n * P:(n + 1) * P] for j in range(lo, lo + nb)])
                        last.then_inc(banks.put(key), 1)
                    else:
                        w = P if kind == "df" else 64
                        emit(key, [v[:, j, h * w:(h + 1) * w] for j in range(TT)], [turned_pt[:, j, :] for j in range(TT)], rows=w)

                for e in plan:
                    kind = e[0]
                    if kind == "feat":
                        need(e[1])
                        w = core.slab(e[1], KD, source[e[1]][4])
                        emit(e, [w[:, k, e[2] * P:(e[2] + 1) * P] for k in range(KD)], xs)
                    elif kind == "tok":
                        need(e[1])
                        w = core.slab(e[1], KD, 512)
                        emit(e, [x[:, k, e[2] * P:(e[2] + 1) * P] for k in range(KD)], [w[:, k, :] for k in range(KD)])
                    elif kind == "kr":
                        w = core.slab("ckv", KD, KVRANK + ROPE_D)
                        emit(e, [w[:, k, KVRANK + ROPE_D - 96:] for k in range(KD)], xs, rows=96)
                    elif kind == "swap":
                        of = {"kr": ("kr",), "mq": ("mq", e[2])}.get(e[1], ("feat", e[1], e[2]))
                        pe.wait_ge(copied, i * COPIES + copy_no[of] + 1)
                        rows, mat = (P, "dswap") if of[0] == "feat" else (96, "mswap")
                        src = proj[e[1]][0:rows, e[2] % (4 if of[0] == "feat" else 2), :]
                        emit(e, [c2(mat)[0:rows, 0:rows]], [src], rows=rows)
                    elif kind == "scores":
                        scores(*e[1:])
                    elif kind == "turn":
                        turn(*e[1:])
                    elif kind == "values":
                        values(*e[1:])
                    elif kind == "msq" and e[1] == "df":
                        pe.wait_ge(squared, i * SQUARES + e[2] + 1)
                        emit(e, [c2("mean_h")], [norm.sq[:, e[2] % 2, :]])
                    elif kind == "msq":
                        first, n, mat = (0, 3, "mean_q") if e[1] == "q" else (3, 2, "mean_kv")
                        pe.wait_ge(squared, i * SQUARES + DF_HEADS + first + n)
                        emit(e, [c2(mat)] * n, [p[:, first + j, :] for j in range(n)])
                    elif kind in ("mv", "mq", "mk"):
                        need("mla")
                        if e == ("mv", 0):
                            pe.wait_ge(latent_done, i * LATENT + LATENT)
                        slot = core.ring[:, slabs.slot("mla"), :]
                        wq = slot[:, 0:3 * 768].rearrange("p (k n) -> p k n", k=3)
                        wkv = slot[:, 3 * 768:].rearrange("p (k n) -> p k n", k=2)
                        if kind == "mv":
                            emit(e, [proj["ckv"][:, k, e[1] * P:(e[1] + 1) * P] for k in range(2)],
                                 [wkv[:, k, :].rearrange("p (h c) -> p h c", c=128)[:, :, 64:128] for k in range(2)])
                        elif kind == "mq":
                            emit(e, [wq[:, k, e[1] * 96:(e[1] + 1) * 96] for k in range(3)], [proj["cq"][:, k, :] for k in range(3)], rows=96)
                        else:
                            emit(e, [wkv[:, k, e[1] * P:e[1] * P + 64] for k in range(2)], [proj["ckv"][:, k, :] for k in range(2)], rows=64)
                    elif kind == "gate":
                        need(("gate", e[1], e[2] // 4))
                        w = core.slab(("gate", e[1], e[2] // 4), KD, 512)
                        emit(e, [w[:, k, (e[2] % 4) * P:(e[2] % 4 + 1) * P] for k in range(KD)], xs)
                    elif kind == "branch":
                        need(("branch", e[1]))
                        if e[2] == 0:
                            pe.wait_ge(head_done, i * HEADS_ALL + HEADS_ALL)
                        w = core.slab(("branch", e[1]), 4, D)
                        emit(e, [w[:, k, e[2] * P:(e[2] + 1) * P] for k in range(4)], [heads_out[:, e[1], k, :] for k in range(4)])
                    elif kind == "wo":
                        need(("wo", e[1] // 4))
                        if e[1] == 0:
                            pe.wait_ge(branch_done, i * (3 * KD) + 3 * KD)
                        w = core.slab(("wo", e[1] // 4), KD, 512)
                        emit(e, [w[:, k, (e[1] % 4) * P:(e[1] % 4 + 1) * P] for k in range(KD)], [merged[:, k, :] for k in range(KD)])
                    elif kind == "norm":
                        norm.tensor(pe, i, e[1], slabs.done(held[0]) if e[1] == 1 else None)
                        if e[1] == 1:
                            pe.wait_ge(norm.ready, norm.at(i, 1, KD))
                    elif kind in ("fg", "fu"):
                        need(("ffn", e[1] // 2))
                        if e == ("fg", 0):
                            pe.wait_ge(norm.ready, norm.at(i, 0, KD))
                        w = core.ring[:, slabs.slot(("ffn", e[1] // 2)), 0:KD * 4 * P].rearrange("p (k h n) -> p k h n", k=KD, h=2)
                        col = (e[1] % 2) * P
                        emit(e, [w[:, k, int(kind == "fu"), col:col + P] for k in range(KD)], xs)
                    else:
                        need(e)
                        if e[1] == 0:
                            pe.wait_ge(hidden_done, i * KF + KF)
                        w = core.slab(e, KF, P)
                        emit(e, [w[:, k, :] for k in range(KF)], [hidden[:, k, :] for k in range(KF)])

            with pe.Fori(0, LAYERS) as i:
                layer(i)

        @block.scalar
        def _(act):
            act.drain().then_inc(layer_done, 1)

            def layer(i):
                act.wait_ge(lam_sums, i + 1)
                act.activation(lam[:, 2:4], lam[:, 0:2], ACT.Exp).then_inc(lam_exps, 1)
                act.wait_ge(params_in, i * 32 + 32)

                def copy(e, dst, rows=P, scale=1.0):
                    banks.filled(act, e, i)
                    act.activation(dst, core.ps(e)[0:rows, :], ACT.Identity, scale=scale).then_inc(banks.done(e), 1)
                    act.drain().then_inc(copied, 1)

                for e in plan:
                    kind = e[0]
                    if kind in ("feat", "tok"):
                        copy(e, proj[e[1]][:, e[2], :], scale=0.125 if e[1] == "naq" else 1.0)
                        if e[1] in ("cq", "ckv"):
                            n = e[2] + (3 if e[1] == "ckv" else 0)
                            if n == 0:
                                banks.filled_too(act, ("turn", "df", DF_HEADS - 1, TT - 1), e, i)
                            act.activation(p[:, n, :], proj[e[1]][:, e[2], :], ACT.Square).then_inc(squared, 1)
                    elif kind == "kr":
                        copy(e, proj["kr"][0:96, 0, :], rows=96)
                    elif kind == "mv":
                        copy(e, proj["mv"][:, e[1], :])
                    elif kind in ("mq", "mk"):
                        if e[1] >= 2:
                            banks.filled_too(act, ("scores", "ml", e[1] - 2, TT - 1, 0), e, i)
                        rows = 96 if kind == "mq" else 64
                        copy(e, proj[kind][0:rows, e[1] % 2, :], rows=rows)
                    elif kind == "scores":
                        for s in of_unit(e[1:]):
                            act.wait_ge(max_done, i * NS + s + 1)
                            key = ("scores", *soft[s])
                            if e[1] == "na":
                                w = near(e[3])[1] * P
                                act.activation(p[:, s % NP, 0:w], p[:, s % NP, 0:w], ACT.Exp, bias=negmax[:, s:s + 1],
                                               accum_out=sums[:, s:s + 1])
                            else:
                                banks.filled(act, key, i)
                                free_slot(act, s, i)
                                if s - soft_no[("ml", 0, 0, 0)] in range(NP):
                                    banks.filled_too(act, ("msq", "kv"), key, i)
                                act.activation(p[:, s % NP, :], core.ps(key)[:, :], ACT.Exp, bias=negmax[:, s:s + 1],
                                               scale=SCALE[e[1]], accum_out=sums[:, s:s + 1]).then_inc(banks.done(key), 1)
                            act.drain().then_inc(exp_done, 1)
                    elif kind == "turn":
                        banks.filled(act, e, i)
                        lo, nb = near(e[3]) if e[1] == "na" else (0, TT)
                        hd = head_no[("values", e[1], e[2])]
                        if e[3] == 0 and hd >= 2:
                            banks.filled_too(act, [k for k, n in head_no.items() if n == hd - 2][0], e, i)
                        act.activation(pt[:, hd % 2, lo:lo + nb, e[3] * P:(e[3] + 1) * P],
                                       core.ps(e)[:, 0:nb * P].rearrange("p (b q) -> p b q", q=P), ACT.Identity)\
                           .then_inc(banks.done(e), 1)
                        act.drain().then_inc(turned, 1)
                    elif kind == "values" and e[1] == "df":
                        banks.filled(act, e, i)
                        if e[2] >= 2:
                            banks.filled_too(act, ("msq", "df", e[2] - 2), e, i)
                        act.activation(norm.sq[:, e[2] % 2, :], core.ps(e)[:, :], ACT.Square).then_inc(squared, 1)
                        act.activation(heads_out[:, 1, e[2], :], core.ps(e)[:, :], ACT.Identity).then_inc(banks.done(e), 1)
                    elif kind == "msq":
                        banks.filled(act, e, i)
                        dst = {"q": side[:, 0, :], "kv": side[:, 1, :]}.get(e[1], side[:, e[-1] % 2, :] if e[1] == "df" else None)
                        if e[1] == "df" and e[2] >= 2:
                            act.wait_ge(head_done, i * HEADS_ALL + head_no[("values", "df", e[2] - 2)] + 1)
                        if e[1] != "df":
                            act.wait_ge(head_done, i * HEADS_ALL + head_no[("values", "df", DF_HEADS - 1)] + 1)
                        act.activation(dst, core.ps(e)[:, :], ACT.Sqrt, bias=core.c("eps6")).then_inc(banks.done(e), 1)
                        act.drain().then_inc(root_done, 1)
                    elif kind == "gate":
                        n = e[1] * KD + e[2]
                        banks.filled(act, e, i)
                        if e[1]:
                            act.wait_ge(branch_done, i * (3 * KD) + n - KD + 1)
                        elif e[2] == 0:
                            banks.filled_too(act, ("values", "ml", MLA_HEADS - 1), e, i)
                        act.activation(gates[:, e[2], :], core.ps(e)[:, :], ACT.Sigmoid, bias=vec("b_gate_2", n))\
                           .then_inc(banks.done(e), 1)
                        act.drain().then_inc(gate_done, 1)
                    elif kind == "norm":
                        norm.scalar(act, i, e[1], lambda k: vec("ln1_b_2" if e[1] == 0 else "ln2_b_2", k))
                    elif kind == "fg":
                        banks.filled(act, e, i)
                        if e[1] >= 2:
                            act.wait_ge(hidden_done, i * KF + e[1] - 1)
                        act.activation(side[:, e[1] % 2, :], core.ps(e)[:, :], ACT.Silu).then_inc(banks.done(e), 1)
                        act.drain().then_inc(silu_done, 1)
                act.drain().then_inc(layer_done, 1)

            with act.Fori(0, LAYERS) as i:
                layer(i)

        @block.vector
        def _(dve):
            dve.wait_ge(const_in, 16)

            def layer(i):
                dve.wait_ge(params_in, i * 32 + 32)
                dve.tensor_tensor(rot[:, 0:128].rearrange("p (a n) -> p a n", a=2), lamv[:, :, 0, :], lamv[:, :, 1, :], ALU.mult)
                dve.drain()
                dve.tensor_reduce(lam[:, 0:2], rot[:, 0:128].rearrange("p (a n) -> p a n", a=2), AX.X, ALU.add)
                dve.drain().then_inc(lam_sums, 1)
                dve.wait_ge(lam_exps, i + 1)
                dve.scalar_tensor_tensor(out=lam[:, 4:5], in0=lam[:, 3:4], scalar=lam[:, 2:3], in1=vec("lam_init"),
                                         op0=ALU.subtract, op1=ALU.subtract)
                dve.tensor_tensor(lam[:, 5:6], vec("diff_subln_g_2"), vec("one_less"), ALU.mult)
                dve.drain()

                recips, combines = [], []

                def maximum(u):
                    kind = u[0]
                    for s in of_unit(u):
                        key, col = ("scores", *soft[s]), negmax[:, s:s + 1]
                        banks.filled(dve, key, i)
                        if kind == "na":
                            _, h, n = u
                            lo, nb = near(n)
                            if (h, n) == (0, 0):
                                dve.wait_ge(table_in, i * (16 * ROWS) + 16 * ROWS)
                            free_slot(dve, s, i)
                            w = p[:, s % NP, 0:nb * P]
                            last = RUN - 1 - (lo - n + 1) * QB
                            bias = table[:, NA_HEADS - 1 - h, last:last + 1]
                            bias = bass.AP(tensor=bias.tensor, offset=bias.offset,
                                           ap=[list(bias.ap[0]), [-QB, nb], [-RPB_W, ROWS], [-1, QB]])
                            four = lambda ap: ap.rearrange("p (b r c) -> p b r c", b=nb, c=QB)
                            dve.tensor_tensor(four(w), four(core.ps(key)[:, 0:nb * P]), bias, ALU.add)\
                               .then_inc(banks.done(key), 1)
                            dve.drain()
                            mask = c2("near0" if n == 0 else "near2" if n == NBLK - 1 else "near1")
                            dve.tensor_tensor_reduce(w, w, mask, 1.0, NEG, ALU.add, ALU.max, col)
                            dve.drain()
                            dve.tensor_scalar(col, col, -1.0, None, ALU.mult)
                        else:
                            dve.tensor_reduce(col, core.ps(key)[:, :], AX.X, ALU.max)
                            dve.drain()
                            dve.tensor_scalar(col, col, -SCALE[kind], None, ALU.mult)
                        dve.drain().then_inc(max_done, 1)

                def invert(u):
                    for s in of_unit(u):
                        dve.wait_ge(exp_done, i * NS + s + 1)
                        dve.reciprocal(recip[:, s:s + 1], sums[:, s:s + 1])
                        dve.drain().then_inc(recip_done, 1)
                    if u[0] == "df":
                        dve.tensor_scalar(recip[:, s:s + 1], recip[:, s:s + 1], lam[:, 4:5], None, ALU.mult)
                        dve.drain()
                        combines.append(u)

                def combine(u):
                    a, b = of_unit(u)
                    dve.wait_ge(scaled, i * SCALED + scaled_no[(*u, 0)] + 1)
                    dve.scalar_tensor_tensor(out=p[:, a % NP, :], in0=p[:, b % NP, :], scalar=recip[:, b:b + 1],
                                             in1=p[:, a % NP, :], op0=ALU.mult, op1=ALU.add).then_inc(combined, 1)

                for e in plan:
                    kind = e[0]
                    if kind == "scores":
                        u = e[1:]
                        maximum(u)
                        before = list(combines)
                        if recips:
                            invert(recips.pop(0))
                        if before:
                            combine(combines.pop(0))
                        recips.append(u)
                    elif kind == "turn":
                        while e[1:] in recips:
                            invert(recips.pop(0))
                        while e[1:] in combines:
                            combine(combines.pop(0))
                    elif kind == "swap":
                        banks.filled(dve, e, i)
                        lo, hi, t = (0, P, "d") if e[1] in ("dfq", "dfk") else (64, 96, "m")
                        src = proj[e[1]][lo:hi, e[2] % (4 if t == "d" else 2), :]
                        dve.tensor_tensor(rot[lo:hi, :], core.ps(e)[lo:hi, :], c2(t + "sin")[lo:hi, :], ALU.mult)\
                           .then_inc(banks.done(e), 1)
                        dve.tensor_tensor(src, src, c2(t + "cos")[lo:hi, :], ALU.mult)
                        dve.drain()
                        for dst in ([proj["mk"][lo:hi, j, :] for j in (0, 1)] if e[1] == "kr" else [src]):
                            dve.tensor_tensor(dst, src, rot[lo:hi, :], ALU.add)
                        dve.drain().then_inc(rotated, 1)
                    elif kind == "values" and e[1] != "df":
                        banks.filled(dve, e, i)
                        h, b = e[2], 0 if e[1] == "na" else 2
                        dve.tensor_copy(heads_out[(h % 2) * 64:(h % 2) * 64 + 64, b, h // 2, :], core.ps(e)[0:64, :])\
                           .then_inc(banks.done(e), 1)
                        dve.drain().then_inc(head_done, 1)
                    elif kind == "msq":
                        n = {"q": DF_HEADS, "kv": DF_HEADS + 1}.get(e[1], e[-1])
                        dve.wait_ge(root_done, i * (DF_HEADS + 2) + n + 1)
                        root = side[:, n % 2, :]
                        dve.reciprocal(root, root)
                        dve.drain()
                        if e[1] == "df":
                            dst = heads_out[:, 1, e[2], :]
                            dve.scalar_tensor_tensor(out=dst, in0=dst, scalar=lam[:, 5:6], in1=root, op0=ALU.mult, op1=ALU.mult)
                            dve.drain().then_inc(head_done, 1)
                        else:
                            name, gain, k = ("cq", "mla_q_norm_g_2", 3) if e[1] == "q" else ("ckv", "mla_kv_norm_g_2", 2)
                            for j in range(k):
                                dst = proj[name][:, j, :]
                                dve.scalar_tensor_tensor(out=dst, in0=dst, scalar=vec(gain, j), in1=root, op0=ALU.mult, op1=ALU.mult)\
                                   .then_inc(latent_done, 1)
                    elif kind == "branch":
                        n = e[1] * KD + e[2]
                        dve.wait_ge(gate_done, i * (3 * KD) + n + 1)
                        banks.filled(dve, e, i)
                        dst = merged[:, e[2], :] if e[1] == 0 else rot[:, :]
                        dve.tensor_tensor(dst, core.ps(e)[:, :], gates[:, e[2], :], ALU.mult).then_inc(banks.done(e), 1)
                        dve.drain()
                        if e[1]:
                            dve.tensor_tensor(merged[:, e[2], :], merged[:, e[2], :], rot[:, :], ALU.add)
                            dve.drain()
                        dve.nop().then_inc(branch_done, 1)
                    elif kind in ("wo", "fo"):
                        banks.filled(dve, e, i)
                        dst = x[:, e[1], :]
                        dve.scalar_tensor_tensor(out=dst, in0=dst, scalar=ALPHA, in1=core.ps(e)[:, :], op0=ALU.mult, op1=ALU.add)\
                           .then_inc(banks.done(e), 1)
                        dve.drain().then_inc(norm.summand, 1)
                    elif kind == "norm":
                        norm.vector(dve, i, e[1], lambda k: vec("ln1_g_2" if e[1] == 0 else "ln2_g_2", k))
                    elif kind == "fu":
                        dve.wait_ge(silu_done, i * KF + e[1] + 1)
                        banks.filled(dve, e, i)
                        dve.tensor_tensor(hidden[:, e[1], :], side[:, e[1] % 2, :], core.ps(e)[:, :], ALU.mult)\
                           .then_inc(banks.done(e), 1)
                        dve.drain().then_inc(hidden_done, 1)

            with dve.Fori(0, LAYERS) as i:
                layer(i)

        @block.gpsimd
        def _(pool):
            with pool.Fori(0, LAYERS) as i:
                for s in range(NS):
                    kind, h, n, j = soft[s]
                    if j:
                        continue
                    pool.wait_ge(recip_done, i * NS + s + 1)
                    w = near(n)[1] * P if kind == "na" else T
                    pool.tensor_tensor(p[:, s % NP, 0:w], p[:, s % NP, 0:w], recip[:, s:s + 1].broadcast_to([P, w]), ALU.mult)\
                        .then_inc(scaled, 1)


class Shared:
    pass


def build_program(nc, ins, out):
    ctx = ExitStack()
    with ctx:
        core = Core(nc, ctx, ins)
        a = Shared()
        with ExitStack() as mix_ctx:
            a.xm = core.sb("xm", [P, KD, T + CTX], mix_ctx)
            a.y = core.sb("y", [P, TT, D], mix_ctx)
            a.c = core.sb("c_in", [P, KD, 2], mix_ctx)
            a.skip = core.sb("skip", [P, HEADS], mix_ctx)
            with ExitStack() as scan_ctx:
                a.xtok = core.sb("xtok", [P, TT + CT, D], scan_ctx)
                a.btok = core.sb("btok", [P, TT + CT, GROUPS * STATE], scan_ctx)
                a.bc = core.sb("bc", [P, 2 * GROUPS, T], scan_ctx)
                a.dt = core.sb("dt", [P, TT + CT, 2 * HEADS], scan_ctx)
                a.dta = core.sb("dta", [P, TT + CT, 2 * HEADS], scan_ctx)
                with ExitStack() as c1:
                    front(core, c1, a)
                with ExitStack() as c2:
                    scan(core, c2, a)
            with ExitStack() as c3:
                mixer(core, c3, a)
        with ExitStack() as moe_ctx:
            b = Shared()
            b.xf_tok = core.sb("xf_tok", [P, TT, D], moe_ctx)
            b.pick = core.sb("pick", [P, TT, EXPERTS * CAP], moe_ctx)
            b.put = core.sb("put", [P, EXPERTS // 2, T], moe_ctx)
            with ExitStack() as c4:
                router(core, c4, b)
            with ExitStack() as c5:
                experts(core, c5, b)
        with ExitStack() as c6:
            entry(core, c6)
        with ExitStack() as c7:
            layers(core, c7, out)



def _permuted_tokens():
    t = np.arange(T).reshape(ROWS, NBLK, QB)
    return t.transpose(1, 0, 2).reshape(-1)


def _rope(half):
    inv = np.exp((-np.log(np.float32(500000.0)) * np.arange(half, dtype=np.float32) / np.float32(half)).astype(np.float32))
    ang = _permuted_tokens().astype(np.float32)[None, :] * inv.astype(np.float32)[:, None]
    return np.cos(ang).astype(np.float32), np.sin(ang).astype(np.float32)


def _rope_tables(first, half, period):
    cos, sin, swap = np.ones((P, T), np.float32), np.zeros((P, T), np.float32), np.zeros((P, P), np.float32)
    c, s = _rope(half)
    for at in range(first, P, period):
        if at + 2 * half > P:
            break
        for j in range(half):
            lo, hi = at + j, at + half + j
            cos[lo] = cos[hi] = c[j]
            sin[lo] = sin[hi] = s[j]
            swap[hi, lo] = -1.0
            swap[lo, hi] = 1.0
    return cos, sin, swap


def _near_masks():
    out = np.full((3, ROWS, QB, 3, ROWS, QB), NEG, np.float32)
    for k, n in enumerate((0, 1, NBLK - 1)):
        for c in range(QB):
            w0 = min(max(QB * n + c - WIN // 2, 0), GRID - WIN)
            for j in range(3):
                for c2 in range(QB):
                    if w0 <= QB * (n - 1 + j) + c2 < w0 + WIN:
                        out[k, :, c, j, :, c2] = 0.0
    return out.reshape(3, P, 3 * P)


def _constants():
    lower = np.tril(np.ones((P, P), np.float32))
    dcos, dsin, dswap = _rope_tables(0, 8, 64)
    mcos, msin, mswap = _rope_tables(64, 16, 64)
    near = _near_masks()
    ones = np.ones((P, P), np.float32)
    parts = {
        "ident": np.eye(P), "ones": ones, "mean_d": ones / D,
        "tri_f": lower.T, "tri_b": lower, "mask_f": np.where(lower.T > 0, 0.0, NEG), "mask_b": np.where(lower > 0, 0.0, NEG),
        "eps6": ones[:, :1] * EPS, "eps5": ones[:, :1] * LN_EPS,
        "slot": np.tile(np.arange(1, CAP + 1)[None, :], (P, 1)),
    }
    second = {
        "dcos": dcos, "dsin": dsin, "mcos": mcos, "msin": msin, "dswap": dswap, "mswap": mswap,
        "mean_q": ones / QRANK, "mean_kv": ones / KVRANK, "mean_h": ones / P,
        "near0": near[0][:, P:], "near1": near[1], "near2": near[2][:, :2 * P],
    }
    return parts, second


def _pack(parts):
    at, where = 0, {}
    for name, a in parts.items():
        where[name] = (at, a.shape[1])
        at += a.shape[1]
    return where, at


_FIRST, _SECOND = _constants()
CON, NCON = _pack(_FIRST)
CON2, NCON2 = _pack(_SECOND)

_VECS = [("ada_b", 48), ("norm1_w", 8), ("norm2_w", 8), ("final_norm_w", 8), ("conv_w", 48), ("conv_b", 16),
         ("ssd_norm_w", 8), ("ln_in_g_2", 8), ("ln_in_b_2", 8)]
_LAYER = [("ln1_g_2", 8), ("ln1_b_2", 8), ("ln2_g_2", 8), ("ln2_b_2", 8), ("b_gate_2", 24), ("diff_subln_g_2", 1),
          ("mla_q_norm_g_2", 3), ("mla_kv_norm_g_2", 2), ("lam_init", 1), ("one_less", 1)]


def _places(columns):
    at, where = 0, {}
    for name, n in columns:
        where[name] = (at, n)
        at += n
    return where, at


VEC, NVEC = _places(_VECS)
LAYER, NLAYER = _places(_LAYER)


def lay_out(x):
    f = lambda n: np.ascontiguousarray(np.asarray(x[n]))
    cols = lambda v: np.ascontiguousarray(v.reshape(-1, P).T)
    g = {
        "xT": np.ascontiguousarray(f("x")[0].T), "ctxT": np.ascontiguousarray(f("ctx")[0].T),
        "cT": np.ascontiguousarray(np.stack([f("c")[0], f("c_ctx")], axis=1)),
        "ada_w": f("ada_w")[0], "w_in": f("w_in")[0], "w_pa": f("w_pa")[0], "w_pb": f("w_pb")[0], "w_o": f("w_o")[0],
        "wsT": np.ascontiguousarray(f("w_s")[0].transpose(0, 2, 1)),
        "rowsA": np.concatenate([f("dt_bias")[0].reshape(-1), f("a_log")[0].reshape(-1), f("d_skip")[0]]),
        "rowsB": np.concatenate([f("sgu_ln_w")[0], f("sgu_ln_b")[0], f("b_s")[0].reshape(-1)]),
    }
    for n in ("w_in_2", "w_out_2", "w_ffn_out_2"):
        g[n] = f(n)
    g["w_ffn_in_2"] = f("w_ffn_in_2").reshape(LAYERS, D, 2, KF // 2, 2 * P).transpose(0, 1, 3, 2, 4).reshape(LAYERS, D, 2 * FF)
    g["w_branch_2"] = f("w_branch_2").reshape(LAYERS, 3 * BR, D)
    tiled = lambda w: w.reshape(LAYERS, -1, P, w.shape[2]).transpose(0, 2, 1, 3).reshape(LAYERS, P, -1)
    g["w_mla_2"] = np.concatenate([tiled(f("w_mla_qb_2")), tiled(f("w_mla_kvb_2"))], axis=2)
    rpb = f("na_rpb_2").reshape(LAYERS, -1)
    edge = np.zeros((LAYERS, RPB_PAD), np.float32)
    g["rpb"] = np.concatenate([edge, rpb, edge], axis=1)[:, ::-1]
    g["lam"] = f("diff_lambda_2").reshape(LAYERS, 256)
    lam_init = [0.8 - 0.6 * float(np.exp(-0.3 * l)) for l in range(LAYERS)]
    extra = {"lam_init": lam_init, "one_less": [1.0 - v for v in lam_init]}
    g["layer_vec"] = np.stack([np.concatenate(
        [np.full((P, 1), extra[n][l], np.float32) if n in extra else cols(f(n)[l]) for n, _ in _LAYER], axis=1)
        for l in range(LAYERS)])
    for n in ("router_w", "w_gate", "w_up", "w_down"):
        g[n] = f(n)[0]
    g["vec"] = np.concatenate([cols(f(n)) for n, _ in _VECS], axis=1)
    g["con"] = np.concatenate([np.asarray(v, np.float32) for v in _FIRST.values()], axis=1)
    g["con2"] = np.concatenate([np.asarray(v, np.float32) for v in _SECOND.values()], axis=1)
    return {k: np.ascontiguousarray(v, dtype=v.dtype) for k, v in g.items()}


def kernel(**inputs):
    import concourse.bacc as bacc
    from concourse.bass_utils import run_bass_kernel_spmd

    nc = bacc.Bacc("TRN2", target_bir_lowering=False, num_devices=1)
    arrays = {"in_" + n: a for n, a in lay_out(inputs).items()}
    ins = {n[3:]: nc.dram_tensor(n, list(a.shape), mybir.dt.from_np(a.dtype), kind="ExternalInput").ap()
           for n, a in arrays.items()}
    out = nc.dram_tensor("out", [D, T], F32, kind="ExternalOutput").ap()
    build_program(nc, ins, out)
    result = run_bass_kernel_spmd(nc, [arrays], core_ids=[0])
    y = np.empty((1, T, D), np.float32)
    y[0, _permuted_tokens()] = result.results[0]["out"].T
    return y
```

```python
from contextlib import ExitStack

import numpy as np

import concourse.bass as bass
from concourse import mybir

F32 = mybir.dt.float32
ALU = mybir.AluOpType
ACT = mybir.ActivationFunctionType
AX = mybir.AxisListType

P = 128
D = 1024
KD = D // P
T = 512
TT = T // P
CTX = 256
CT = CTX // P
SLAB = 4352
SLOTS = 3
RAW, HIGH = 6, 3
PIECE, PIECES, HALVES = 2304, 3, 2
BANKS = 8
NEG = -1.0e30

HEADS, HDIM, GROUPS, STATE = 16, 64, 4, 128
HPG = HEADS // GROUPS
XBC = D + 2 * GROUPS * STATE
NSCAN = XBC + 2 * HEADS
EPS = 1e-6
EXPERTS, CAP = 16, 64

LAYERS = 2
GRID = 64
ROWS = T // GRID
QB = 16
NBLK = GRID // QB
WIN = 16
RPB_W = 2 * WIN - 1
RPB_H = 15
RUN = (ROWS - 1) * RPB_W + 3 * QB
RPB_PAD = 16
NA_HEADS, DF_HEADS, MLA_HEADS = 8, 4, 8
BR = 512
FF = 2816
KF = FF // P
QRANK, KVRANK, ROPE_D = 384, 256, 32
ALPHA = 4.0 ** 0.25
SCALE = {"df": 64 ** -0.5, "ml": 96 ** -0.5}
LN_EPS = 1e-5


class Ring:

    def __init__(self, full, free, step, given=0):
        self.given = given
        self.full, self.free, self.step, self.n = full, free, step, len(full)
        self.base, self.pos = [0] * self.n, 0
        self.reps = 0

    def narrowed(self, n):
        ring = Ring(self.full[:n], self.free[:n], self.step, self.given)
        ring.base = [b + self.reps * c for b, c in zip(self.base, self.count)][:n]
        return ring

    def begin(self, keys, reps=1):
        if self.reps:
            self.base = [b + self.reps * c for b, c in zip(self.base, self.count)]
            self.pos = (self.pos + len(self.use)) % self.n
        self.reps, self.count, self.use = reps, [0] * self.n, {}
        for k, key in enumerate(keys):
            slot = (self.pos + k) % self.n
            assert key not in self.use, key
            self.use[key] = (slot, self.base[slot] + self.count[slot])
            self.count[slot] += 1

    def slot(self, key):
        return self.use[key][0]

    def filled(self, eng, key, i=0):
        slot, before = self.use[key]
        eng.wait_ge(self.full[slot], i * (self.step * self.count[slot]) + self.step * (before + 1))

    def filled_too(self, eng, key, later, i=0):
        if self.use[key][0] != self.use[later][0]:
            self.filled(eng, key, i)

    def vacant(self, eng, key, i=0):
        slot, before = self.use[key]
        if before + self.given:
            eng.wait_ge(self.free[slot], i * self.count[slot] + before + self.given)

    def put(self, key):
        return self.full[self.use[key][0]]

    def done(self, key):
        return self.free[self.use[key][0]]


TWINS = {}


def r32(ap):
    return bass.AP(tensor=TWINS[ap.tensor.name], offset=ap.offset, ap=[list(d) for d in ap.ap])


def bcast_rows(v, n):
    return v.rearrange("(a n) -> a n", a=1).broadcast_to([P, n])


def w_tiles(w, r0, rows, c0, cols):
    return w[r0:r0 + rows, c0:c0 + cols].rearrange("(k p) n -> p k n", p=P)


class Core:

    def __init__(self, nc, ctx, ins):
        self.nc, self.ctx, self.ins = nc, ctx, ins
        self.stage = ""
        self.ring = self.sb("ring", [P, SLOTS, SLAB])
        self.slabs = Ring([self.sem(f"slab_full{i}") for i in range(SLOTS)],
                          [self.sem(f"slab_read{i}") for i in range(SLOTS)], 16)
        self.bank = [ctx.enter_context(nc.psum_tensor(f"bank{i}", [P, 512], F32)) for i in range(BANKS)]
        self.banks = Ring([self.sem(f"bank_full{i}") for i in range(BANKS)],
                          [self.sem(f"bank_read{i}") for i in range(BANKS)], 1)
        self.pieces = Ring([self.sem(f"piece_full{i}") for i in range(RAW)],
                           [self.sem(f"piece_read{i}") for i in range(RAW)], 16, given=1)
        self.halves = Ring([self.sem(f"split_done{i}") for i in range(HIGH)],
                           [self.sem(f"split_read{i}") for i in range(HIGH)], 1, given=1)
        self.norm_sems = [self.sem("norm_" + n) for n in
                          ("summand", "centred", "squared", "square_read", "root", "scaled", "shifted", "ready")]
        self.vec = self.sb("vec", [P, NVEC])
        self.con = self.sb("con", [P, NCON])
        self.x = self.sb("x", [P, KD, T])
        self.mod = self.sb("mod", [P, 48, 2])

    def sb(self, name, shape, ctx=None):
        with self.nc.sbuf_tensor(self.stage + name, shape, F32) as buf:
            pass
        TWINS[buf.name] = (ctx or self.ctx).enter_context(
            self.nc.sbuf_tensor(self.stage + name + "_r", shape, mybir.dt.float32r))
        return buf

    def sem(self, name, ctx=None):
        return (ctx or self.ctx).enter_context(self.nc.semaphore(self.stage + name))

    def v(self, name, i=0, n=1):
        a = VEC[name][0] + i
        return self.vec[:, a:a + n]

    def c(self, name, rows=P):
        a, n = CON[name][:2]
        return self.con[0:rows, a:a + n]

    def ps(self, key):
        return self.bank[self.banks.slot(key)]

    def slab(self, key, k, n):
        return self.ring[:, self.slabs.slot(key), 0:k * n].rearrange("p (k n) -> p k n", k=k)


def load_slab(core, sp, key, src, i=0, at=0):
    _, k, n = src.shape
    core.slabs.vacant(sp, key, i)
    dst = core.ring[:, core.slabs.slot(key), at:at + k * n].rearrange("p (k n) -> p k n", k=k)
    sp.dma_start(dst, src).then_inc(core.slabs.put(key), 16)


def product(pe, out, lhs, rhs, read=None):
    n = len(lhs)
    for k in range(n):
        last = pe.matmul(out, lhs[k], rhs[k], start=k == 0, stop=k == n - 1)
        if k == 0 and read is not None:
            last.then_inc(read, 1)
    return last


def front(core, ctx, a):
    core.stage = "front_"
    nc, I = core.nc, core.ins
    TA = T + CTX
    NM = XBC // P
    sem = lambda n: core.sem(n, ctx)
    pad = core.sb("pad", [P, 2, TA + 3], ctx)
    conv = core.sb("conv", [P, 2, TA + 1], ctx)
    act_x = core.sb("act_x", [P, 2, TA], ctx)
    sq = core.sb("sq", [P, 2, TA], ctx)
    rstd = core.sb("rstd", [P, TA], ctx)
    scale1 = core.sb("scale1", [P, KD, 2], ctx)
    dtw = core.sb("dtw", [P, 6, CT + TT, 2 * HEADS], ctx)
    raw, mag, ex, one_ex, ln_ex, rest = (dtw[:, k] for k in range(6))
    rows = core.sb("rowsA", [P, 5 * HEADS], ctx)
    dt_bias, a_neg = rows[:, 0:2 * HEADS], rows[:, 2 * HEADS:4 * HEADS]
    const_in, x_in, pad_zero = sem("const_in"), sem("x_in"), sem("pad_zero")
    c_silu = sem("c_silu")
    sq_done, sq_used, root_done = sem("sq_done"), sem("sq_used"), sem("root_done")
    scaled, xm_done = sem("scaled"), sem("xm_done")
    dt_dve, dt_act = sem("dt_dve"), sem("dt_act")
    pad_done, conv_done, act_done = sem("pad_done"), sem("conv_done"), sem("act_done")

    ada = [("ada", s) for s in range(4)]
    xbc = [("xbc", s) for s in range(4)]
    core.slabs.begin(ada + ["dtw"] + xbc)
    keys = ["rms_l", "rms_c"] + ada + ["dt"]
    for m in range(NM):
        keys += [("xl", m)] + ([("xc", m)] if m < 12 else [])
        if m >= 1 and m - 1 < 12:
            keys += [("tl", m - 1), ("tc", m - 1)]
    core.banks.begin(keys)

    with nc.Block() as block:
        @block.sync
        def _(sp):
            sp.dma_start(core.con[:, :], I["con"]).then_inc(const_in, 16)
            sp.dma_start(core.vec[:, :], I["vec"]).then_inc(const_in, 16)
            sp.dma_start(a.c[:, :, :], I["cT"].rearrange("(k p) n -> p k n", p=P)).then_inc(const_in, 16)
            sp.dma_start(a.xm[:, :, 0:T], I["xT"].rearrange("(k p) n -> p k n", p=P)).then_inc(x_in, 16)
            sp.dma_start(a.xm[:, :, T:TA], I["ctxT"].rearrange("(k p) n -> p k n", p=P)).then_inc(x_in, 16)
            sp.dma_start(rows[:, :], bcast_rows(I["rowsA"], 5 * HEADS)).then_inc(const_in, 16)
            for s in range(4):
                load_slab(core, sp, ("ada", s), w_tiles(I["ada_w"], 0, D, 512 * s, 512))
            load_slab(core, sp, "dtw", w_tiles(I["w_in"], 0, D, XBC, 2 * HEADS))
            for s in range(4):
                load_slab(core, sp, ("xbc", s), w_tiles(I["w_in"], 0, D, 512 * s, 512))

        @block.tensor
        def _(pe):
            pe.wait_ge(const_in, 64)
            core.banks.vacant(pe, "rms_l")
            core.banks.vacant(pe, "rms_c")
            for k in range(KD):
                pe.wait_ge(sq_done, k + 1)
                last = pe.matmul(core.ps("rms_l")[:, :], core.c("mean_d"), sq[:, k % 2, 0:T],
                                 start=k == 0, stop=k == KD - 1)
                if k == KD - 1:
                    last.then_inc(core.banks.put("rms_l"), 1)
                last = pe.matmul(core.ps("rms_c")[:, 0:CTX], core.c("mean_d"), sq[:, k % 2, T:TA],
                                 start=k == 0, stop=k == KD - 1)
                if k < KD - 1:
                    last.then_inc(sq_used, 1)
            last.then_inc(core.banks.put("rms_c"), 1)
            pe.wait_ge(c_silu, 1)
            for s in range(4):
                core.slabs.filled(pe, ("ada", s))
                core.banks.vacant(pe, ("ada", s))
                w = core.slab(("ada", s), KD, 512)
                for m in range(4):
                    last = product(pe, core.ps(("ada", s))[:, 2 * m:2 * m + 2],
                                   [w[:, k, m * P:(m + 1) * P] for k in range(KD)],
                                   [a.c[:, k, :] for k in range(KD)],
                                   core.slabs.done(("ada", s - 1)) if s and m == 0 else None)
                last.then_inc(core.banks.put(("ada", s)), 1)
            pe.wait_ge(xm_done, 2 * KD)
            core.slabs.filled(pe, "dtw")
            core.banks.vacant(pe, "dt")
            w = core.slab("dtw", KD, 2 * HEADS)
            for t in range(TT + CT):
                last = product(pe, core.ps("dt")[:, t * 32:t * 32 + 32],
                               [a.xm[:, k, t * P:(t + 1) * P] for k in range(KD)],
                               [w[:, k, :] for k in range(KD)],
                               core.slabs.done(("ada", 3)) if t == 0 else None)
            last.then_inc(core.banks.put("dt"), 1)

            def turn(m):
                pe.wait_ge(act_done, m + 1)
                src = act_x[:, m % 2]
                for name, t0, n in (("tl", 0, TT), ("tc", TT, CT)):
                    core.banks.vacant(pe, (name, m))
                    for t in range(n):
                        last = pe.transpose(core.ps((name, m))[:, t * P:(t + 1) * P],
                                            src[:, (t0 + t) * P:(t0 + t + 1) * P], core.c("ident"))
                    last.then_inc(core.banks.put((name, m)), 1)

            for m in range(NM):
                read = None
                if m % 4 == 0:
                    core.slabs.filled(pe, ("xbc", m // 4))
                    read = core.slabs.done(("xbc", m // 4 - 1) if m else "dtw")
                w = core.slab(("xbc", m // 4), KD, 512)
                cut = [w[:, k, (m % 4) * P:(m % 4 + 1) * P] for k in range(KD)]
                core.banks.vacant(pe, ("xl", m))
                last = product(pe, core.ps(("xl", m))[:, :], cut, [a.xm[:, k, 0:T] for k in range(KD)], read)
                last.then_inc(core.banks.put(("xl", m)), 1)
                if m < 12:
                    core.banks.vacant(pe, ("xc", m))
                    last = product(pe, core.ps(("xc", m))[:, 0:CTX], cut, [a.xm[:, k, T:TA] for k in range(KD)])
                    last.then_inc(core.banks.put(("xc", m)), 1)
                if m >= 1 and m - 1 < 12:
                    turn(m - 1)
            pe.drain().then_inc(core.slabs.done(("xbc", 3)), 1)

        @block.scalar
        def _(act):
            act.wait_ge(x_in, 32)
            for k in range(KD):
                if k >= 2:
                    act.wait_ge(sq_used, k - 1)
                act.activation(sq[:, k % 2, :], a.xm[:, k, :], ACT.Square).then_inc(sq_done, 1)
            act.wait_ge(const_in, 64)
            core.banks.filled(act, "rms_l")
            core.banks.filled(act, "rms_c")
            act.activation(rstd[:, 0:T], core.ps("rms_l")[:, :], ACT.Sqrt,
                           bias=core.c("eps6")).then_inc(core.banks.done("rms_l"), 1)
            act.activation(rstd[:, T:TA], core.ps("rms_c")[:, 0:CTX], ACT.Sqrt,
                           bias=core.c("eps6")).then_inc(core.banks.done("rms_c"), 1)
            act.drain().then_inc(root_done, 1)
            act.activation(a.c[:, :, :], a.c[:, :, :], ACT.Silu).then_inc(c_silu, 1)
            for k in range(KD):
                for j, (lo, hi) in enumerate(((0, T), (T, TA))):
                    act.wait_ge(scaled, 2 * k + j + 1)
                    act.activation(a.xm[:, k, lo:hi], a.xm[:, k, lo:hi], ACT.Identity,
                                   bias=core.mod[:, k, j:j + 1]).then_inc(xm_done, 1)
            act.wait_ge(dt_dve, 1)
            act.activation(mag, raw, ACT.Abs).then_inc(dt_act, 1)
            act.wait_ge(dt_act, 1)
            act.activation(ex, mag, ACT.Exp, scale=-1.0)
            act.activation(a_neg, a_neg, ACT.Exp).then_inc(dt_act, 1)
            act.wait_ge(dt_dve, 2)
            act.activation(ln_ex, one_ex, ACT.Ln).then_inc(dt_act, 1)

            def silu(m):
                act.wait_ge(conv_done, m + 1)
                if m >= 12:
                    act.activation(a.bc[:, m - 8, :], conv[:, m % 2, 0:T], ACT.Silu, bias=core.v("conv_b", m))\
                       .then_inc(act_done, 1)
                    return
                if m >= 2:
                    core.banks.filled(act, ("tc", m - 2))
                act.activation(act_x[:, m % 2, 0:T], conv[:, m % 2, 0:T], ACT.Silu, bias=core.v("conv_b", m))
                act.activation(act_x[:, m % 2, T:TA], conv[:, m % 2, T + 1:TA + 1], ACT.Silu,
                               bias=core.v("conv_b", m))
                act.drain().then_inc(act_done, 1)
                if m >= 8:
                    act.activation(a.bc[:, m - 8, :], act_x[:, m % 2, 0:T], ACT.Identity)

            act.wait_ge(pad_zero, 1)
            for m in range(NM):
                core.banks.filled(act, ("xl", m))
                if m >= 2:
                    act.wait_ge(conv_done, m - 1)
                act.activation(pad[:, m % 2, 1:T + 1], core.ps(("xl", m))[:, :], ACT.Identity)\
                   .then_inc(core.banks.done(("xl", m)), 1)
                if m < 12:
                    core.banks.filled(act, ("xc", m))
                    act.activation(pad[:, m % 2, T + 2:TA + 2], core.ps(("xc", m))[:, 0:CTX], ACT.Identity)\
                       .then_inc(core.banks.done(("xc", m)), 1)
                act.drain().then_inc(pad_done, 1)
                if m >= 1:
                    silu(m - 1)
            silu(NM - 1)

        @block.vector
        def _(dve):
            dve.wait_ge(const_in, 64)
            for s in range(4):
                core.banks.filled(dve, ("ada", s))
                bias = core.v("ada_b", 4 * s, 4).unsqueeze(2).broadcast_to([P, 4, 2])
                dve.tensor_tensor(core.mod[:, 4 * s:4 * s + 4, :],
                                  core.ps(("ada", s))[:, 0:8].rearrange("p (m j) -> p m j", j=2), bias,
                                  ALU.add).then_inc(core.banks.done(("ada", s)), 1)
            dve.drain()
            dve.tensor_scalar(scale1[:, :, :], core.mod[:, KD:2 * KD, :], 1.0, None, ALU.add)
            dve.drain()
            dve.tensor_tensor(scale1[:, :, :], scale1[:, :, :],
                              core.v("norm1_w", 0, KD).unsqueeze(2).broadcast_to([P, KD, 2]), ALU.mult)
            dve.wait_ge(root_done, 1)
            dve.reciprocal(rstd[:, :], rstd[:, :])
            dve.drain()
            for k in range(KD):
                for j, (lo, hi) in enumerate(((0, T), (T, TA))):
                    dve.scalar_tensor_tensor(out=a.xm[:, k, lo:hi], in0=a.xm[:, k, lo:hi],
                                             scalar=scale1[:, k, j:j + 1], in1=rstd[:, lo:hi],
                                             op0=ALU.mult, op1=ALU.mult).then_inc(scaled, 1)
            core.banks.filled(dve, "dt")
            bias = dt_bias.unsqueeze(1).broadcast_to([P, CT + TT, 2 * HEADS])
            dve.tensor_tensor(raw, core.ps("dt")[:, 0:192].rearrange("p (t h) -> p t h", h=2 * HEADS), bias,
                              ALU.add).then_inc(core.banks.done("dt"), 1)
            dve.drain().then_inc(dt_dve, 1)
            dve.wait_ge(dt_act, 2)
            dve.tensor_scalar(one_ex, ex, 1.0, None, ALU.add)
            dve.drain().then_inc(dt_dve, 1)
            dve.tensor_scalar(rest, one_ex, -1.0, None, ALU.add)
            dve.drain()
            dve.tensor_tensor(rest, ex, rest, ALU.subtract)
            dve.reciprocal(mag, one_ex)
            dve.drain()
            dve.tensor_tensor(rest, rest, mag, ALU.mult)
            dve.wait_ge(dt_act, 3)
            dve.drain()
            dve.tensor_tensor(rest, rest, ln_ex, ALU.add)
            dve.drain()
            dve.scalar_tensor_tensor(out=a.dt[:, :, :], in0=raw, scalar=0.0, in1=rest, op0=ALU.max, op1=ALU.add)
            dve.drain()
            dve.scalar_tensor_tensor(out=a.dta[:, :, :], in0=a.dt[:, :, :], scalar=-1.0,
                                     in1=a_neg.unsqueeze(1).broadcast_to([P, CT + TT, 2 * HEADS]),
                                     op0=ALU.mult, op1=ALU.mult)

            def tokens(m):
                dst, col = (a.xtok, m) if m < 8 else (a.btok, m - 8)
                for name, t0, n in (("tl", 0, TT), ("tc", TT, CT)):
                    core.banks.filled(dve, (name, m))
                    last = dve.tensor_copy(dst[:, t0:t0 + n, col * P:(col + 1) * P],
                                           core.ps((name, m))[:, 0:n * P].rearrange("p (t f) -> p t f", f=P))
                    last.then_inc(core.banks.done((name, m)), 1)

            for m in range(NM):
                dve.wait_ge(pad_done, m + 1)
                if m >= 2:
                    dve.wait_ge(act_done, m - 1)
                n = TA + 1 if m < 12 else T
                src, dst = pad[:, m % 2], conv[:, m % 2, 0:n]
                dve.tensor_scalar(dst, src[:, 0:n], core.v("conv_w", m), None, ALU.mult)
                dve.drain()
                for tap in (1, 2):
                    dve.scalar_tensor_tensor(out=dst, in0=src[:, tap:n + tap], scalar=core.v("conv_w", NM * tap + m),
                                             in1=dst, op0=ALU.mult, op1=ALU.add)
                    if tap == 1:
                        dve.drain()
                dve.drain().then_inc(conv_done, 1)
                if m >= 2 and m - 2 < 12:
                    tokens(m - 2)

        @block.gpsimd
        def _(pool):
            pool.memset(pad[:, :, :], 0.0).then_inc(pad_zero, 1)
            pool.wait_ge(const_in, 64)
            pool.tensor_copy(a.skip[:, :], rows[:, 4 * HEADS:5 * HEADS])


def scan(core, ctx, a):
    core.stage = "scan_"
    nc = core.nc
    sem = lambda n: core.sem(n, ctx)
    NT, H2 = TT + CT, 2 * HEADS
    acum = core.sb("acum", [P, NT, H2], ctx)
    grow = core.sb("grow", [P, NT, H2], ctx)
    total = core.sb("total", [P, NT, H2], ctx)
    toend = core.sb("toend", [P, NT, H2], ctx)
    spare = core.x[:, :, :].rearrange("p m t -> p (m t)")
    cb = spare[:, 0:TT * GROUPS * P].rearrange("p (t n) -> p t n", t=TT)
    xdt, xend = spare[:, 2 * D:3 * D], spare[:, 3 * D:4 * D]
    h = core.sb("h", [P, 2, D], ctx)
    NSEG = 6
    seg = core.sb("seg", [P, NSEG, HPG * P], ctx)
    part = core.sb("part", [P, D], ctx)
    acum_done, exp_done, cb_done, toend_done = sem("acum_done"), sem("exp_done"), sem("cb_done"), sem("toend_done")
    seg_done, decay_done, mt_done, mt_used = sem("seg_done"), sem("decay_done"), sem("mt_done"), sem("mt_used")
    xdt_done, xdt_used, xend_done, xend_used = sem("xdt_done"), sem("xdt_used"), sem("xend_done"), sem("xend_used")
    h_done, part_done, part_used = sem("h_done"), sem("part_done"), sem("part_used")

    ctx_steps = [(d, TT + (k if d == 0 else CT - 1 - k), False) for k in range(CT) for d in (0, 1)]
    lat_steps = [(d, k if d == 0 else TT - 1 - k, True) for k in range(TT) for d in (0, 1)]
    steps = ctx_steps + lat_steps
    outs = [u for u, s in enumerate(steps) if s[2]]
    feeds = [u for u, s in enumerate(steps) if u < len(steps) - 2]
    G = range(GROUPS)
    keys = ["sums"] + [("cb", t) for t in range(TT)]
    first = outs[0]

    def seg_keys(u):
        return [("seg", u, g) for g in G]

    keys += [k for u in range(first) for k in (("st", u, 0), ("st", u, 1))] + seg_keys(first)
    for u in outs:
        if u + 1 in outs:
            keys += seg_keys(u + 1)
        keys += [("off", u, 0), ("off", u, 1)]
        if u in feeds:
            keys += [("st", u, 0), ("st", u, 1)]
        keys += [("diag", u, 0), ("diag", u, 1)]
    core.slabs.begin([])
    core.banks.begin(keys)
    order = {u: n for n, u in enumerate(outs)}
    feed_no = {u: n for n, u in enumerate(feeds)}
    per_head = lambda ap: ap.unsqueeze(2).broadcast_to([P, HEADS, HDIM])
    by_head = lambda ap: ap.rearrange("p (h f) -> p h f", f=HDIM)

    with nc.Block() as block:
        @block.tensor
        def _(pe):
            core.banks.vacant(pe, "sums")
            sums = core.ps("sums")
            for d, tri in enumerate(("tri_f", "tri_b")):
                pe.matmul(sums[:, d * 96:d * 96 + 96], core.c(tri), a.dta[:, :, d * HEADS:(d + 1) * HEADS],
                          start=True, stop=True)
            pe.matmul(sums[:, 192:384], core.c("ones"), a.dta[:, :, :], start=True, stop=True)\
              .then_inc(core.banks.put("sums"), 1)
            for t in range(TT):
                core.banks.vacant(pe, ("cb", t))
                for g in G:
                    last = pe.matmul(core.ps(("cb", t))[:, g * P:(g + 1) * P], a.bc[:, g, t * P:(t + 1) * P],
                                     a.bc[:, GROUPS + g, t * P:(t + 1) * P], start=True, stop=True)
                last.then_inc(core.banks.put(("cb", t)), 1)

            def state(u):
                t = steps[u][1]
                pe.wait_ge(xend_done, feed_no[u] + 1)
                for half in (0, 1):
                    core.banks.vacant(pe, ("st", u, half))
                    for g in (2 * half, 2 * half + 1):
                        last = pe.matmul(core.ps(("st", u, half))[:, (g % 2) * 256:(g % 2) * 256 + 256],
                                         a.btok[:, t, g * P:(g + 1) * P], xend[:, g * 256:(g + 1) * 256],
                                         start=True, stop=True)
                    last.then_inc(core.banks.put(("st", u, half)), 1)

            def sums_of(u):
                d, t, _ = steps[u]
                for g in G:
                    core.banks.vacant(pe, ("seg", u, g))
                    for r in range(HPG):
                        col = d * HEADS + g * HPG + r
                        last = pe.matmul(core.ps(("seg", u, g))[:, r * P:(r + 1) * P],
                                         a.dta[:, t, col:col + 1].broadcast_to([P, P]),
                                         core.c("tri_b" if d else "tri_f"), start=True, stop=True)
                    last.then_inc(core.banks.put(("seg", u, g)), 1)

            for u in range(first):
                state(u)
            sums_of(first)
            for u in outs:
                d, t, _ = steps[u]
                if u + 1 in outs:
                    sums_of(u + 1)
                pe.wait_ge(h_done, u - 1)
                for half in (0, 1):
                    core.banks.vacant(pe, ("off", u, half))
                    for g in (2 * half, 2 * half + 1):
                        last = pe.matmul(core.ps(("off", u, half))[:, (g % 2) * 256:(g % 2) * 256 + 256],
                                         a.bc[:, GROUPS + g, t * P:(t + 1) * P], h[:, d, g * 256:(g + 1) * 256],
                                         start=True, stop=True)
                    last.then_inc(core.banks.put(("off", u, half)), 1)
                if u in feeds:
                    state(u)
                pe.wait_ge(xdt_done, order[u] + 1)
                for half in (0, 1):
                    core.banks.vacant(pe, ("diag", u, half))
                    for g in (2 * half, 2 * half + 1):
                        n = order[u] * GROUPS + g
                        pe.wait_ge(mt_done, n + 1)
                        for r in range(HPG):
                            hd = g * HPG + r
                            last = pe.matmul(core.ps(("diag", u, half))[:, (hd % 8) * HDIM:(hd % 8 + 1) * HDIM],
                                             seg[:, n % NSEG, r * P:(r + 1) * P], xdt[:, hd * HDIM:(hd + 1) * HDIM],
                                             start=True, stop=True)
                            if r == HPG - 1 and g % 2 == 0:
                                last.then_inc(mt_used, 1)
                    last.then_inc(core.banks.put(("diag", u, half)), 1)

        @block.scalar
        def _(act):
            act.wait_ge(acum_done, 1)
            act.activation(grow[:, :, :], acum[:, :, :], ACT.Exp)
            act.activation(total[:, :, :], total[:, :, :], ACT.Exp)
            act.activation(toend[:, :, :], toend[:, :, :], ACT.Exp)
            act.drain().then_inc(exp_done, 1)
            for t in range(TT):
                core.banks.filled(act, ("cb", t))
                act.activation(cb[:, t, :], core.ps(("cb", t))[:, :], ACT.Identity)\
                   .then_inc(core.banks.done(("cb", t)), 1)
            act.drain().then_inc(cb_done, 1)
            for n in range(len(outs) * GROUPS):
                act.wait_ge(seg_done, n + 1)
                act.activation(seg[:, n % NSEG, :], seg[:, n % NSEG, :], ACT.Exp).then_inc(decay_done, 1)

        @block.vector
        def _(dve):
            core.banks.filled(dve, "sums")
            sums = core.ps("sums")
            for d in (0, 1):
                dve.tensor_copy(acum[:, :, d * HEADS:(d + 1) * HEADS],
                                sums[:, d * 96:d * 96 + 96].rearrange("p (t h) -> p t h", h=HEADS))
            dve.tensor_copy(total[:, :, :], sums[:, 192:384].rearrange("p (t h) -> p t h", h=H2))\
               .then_inc(core.banks.done("sums"), 1)
            dve.drain()
            dve.tensor_tensor(toend[:, :, :], total[:, :, :], acum[:, :, :], ALU.subtract)
            dve.drain().then_inc(acum_done, 1)
            dve.wait_ge(exp_done, 1)
            dve.tensor_tensor(toend[:, :, :], toend[:, :, :], a.dt[:, :, :], ALU.mult)
            dve.drain().then_inc(toend_done, 1)

            def carry(u):
                d, t, _ = steps[u]
                if u >= 2:
                    if u in outs:
                        core.banks.filled(dve, ("off", u, 1))
                    dve.tensor_tensor(by_head(h[:, d, :]), by_head(h[:, d, :]),
                                      per_head(total[:, t, d * HEADS:(d + 1) * HEADS]), ALU.mult)
                    dve.drain()
                for half in (0, 1):
                    core.banks.filled(dve, ("st", u, half))
                    dst, src = h[:, d, half * 512:half * 512 + 512], core.ps(("st", u, half))[:, :]
                    last = dve.tensor_tensor(dst, dst, src, ALU.add) if u >= 2 else dve.tensor_copy(dst, src)
                    last.then_inc(core.banks.done(("st", u, half)), 1)
                dve.drain().then_inc(h_done, 1)

            def segments(u):
                d, t, _ = steps[u]
                for g in G:
                    n = order[u] * GROUPS + g
                    core.banks.filled(dve, ("seg", u, g))
                    if n >= NSEG:
                        old = n - NSEG
                        if old % 2 == 0:
                            dve.wait_ge(mt_used, old // 2 + 1)
                        else:
                            core.banks.filled(dve, ("diag", outs[old // GROUPS], (old % GROUPS) // 2))
                    for r in range(HPG):
                        col = d * HEADS + g * HPG + r
                        last = dve.scalar_tensor_tensor(
                            out=seg[:, n % NSEG, r * P:(r + 1) * P], in0=core.ps(("seg", u, g))[:, r * P:(r + 1) * P],
                            scalar=acum[:, t, col:col + 1], in1=core.c("mask_b" if d else "mask_f"),
                            op0=ALU.subtract, op1=ALU.add)
                    last.then_inc(core.banks.done(("seg", u, g)), 1)
                    dve.drain().then_inc(seg_done, 1)

            def scaled_x(u):
                d, t, _ = steps[u]
                if order[u]:
                    core.banks.filled(dve, ("diag", u - 1, 1))
                dve.tensor_tensor(by_head(xdt[:, :]), by_head(a.xtok[:, t, :]),
                                  per_head(a.dt[:, t, d * HEADS:(d + 1) * HEADS]), ALU.mult).then_inc(xdt_done, 1)

            for u in range(first):
                carry(u)
            segments(first)
            for u in outs:
                d, t, _ = steps[u]
                scaled_x(u)
                if u in feeds:
                    carry(u)
                if u + 1 in outs:
                    segments(u + 1)
                if order[u]:
                    dve.wait_ge(part_used, order[u])
                for half in (0, 1):
                    lo = half * 512
                    core.banks.filled(dve, ("off", u, half))
                    dve.tensor_tensor(by_head(part[:, :])[:, 8 * half:8 * half + 8],
                                      by_head(core.ps(("off", u, half))[:, :]),
                                      per_head(grow[:, t, d * HEADS:(d + 1) * HEADS])[:, 8 * half:8 * half + 8],
                                      ALU.mult).then_inc(core.banks.done(("off", u, half)), 1)
                    core.banks.filled(dve, ("diag", u, half))
                    dve.drain()
                    dve.tensor_tensor(part[:, lo:lo + 512], part[:, lo:lo + 512], core.ps(("diag", u, half))[:, :],
                                      ALU.add).then_inc(core.banks.done(("diag", u, half)), 1)
                dve.drain().then_inc(part_done, 1)

        @block.gpsimd
        def _(pool):
            def to_end(u):
                d, t, _ = steps[u]
                n = feed_no[u]
                if n:
                    core.banks.filled(pool, ("st", feeds[n - 1], 1))
                pool.tensor_tensor(by_head(xend[:, :]), by_head(a.xtok[:, t, :]),
                                   per_head(toend[:, t, d * HEADS:(d + 1) * HEADS]), ALU.mult).then_inc(xend_done, 1)

            def decays(u):
                t = steps[u][1]
                for g in G:
                    n = order[u] * GROUPS + g
                    pool.wait_ge(decay_done, n + 1)
                    cbg = cb[:, t, g * P:(g + 1) * P].unsqueeze(1).broadcast_to([P, HPG, P])
                    m = seg[:, n % NSEG, :].rearrange("p (r i) -> p r i", i=P)
                    pool.tensor_tensor(m, m, cbg, ALU.mult).then_inc(mt_done, 1)

            def add_part(u):
                t = steps[u][1]
                pool.wait_ge(part_done, order[u] + 1)
                pool.tensor_tensor(a.y[:, t, :], a.y[:, t, :], part[:, :], ALU.add).then_inc(part_used, 1)

            pool.wait_ge(toend_done, 1)
            for u in range(first):
                to_end(u)
            for t in range(TT):
                pool.tensor_tensor(by_head(a.y[:, t, :]), by_head(a.xtok[:, t, :]), per_head(a.skip[:, :]), ALU.mult)
            pool.drain()
            pool.wait_ge(cb_done, 1)
            for u in outs:
                t = steps[u][1]
                if u in feeds:
                    to_end(u)
                decays(u)
                if order[u]:
                    add_part(u - 1)
            add_part(outs[-1])


def mixer(core, ctx, a):
    core.stage = "mixer_"
    nc, I = core.nc, core.ins
    sem = lambda n: core.sem(n, ctx)
    Z0, V0, U0 = NSCAN, NSCAN + 2 * D, NSCAN + D
    GA, GB = NSCAN + 3 * D, NSCAN + 4 * D
    v = core.sb("v", [P, TT, D], ctx)
    u = core.sb("u", [P, KD, T], ctx)
    yt = core.sb("yt", [P, KD, T], ctx)
    ws = core.sb("ws", [P, KD, P], ctx)
    gate = core.sb("gate", [P, 4, T], ctx)
    rows = core.sb("rowsB", [P, 2 * D + KD * P], ctx)
    ln_w, ln_b, b_s = rows[:, 0:D], rows[:, D:2 * D], rows[:, 2 * D:]
    zs = core.sb("zs", [P, 2, 512], ctx)
    tmp = core.sb("tmp", [P, 2, T], ctx)
    ssq = core.sb("ssq", [P, TT, GROUPS], ctx)
    bn = core.sb("bn", [P, TT, 2, 6], ctx)
    mv = core.sb("mv", [P, TT, 2], ctx)
    merged = v[:, :, :].rearrange("p t n -> p (t n)").rearrange("p (m t) -> p m t", t=T)
    zs_done, zs_used, ssq_done, y_done = sem("zs_done"), sem("zs_used"), sem("ssq_done"), sem("y_done")
    v_done, v_ready, u_done, root2_done, mv_done = sem("v_done"), sem("v_ready"), sem("u_done"), sem("root2_done"), sem("mv_done")
    sgu_done, yt_done, gate_done, merged_done = sem("sgu_done"), sem("yt_done"), sem("gate_done"), sem("merged_done")
    rows_in, res_in, gated, mod2_done = sem("rows_in"), sem("res_in"), sem("gated"), sem("mod2_done")
    v_norm, merged_a = sem("v_norm"), sem("merged_a")

    merge_slabs = [(n, hh) for hh in (0, 1) for n in ("ga", "pa", "gb", "pb")]
    slab_list = [("z", 0), ("z", 1), ("v", 0), ("v", 1), ("u", 0), ("u", 1)] + [("ada", s) for s in range(4, 12)] \
        + merge_slabs + [("wo", 0), ("wo", 1)]
    core.slabs.begin(slab_list)
    tok = [(t, hh) for hh in (0, 1) for t in range(TT)]
    merge_tiles = [(n, m) for n, hh in merge_slabs for m in range(4 * hh, 4 * hh + 4)]
    core.banks.begin([("z", *k) for k in tok] + [("v", *k) for k in tok] + [("u", m) for m in range(KD)]
                     + [("ada", s) for s in range(4, 12)]
                     + [("yt", m) for m in range(KD)] + [("mx", g) for g in range(KD)]
                     + merge_tiles + [("wo", m) for m in range(KD)])
    tile_no = {k: n for n, k in enumerate(merge_tiles)}
    source = {("z", s): w_tiles(I["w_in"], 0, D, Z0 + 512 * s, 512) for s in (0, 1)}
    source |= {("v", s): w_tiles(I["w_in"], 0, D, V0 + 512 * s, 512) for s in (0, 1)}
    source |= {("u", s): w_tiles(I["w_in"], 0, D, U0 + 512 * s, 512) for s in (0, 1)}
    source |= {("ada", s): w_tiles(I["ada_w"], 0, D, 512 * s, 512) for s in range(4, 12)}
    source |= {("ga", s): w_tiles(I["w_in"], 0, D, GA + 512 * s, 512) for s in (0, 1)}
    source |= {("gb", s): w_tiles(I["w_in"], 0, D, GB + 512 * s, 512) for s in (0, 1)}
    source |= {("pa", s): w_tiles(I["w_pa"], 0, D, 512 * s, 512) for s in (0, 1)}
    source |= {("pb", s): w_tiles(I["w_pb"], 0, D, 512 * s, 512) for s in (0, 1)}
    source |= {("wo", s): w_tiles(I["w_o"], 0, D, 512 * s, 512) for s in (0, 1)}

    with nc.Block() as block:
        @block.sync
        def _(sp):
            sp.dma_start(ws[:, :, :], I["wsT"].rearrange("g j i -> j g i")).then_inc(rows_in, 16)
            sp.dma_start(rows[:, :], bcast_rows(I["rowsB"], 2 * D + KD * P)).then_inc(rows_in, 16)
            for n, key in enumerate(slab_list):
                load_slab(core, sp, key, source[key])
                if n == 2:
                    sp.dma_start(core.x[:, :, :], I["xT"].rearrange("(k p) n -> p k n", p=P)).then_inc(res_in, 16)

        @block.tensor
        def _(pe):
            prev = None

            def begin(key):
                nonlocal prev
                core.slabs.filled(pe, key)
                read, prev = (core.slabs.done(prev) if prev else None), key
                return read

            def by_feature(name, s, src, m0=0):
                read = begin((name, s))
                w = core.slab((name, s), KD, 512)
                for m in range(4):
                    key = (name, 4 * s + m)
                    core.banks.vacant(pe, key)
                    product(pe, core.ps(key)[:, :], [w[:, k, m * P:(m + 1) * P] for k in range(KD)],
                            [src[:, k, 0:T] for k in range(KD)], read if m == 0 else None)\
                        .then_inc(core.banks.put(key), 1)

            for name in ("z", "v"):
                for s in (0, 1):
                    read = begin((name, s))
                    w = core.slab((name, s), KD, 512)
                    for t in range(TT):
                        key = (name, t, s)
                        core.banks.vacant(pe, key)
                        product(pe, core.ps(key)[:, :], [a.xm[:, k, t * P:(t + 1) * P] for k in range(KD)],
                                [w[:, k, :] for k in range(KD)], read if t == 0 else None)\
                            .then_inc(core.banks.put(key), 1)
            for s in (0, 1):
                by_feature("u", s, a.xm)
            for s in range(4, 12):
                read = begin(("ada", s))
                core.banks.vacant(pe, ("ada", s))
                w = core.slab(("ada", s), KD, 512)
                for m in range(4):
                    last = product(pe, core.ps(("ada", s))[:, 2 * m:2 * m + 2],
                                   [w[:, k, m * P:(m + 1) * P] for k in range(KD)],
                                   [a.c[:, k, :] for k in range(KD)], read if m == 0 else None)
                last.then_inc(core.banks.put(("ada", s)), 1)
            pe.wait_ge(y_done, 1)
            for m in range(KD):
                core.banks.vacant(pe, ("yt", m))
                for t in range(TT):
                    last = pe.transpose(core.ps(("yt", m))[:, t * P:(t + 1) * P], a.y[:, t, m * P:(m + 1) * P],
                                        core.c("ident"))
                last.then_inc(core.banks.put(("yt", m)), 1)
            pe.wait_ge(rows_in, 32)
            pe.wait_ge(v_ready, TT)
            for g in range(KD):
                core.banks.vacant(pe, ("mx", g))
                for c in range(TT):
                    last = pe.matmul(core.ps(("mx", g))[:, c * P:(c + 1) * P], v[:, c, g * P:(g + 1) * P],
                                     ws[:, g, :], start=True, stop=True)
                last.then_inc(core.banks.put(("mx", g)), 1)
            for hh in (0, 1):
                by_feature("ga", hh, a.xm)
                pe.wait_ge(yt_done, KD)
                by_feature("pa", hh, yt)
                by_feature("gb", hh, a.xm)
                pe.wait_ge(sgu_done, KD)
                by_feature("pb", hh, u)
            pe.wait_ge(merged_done, KD)
            for s in (0, 1):
                by_feature("wo", s, merged)
            pe.drain().then_inc(core.slabs.done(("wo", 1)), 1)

        @block.scalar
        def _(act):
            for n, (t, hh) in enumerate(tok):
                core.banks.filled(act, ("z", t, hh))
                if n >= 2:
                    act.wait_ge(zs_used, n - 1)
                act.activation(zs[:, n % 2, :], core.ps(("z", t, hh))[:, :], ACT.Silu)\
                   .then_inc(core.banks.done(("z", t, hh)), 1)
                act.drain().then_inc(zs_done, 1)
            for n, (t, hh) in enumerate(tok):
                core.banks.filled(act, ("v", t, hh))
                act.activation(v[:, t, hh * 512:hh * 512 + 512], core.ps(("v", t, hh))[:, :], ACT.Gelu_apprx_tanh)\
                   .then_inc(core.banks.done(("v", t, hh)), 1)
                act.drain().then_inc(v_done, 1)
            for m in range(KD):
                core.banks.filled(act, ("u", m))
                act.activation(u[:, m, :], core.ps(("u", m))[:, :], ACT.Gelu_apprx_tanh)\
                   .then_inc(core.banks.done(("u", m)), 1)
            act.drain().then_inc(u_done, 1)
            act.wait_ge(gated, 2 * TT)
            for t in range(TT):
                for g in range(GROUPS):
                    act.activation(tmp[:, 0, 0:256], a.y[:, t, g * 256:(g + 1) * 256], ACT.Square,
                                   accum_out=ssq[:, t, g:g + 1])
                    act.drain()
            act.activation(ssq[:, :, :], ssq[:, :, :], ACT.Sqrt, scale=1.0 / 256, bias=core.c("eps6"))
            act.wait_ge(mv_done, 1)
            act.activation(mv[:, :, 1:2], mv[:, :, 1:2], ACT.Sqrt, bias=core.c("eps6"))
            act.drain().then_inc(root2_done, 1)
            for m in range(KD):
                core.banks.filled(act, ("yt", m))
                act.activation(yt[:, m, :], core.ps(("yt", m))[:, :], ACT.Identity,
                               scale=core.v("ssd_norm_w", m)).then_inc(core.banks.done(("yt", m)), 1)
                act.drain().then_inc(yt_done, 1)
            k = 0
            for hh in (0, 1):
                for name in ("ga", "gb"):
                    if k:
                        act.wait_ge(merged_a, 4 * k)
                    for m in range(4 * hh, 4 * hh + 4):
                        core.banks.filled(act, (name, m))
                        act.activation(gate[:, m % 4, :], core.ps((name, m))[:, :], ACT.Sigmoid)\
                           .then_inc(core.banks.done((name, m)), 1)
                        act.drain().then_inc(gate_done, 1)
                    k += 1

        @block.vector
        def _(dve):
            for n, (t, hh) in enumerate(tok):
                dve.wait_ge(zs_done, n + 1)
                dst = a.y[:, t, hh * 512:hh * 512 + 512]
                dve.tensor_tensor(dst, dst, zs[:, n % 2, :], ALU.mult).then_inc(zs_used, 1)
                dve.drain().then_inc(gated, 1)
            for n, (t, hh) in enumerate(tok):
                dve.wait_ge(v_done, n + 1)
                dve.bn_stats(bn[:, t, hh, :], v[:, t, hh * 512:hh * 512 + 512])
            dve.drain()
            for t in range(TT):
                dve.bn_aggr(mv[:, t, :], bn[:, t, :, :].rearrange("p a b -> p (a b)"))
            dve.drain().then_inc(mv_done, 1)
            for s in range(4, 12):
                core.banks.filled(dve, ("ada", s))
                bias = core.v("ada_b", 4 * s, 4).unsqueeze(2).broadcast_to([P, 4, 2])
                dve.tensor_tensor(core.mod[:, 4 * s:4 * s + 4, :],
                                  core.ps(("ada", s))[:, 0:8].rearrange("p (m j) -> p m j", j=2), bias,
                                  ALU.add).then_inc(core.banks.done(("ada", s)), 1)
            dve.wait_ge(root2_done, 1)
            dve.reciprocal(ssq[:, :, :], ssq[:, :, :])
            dve.reciprocal(mv[:, :, 1:2], mv[:, :, 1:2])
            dve.drain()
            for t in range(TT):
                dst = a.y[:, t, :].rearrange("p (g f) -> p g f", g=GROUPS)
                dve.tensor_tensor(dst, dst, ssq[:, t, :].unsqueeze(2).broadcast_to([P, GROUPS, 256]), ALU.mult)
            dve.drain().then_inc(y_done, 1)
            for t in range(TT):
                dve.tensor_scalar(v[:, t, :], v[:, t, :], mv[:, t, 0:1], mv[:, t, 1:2], ALU.subtract, ALU.mult)
                dve.drain().then_inc(v_norm, 1)
            dve.wait_ge(u_done, 1)
            for g in range(KD):
                core.banks.filled(dve, ("mx", g))
                mixed = tmp[:, 1, :]
                dve.tensor_tensor(mixed.rearrange("p (c i) -> p c i", i=P),
                                  core.ps(("mx", g))[:, :].rearrange("p (c i) -> p c i", i=P),
                                  b_s[:, g * P:(g + 1) * P].unsqueeze(1).broadcast_to([P, TT, P]), ALU.add)\
                   .then_inc(core.banks.done(("mx", g)), 1)
                dve.drain()
                dve.tensor_tensor(u[:, g, :], u[:, g, :], mixed, ALU.mult)
                dve.drain().then_inc(sgu_done, 1)
            k = 0
            for hh in (0, 1):
                for name in ("pa", "pb"):
                    for m in range(4 * hh, 4 * hh + 4):
                        dve.wait_ge(gate_done, k + 1)
                        core.banks.filled(dve, (name, m))
                        k += 1
                        if name == "pa":
                            dve.tensor_tensor(merged[:, m, :], core.ps((name, m))[:, :], gate[:, m % 4, :], ALU.mult)\
                               .then_inc(core.banks.done((name, m)), 1)
                            dve.drain().then_inc(merged_a, 1)
                        else:
                            dve.tensor_tensor(tmp[:, 1, :], core.ps((name, m))[:, :], gate[:, m % 4, :], ALU.mult)\
                               .then_inc(core.banks.done((name, m)), 1)
                            dve.drain().then_inc(merged_a, 1)
                            dve.tensor_tensor(merged[:, m, :], merged[:, m, :], tmp[:, 1, :], ALU.add)
                            dve.drain().then_inc(merged_done, 1)
            dve.wait_ge(res_in, 16)
            for m in range(KD):
                core.banks.filled(dve, ("wo", m))
                dve.scalar_tensor_tensor(out=core.x[:, m, :], in0=core.ps(("wo", m))[:, :],
                                         scalar=core.mod[:, 2 * KD + m, 0:1], in1=core.x[:, m, :],
                                         op0=ALU.mult, op1=ALU.add).then_inc(core.banks.done(("wo", m)), 1)

        @block.gpsimd
        def _(pool):
            pool.wait_ge(rows_in, 32)
            for t in range(TT):
                pool.wait_ge(v_norm, t + 1)
                pool.tensor_tensor(v[:, t, :], v[:, t, :], ln_w, ALU.mult)
                pool.drain()
                pool.tensor_tensor(v[:, t, :], v[:, t, :], ln_b, ALU.add)
                pool.drain().then_inc(v_ready, 1)


def router(core, ctx, b):
    core.stage = "router_"
    nc, I = core.nc, core.ins
    sem = lambda n: core.sem(n, ctx)
    xf = core.sb("xf", [P, KD, T], ctx)
    gates = core.sb("gates", [P, TT, EXPERTS * CAP], ctx)
    sq = core.sb("sq", [P, 2, T], ctx)
    rstd = core.sb("rstd", [P, T], ctx)
    scale2 = core.sb("scale2", [P, KD], ctx)
    rw = core.sb("rw", [P, KD, EXPERTS], ctx)
    aff = core.sb("aff", [P, TT, EXPERTS], ctx)
    top = core.sb("top", [P, TT], ctx)
    den = core.sb("den", [P, TT], ctx)
    pos = core.sb("pos", [P, TT, EXPERTS], ctx)
    mask = core.sb("mask", [P, TT, EXPERTS], ctx)
    work = core.sb("work", [EXPERTS, T], ctx)
    best = core.sb("best", [EXPERTS, 8], ctx)
    names = ["rw_in", "sq_done", "sq_used", "root_done", "scaled", "xf_done", "top_done", "exp_done", "aff_done",
             "mask_done", "masked_done", "pick_done", "gates_done", "xt_round"]
    rw_in, sq_done, sq_used, root_done, scaled, xf_done, top_done, exp_done, aff_done, mask_done, masked_done, \
        pick_done, gates_done, xt_round = (sem(n) for n in names)
    PAIRS = EXPERTS // 2
    core.slabs.begin([])
    core.banks.begin(["rms", "logits"] + [("xt", t, hh) for t in range(TT) for hh in (0, 1)]
                     + ["aff", "mask", "pos"] + [("put", p) for p in range(PAIRS)])
    with nc.Block() as block:
        @block.sync
        def _(sp):
            sp.dma_start(rw[:, :, :], w_tiles(I["router_w"], 0, D, 0, EXPERTS)).then_inc(rw_in, 16)

        @block.tensor
        def _(pe):
            core.banks.vacant(pe, "rms")
            for k in range(KD):
                pe.wait_ge(sq_done, k + 1)
                last = pe.matmul(core.ps("rms")[:, :], core.c("mean_d"), sq[:, k % 2, :], start=k == 0, stop=k == KD - 1)
                if k < KD - 1:
                    last.then_inc(sq_used, 1)
            last.then_inc(core.banks.put("rms"), 1)
            pe.wait_ge(xf_done, KD)
            pe.wait_ge(rw_in, 16)
            core.banks.vacant(pe, "logits")
            for t in range(TT):
                last = product(pe, core.ps("logits")[:, t * EXPERTS:(t + 1) * EXPERTS],
                               [xf[:, k, t * P:(t + 1) * P] for k in range(KD)], [rw[:, k, :] for k in range(KD)])
            last.then_inc(core.banks.put("logits"), 1)
            for t in range(TT):
                for hh in (0, 1):
                    core.banks.vacant(pe, ("xt", t, hh))
                    for m in range(4):
                        last = pe.transpose(core.ps(("xt", t, hh))[:, m * P:(m + 1) * P],
                                            xf[:, 4 * hh + m, t * P:(t + 1) * P], core.c("ident"))
                    last.then_inc(core.banks.put(("xt", t, hh)), 1)
            pe.wait_ge(aff_done, 1)
            core.banks.vacant(pe, "aff")
            for t in range(TT):
                last = pe.transpose(core.ps("aff")[0:EXPERTS, t * P:(t + 1) * P], aff[:, t, :], core.c("ident"))
            last.then_inc(core.banks.put("aff"), 1)
            pe.wait_ge(mask_done, 1)
            core.banks.vacant(pe, "mask")
            for t in range(TT):
                last = pe.transpose(core.ps("mask")[:, t * EXPERTS:(t + 1) * EXPERTS], work[:, t * P:(t + 1) * P],
                                    core.c("ident")[0:EXPERTS, 0:EXPERTS])
            last.then_inc(core.banks.put("mask"), 1)
            pe.wait_ge(masked_done, 1)
            core.banks.vacant(pe, "pos")
            for t in range(TT):
                last = product(pe, core.ps("pos")[:, t * EXPERTS:(t + 1) * EXPERTS],
                               [core.c("ones")] * t + [core.c("tri_f")], [mask[:, j, :] for j in range(t + 1)])
            last.then_inc(core.banks.put("pos"), 1)
            pe.wait_ge(gates_done, TT)
            for p in range(PAIRS):
                core.banks.vacant(pe, ("put", p))
                for t in range(TT):
                    last = pe.transpose(core.ps(("put", p))[:, t * P:(t + 1) * P], gates[:, t, p * P:(p + 1) * P],
                                        core.c("ident"))
                last.then_inc(core.banks.put(("put", p)), 1)

        @block.scalar
        def _(act):
            for k in range(KD):
                if k >= 2:
                    act.wait_ge(sq_used, k - 1)
                act.activation(sq[:, k % 2, :], core.x[:, k, :], ACT.Square).then_inc(sq_done, 1)
            core.banks.filled(act, "rms")
            act.activation(rstd[:, :], core.ps("rms")[:, :], ACT.Sqrt, bias=core.c("eps6"))\
               .then_inc(core.banks.done("rms"), 1)
            act.drain().then_inc(root_done, 1)
            for k in range(KD):
                act.wait_ge(scaled, k + 1)
                act.activation(xf[:, k, :], xf[:, k, :], ACT.Identity, bias=core.mod[:, 3 * KD + k, 0:1])\
                   .then_inc(xf_done, 1)
            act.wait_ge(top_done, 1)
            for t in range(TT):
                act.activation(aff[:, t, :], aff[:, t, :], ACT.Exp, bias=top[:, t:t + 1], accum_out=den[:, t:t + 1])
            act.drain().then_inc(exp_done, 1)
            for t in range(TT):
                for hh in (0, 1):
                    core.banks.filled(act, ("xt", t, hh))
                    act.activation(r32(b.xf_tok[:, t, 0, hh * 512:hh * 512 + 512]), core.ps(("xt", t, hh))[:, :], ACT.Identity)\
                       .then_inc(xt_round, 1)
            for p in range(PAIRS):
                core.banks.filled(act, ("put", p))
                act.activation(b.put[:, p, :], core.ps(("put", p))[:, :], ACT.Identity)\
                   .then_inc(core.banks.done(("put", p)), 1)

        @block.vector
        def _(dve):
            dve.tensor_scalar(scale2[:, :], core.mod[:, 4 * KD:5 * KD, 0], 1.0, None, ALU.add)
            dve.drain()
            dve.tensor_tensor(scale2[:, :], scale2[:, :], core.v("norm2_w", 0, KD), ALU.mult)
            dve.wait_ge(root_done, 1)
            dve.reciprocal(rstd[:, :], rstd[:, :])
            dve.drain()
            for k in range(KD):
                dve.scalar_tensor_tensor(out=xf[:, k, :], in0=core.x[:, k, :], scalar=scale2[:, k:k + 1],
                                         in1=rstd[:, :], op0=ALU.mult, op1=ALU.mult).then_inc(scaled, 1)
            core.banks.filled(dve, "logits")
            dve.tensor_copy(aff[:, :, :], core.ps("logits")[:, 0:TT * EXPERTS].rearrange("p (t e) -> p t e", e=EXPERTS))\
               .then_inc(core.banks.done("logits"), 1)
            dve.drain()
            dve.tensor_reduce(top[:, :], aff[:, :, :], AX.X, ALU.max)
            dve.drain()
            dve.tensor_scalar(top[:, :], top[:, :], -1.0, None, ALU.mult)
            dve.drain().then_inc(top_done, 1)
            dve.wait_ge(exp_done, 1)
            dve.reciprocal(den[:, :], den[:, :])
            dve.drain()
            dve.tensor_tensor(aff[:, :, :], aff[:, :, :], den[:, :].unsqueeze(2).broadcast_to([P, TT, EXPERTS]), ALU.mult)
            dve.drain().then_inc(aff_done, 1)
            for t in range(TT):
                for hh in (0, 1):
                    cols = slice(hh * 512, hh * 512 + 512)
                    dve.wait_ge(xt_round, 2 * t + hh + 1)
                    dve.tensor_tensor(r32(b.xf_tok[:, t, 1, cols]), core.ps(("xt", t, hh))[:, :], r32(b.xf_tok[:, t, 0, cols]),
                                      ALU.subtract).then_inc(core.banks.done(("xt", t, hh)), 1)
            core.banks.filled(dve, "aff")
            dve.tensor_copy(work[:, :], core.ps("aff")[0:EXPERTS, :]).then_inc(core.banks.done("aff"), 1)
            for _ in range(CAP // 8):
                dve.drain()
                dve.max(best[:, :], work[:, :])
                dve.drain()
                dve.match_replace(work[:, :], best[:, :], work[:, :], -1.0)
            dve.drain()
            dve.tensor_scalar(work[:, :], work[:, :], 0.0, None, ALU.is_lt)
            dve.drain().then_inc(mask_done, 1)
            core.banks.filled(dve, "mask")
            dve.tensor_copy(mask[:, :, :], core.ps("mask")[:, 0:TT * EXPERTS].rearrange("p (t e) -> p t e", e=EXPERTS))\
               .then_inc(core.banks.done("mask"), 1)
            dve.drain().then_inc(masked_done, 1)
            core.banks.filled(dve, "pos")
            dve.tensor_tensor(pos[:, :, :], core.ps("pos")[:, 0:TT * EXPERTS].rearrange("p (t e) -> p t e", e=EXPERTS),
                              mask[:, :, :], ALU.mult).then_inc(core.banks.done("pos"), 1)
            dve.drain()
            over = lambda ap: ap.unsqueeze(2).broadcast_to([P, EXPERTS, CAP])
            for t in range(TT):
                dve.tensor_tensor(r32(b.pick[:, t, :]).rearrange("p (e s) -> p e s", s=CAP),
                                  core.c("slot").unsqueeze(1).broadcast_to([P, EXPERTS, CAP]), over(pos[:, t, :]),
                                  ALU.is_equal).then_inc(pick_done, 1)

        @block.gpsimd
        def _(pool):
            pool.wait_ge(aff_done, 1)
            for t in range(TT):
                pool.wait_ge(pick_done, t + 1)
                pool.tensor_tensor(gates[:, t, :].rearrange("p (e s) -> p e s", s=CAP),
                                   r32(b.pick[:, t, :]).rearrange("p (e s) -> p e s", s=CAP),
                                   aff[:, t, :].unsqueeze(2).broadcast_to([P, EXPERTS, CAP]), ALU.mult)\
                    .then_inc(gates_done, 1)


def experts(core, ctx, b):
    core.stage = "experts_"
    nc, I = core.nc, core.ins
    sem = lambda n: core.sem(n, ctx)
    PAIRS = EXPERTS // 2
    HK = KD // 2
    SIZE, LEAD = HK * 512, 2
    xg = core.sb("xg", [P, KD, 2, 2 * CAP], ctx)
    ht = core.sb("ht", [P, KD, 2 * CAP], ctx)
    hid = core.sb("hid", [CAP, 2, D], ctx)
    up = core.sb("up", [CAP, 512], ctx)
    part = core.sb("part", [P, 2, 512], ctx)
    y = core.sb("yslot", [P, D], ctx)
    high = core.sb("high", [P, HIGH, SIZE], ctx)
    raw_flat = core.ring[:, :, :].rearrange("p a b -> p (a b)")
    banks = core.banks
    slabs, halves = core.pieces, core.halves
    raw = lambda key: raw_flat[:, slabs.slot(key) * SIZE:(slabs.slot(key) + 1) * SIZE]
    hi = lambda key: high[:, halves.slot(key), :]

    plan = [("g", 0, 0), ("u", 0, 0), ("g", 1, 0), ("u", 1, 0), ("g", 0, 1), ("ht", 0), ("d", 0, 0), ("d", 1, 0),
            ("u", 0, 1), ("g", 1, 1), ("u", 1, 1), ("ht", 1), ("d", 0, 1), ("d", 1, 1)]
    products = [e for e in plan if e[0] != "ht"]
    pieces = [(*e, kk) for e in products for kk in (0, 1)]
    folds = len(products)
    slabs.begin(pieces, reps=PAIRS)
    halves.begin(pieces, reps=PAIRS)
    banks.begin([("xg", c, q) for c in (0, 1) for q in (0, 1)] + plan + [("sc", m) for m in range(KD)], reps=PAIRS)
    weight = {"g": I["w_gate"], "u": I["w_up"], "d": I["w_down"]}
    xg_done, slab_round, part_done, folded, silu_done, hid_done, ht_round, ht_done = (
        sem(n) for n in ("xg_done", "slab_round", "part_done", "folded", "silu_done", "hid_done", "ht_round", "ht_done"))
    rows = lambda e: slice(CAP * e[2], CAP * e[2] + CAP) if e[0] == "d" else slice(0, CAP)
    others = lambda e: slice(0, CAP) if rows(e).start else slice(CAP, P)
    fold_no = {e: n for n, e in enumerate(products)}
    hid_no = {(hh, e): n for n, (hh, e) in enumerate((p[1], p[2]) for p in products if p[0] == "u")}

    with nc.Block() as block:
        @block.sync
        def _(sp):
            with sp.Fori(0, PAIRS) as i:
                for key in pieces:
                    n, hh, e, kk = key
                    at = sp.snap(2 * i + e, min_val=0, max_val=EXPERTS - 1)
                    slabs.vacant(sp, key, i)
                    src = weight[n][bass.ds(at, 1), HK * P * kk:HK * P * (kk + 1), 512 * hh:512 * hh + 512]
                    sp.dma_start(raw(key).rearrange("p (k n) -> p k n", k=HK), src.rearrange("a (k p) n -> p (a k) n", p=P))\
                      .then_inc(slabs.put(key), 16)

        @block.tensor
        def _(pe):
            for free in slabs.free + halves.free:
                pe.nop().then_inc(free, 1)
            with pe.Fori(0, PAIRS) as i:
                col = pe.snap(i * P, min_val=0, max_val=(PAIRS - 1) * P)
                for c in (0, 1):
                    for q in (0, 1):
                        banks.vacant(pe, ("xg", c, q), i)
                        for m in range(4):
                            last = product(pe, core.ps(("xg", c, q))[:, m * P:(m + 1) * P],
                                           [r32(b.xf_tok[:, t, c, (4 * q + m) * P:(4 * q + m + 1) * P]) for t in range(TT)],
                                           [r32(b.pick[:, t, bass.ds(col, P)]) for t in range(TT)])
                        last.then_inc(banks.put(("xg", c, q)), 1)
                pe.wait_ge(xg_done, 4 * i + 4)
                to_tell = []
                for e in plan:
                    banks.vacant(pe, e, i)
                    if e[0] == "ht":
                        pe.wait_ge(hid_done, 4 * i + 1 + max(n for (hh, x), n in hid_no.items() if x == e[1]))
                        for k in range(KD):
                            last = pe.matmul(core.ps(e)[:, k * CAP:(k + 1) * CAP], hid[:, e[1], k * P:(k + 1) * P],
                                             core.c("ident")[0:CAP, 0:CAP], start=True, stop=True)
                        last.then_inc(banks.put(e), 1)
                        continue
                    if e[0] == "d" and e[1] == 0:
                        pe.wait_ge(ht_done, 2 * i + e[2] + 1)
                    for kk in (0, 1):
                        key = (*e, kk)
                        halves.filled(pe, key, i)
                        w_hi, w_lo = (w.rearrange("p (k n) -> p k n", k=HK) for w in (hi(key), raw(key)))
                        for k in range(HK):
                            lhs = r32(ht[:, HK * kk + k, :] if e[0] == "d" else xg[:, HK * kk + k, e[2], :])
                            for w in (w_hi, w_lo):
                                last = pe.matmul(core.ps(e)[:, :], lhs, r32(w[:, k, :]), start=kk == 0 and k == 0 and w is w_hi,
                                                 stop=kk == 1 and k == HK - 1 and w is w_lo)
                                if to_tell:
                                    last.then_inc(to_tell.pop(0), 1)
                        to_tell = [slabs.done(key), halves.done(key)]
                    last.then_inc(banks.put(e), 1)
                pe.wait_ge(folded, folds * i + folds)
                for m in range(KD):
                    banks.vacant(pe, ("sc", m), i)
                    last = pe.matmul(core.ps(("sc", m))[:, :], y[:, m * P:(m + 1) * P], b.put[:, bass.ds(i, 1), :]
                                     .rearrange("p a n -> p (a n)"), start=True, stop=True)
                    last.then_inc(banks.put(("sc", m)), 1)
                    if to_tell:
                        pe.nop().then_inc(to_tell.pop(0), 1)

        @block.scalar
        def _(act):
            def round_piece(n, i):
                key = pieces[n]
                slabs.filled(act, key, i)
                halves.vacant(act, key, i)
                act.activation(r32(hi(key)), raw(key), ACT.Identity).then_inc(slab_round, 1)

            def silu(e, i):
                act.wait_ge(folded, folds * i + fold_no[e] + 1)
                dst = hid[:, e[2], 512 * e[1]:512 * e[1] + 512]
                act.activation(dst, dst, ACT.Silu).then_inc(silu_done, 1)

            with act.Fori(0, PAIRS) as i:
                for n in range(LEAD):
                    round_piece(n, i)
                for c in (0, 1):
                    for q in (0, 1):
                        banks.filled(act, ("xg", c, q), i)
                        act.activation(r32(xg[:, 4 * q:4 * q + 4, :, c * CAP:(c + 1) * CAP]),
                                       core.ps(("xg", c, q))[:, :].rearrange("p (m e s) -> p m e s", m=4, e=2), ACT.Identity)\
                           .then_inc(banks.done(("xg", c, q)), 1)
                        act.drain().then_inc(xg_done, 1)
                n = 0
                for e in plan:
                    if e[0] == "ht":
                        banks.filled(act, e, i)
                        act.activation(r32(ht[:, :, 0:CAP]), core.ps(e)[:, :].rearrange("p (k s) -> p k s", k=KD), ACT.Identity)\
                           .then_inc(ht_round, 1)
                        continue
                    for _ in (0, 1):
                        if n + LEAD < len(pieces):
                            round_piece(n + LEAD, i)
                        n += 1
                    banks.filled(act, e, i)
                    if fold_no[e] >= 2:
                        act.wait_ge(folded, folds * i + fold_no[e] - 1)
                    act.activation(part[rows(e), fold_no[e] % 2, :], core.ps(e)[others(e), :], ACT.Identity).then_inc(part_done, 1)
                    if e[0] == "u":
                        silu(("g", e[1], e[2]), i)

        @block.vector
        def _(dve):
            def rest_of_piece(n, i):
                key = pieces[n]
                dve.wait_ge(slab_round, len(pieces) * i + n + 1)
                dve.tensor_tensor(r32(raw(key)), raw(key), r32(hi(key)), ALU.subtract).then_inc(halves.put(key), 1)

            with dve.Fori(0, PAIRS) as i:
                for n in range(LEAD):
                    rest_of_piece(n, i)
                n = 0
                for e in plan:
                    if e[0] == "ht":
                        dve.wait_ge(ht_round, 2 * i + e[1] + 1)
                        dve.tensor_tensor(r32(ht[:, :, CAP:2 * CAP]), core.ps(e)[:, :].rearrange("p (k s) -> p k s", k=KD),
                                          r32(ht[:, :, 0:CAP]), ALU.subtract).then_inc(banks.done(e), 1)
                        dve.drain().then_inc(ht_done, 1)
                        continue
                    for _ in (0, 1):
                        if n + LEAD < len(pieces):
                            rest_of_piece(n + LEAD, i)
                        n += 1
                    dve.wait_ge(part_done, folds * i + fold_no[e] + 1)
                    cols = slice(512 * e[1], 512 * e[1] + 512)
                    dst = {"g": hid[:, e[2], cols], "u": up[:, :], "d": y[rows(e), cols]}[e[0]]
                    dve.tensor_tensor(dst, core.ps(e)[rows(e), :], part[rows(e), fold_no[e] % 2, :], ALU.add)\
                       .then_inc(banks.done(e), 1)
                    dve.drain().then_inc(folded, 1)
                    if e[0] == "u":
                        dve.wait_ge(silu_done, 4 * i + hid_no[e[1:]] + 1)
                        dve.tensor_tensor(hid[:, e[2], cols], hid[:, e[2], cols], up[:, :], ALU.mult)
                        dve.drain().then_inc(hid_done, 1)
                for m in range(KD):
                    banks.filled(dve, ("sc", m), i)
                    dve.scalar_tensor_tensor(out=core.x[:, m, :], in0=core.ps(("sc", m))[:, :],
                                             scalar=core.mod[:, 5 * KD + m, 0:1], in1=core.x[:, m, :],
                                             op0=ALU.mult, op1=ALU.add).then_inc(banks.done(("sc", m)), 1)


def blocked(ap):
    return ap.rearrange("p (r n c) -> p n r c", n=NBLK, c=QB)


class Norm:

    def __init__(self, core, ctx, per, sq, before=0):
        self.core, self.per, self.sq, self.before = core, per, sq, before
        self.rstd = core.sb("norm_rstd", [P, T], ctx)
        self.summand, self.centred, self.squared, self.square_read, self.root, self.scaled, self.shifted, self.ready = core.norm_sems

    def at(self, i, n, k, each=KD):
        return i * (self.per * each) + (self.before + n) * each + k

    def tensor(self, pe, i, n, told=()):
        core, banks = self.core, self.core.banks
        banks.vacant(pe, ("mean", n), i)
        for k in range(KD):
            pe.wait_ge(self.summand, self.at(i, n, k + 1))
            last = pe.matmul(core.ps(("mean", n))[:, :], core.c("mean_d"), core.x[:, k, :],
                             start=k == 0, stop=k == KD - 1)
            if k < len(told):
                last.then_inc(told[k], 1)
        last.then_inc(banks.put(("mean", n)), 1)
        banks.vacant(pe, ("var", n), i)
        for k in range(KD):
            pe.wait_ge(self.squared, self.at(i, n, k + 1))
            last = pe.matmul(core.ps(("var", n))[:, :], core.c("mean_d"), self.sq[:, k % 2, :],
                             start=k == 0, stop=k == KD - 1)
            if k < KD - 1:
                last.then_inc(self.square_read, 1)
        last.then_inc(banks.put(("var", n)), 1)

    def vector(self, dve, i, n, gain):
        core, banks = self.core, self.core.banks
        banks.filled(dve, ("mean", n), i)
        for k in range(KD):
            last = dve.tensor_tensor(core.x[:, k, :], core.x[:, k, :], core.ps(("mean", n))[:, :], ALU.subtract)
            if k == KD - 1:
                last.then_inc(banks.done(("mean", n)), 1)
                dve.drain().then_inc(self.centred, 1)
            else:
                last.then_inc(self.centred, 1)
        dve.wait_ge(self.root, self.at(i, n, 1, 1))
        dve.reciprocal(self.rstd[:, :], self.rstd[:, :])
        dve.drain()
        for k in range(KD):
            dve.scalar_tensor_tensor(out=core.x[:, k, :], in0=core.x[:, k, :], scalar=gain(k),
                                     in1=self.rstd[:, :], op0=ALU.mult, op1=ALU.mult).then_inc(self.scaled, 1)
        for k in range(KD):
            dve.wait_ge(self.shifted, self.at(i, n, k + 1))
            dve.tensor_tensor(r32(core.x[:, k, :]), core.x[:, k, :], r32(core.x_hi[k]), ALU.subtract).then_inc(self.ready, 1)

    def scalar(self, act, i, n, shift):
        core, banks = self.core, self.core.banks
        for k in range(KD):
            act.wait_ge(self.centred, self.at(i, n, k + 1))
            if k >= 2:
                act.wait_ge(self.square_read, self.at(i, n, k - 1, KD - 1))
            act.activation(self.sq[:, k % 2, :], core.x[:, k, :], ACT.Square).then_inc(self.squared, 1)
        banks.filled(act, ("var", n), i)
        act.activation(self.rstd[:, :], core.ps(("var", n))[:, :], ACT.Sqrt, bias=core.c("eps5"))\
           .then_inc(banks.done(("var", n)), 1)
        act.drain().then_inc(self.root, 1)
        for k in range(KD):
            act.wait_ge(self.scaled, self.at(i, n, k + 1))
            act.activation(r32(core.x_hi[k]), core.x[:, k, :], ACT.Identity, bias=shift(k))
            act.activation(core.x[:, k, :], core.x[:, k, :], ACT.Identity, bias=shift(k))
            act.drain().then_inc(self.shifted, 1)


def entry(core, ctx):
    core.stage = "entry_"
    nc = core.nc
    sem = lambda n: core.sem(n, ctx)
    norm = Norm(core, ctx, 1, core.sb("norm_sq", [P, 2, T], ctx))
    old = core.sb("old", [P, KD, T], ctx)
    sq_done, sq_used, root_done = sem("sq_done"), sem("sq_used"), sem("root_done")
    core.slabs.begin([])
    core.banks.begin(["rms", ("mean", 0), ("var", 0)])
    with nc.Block() as block:
        @block.tensor
        def _(pe):
            core.banks.vacant(pe, "rms")
            for k in range(KD):
                pe.wait_ge(sq_done, k + 1)
                last = pe.matmul(core.ps("rms")[:, :], core.c("mean_d"), norm.sq[:, k % 2, :], start=k == 0, stop=k == KD - 1)
                if k < KD - 1:
                    last.then_inc(sq_used, 1)
            last.then_inc(core.banks.put("rms"), 1)
            norm.tensor(pe, 0, 0)

        @block.scalar
        def _(act):
            for k in range(KD):
                if k >= 2:
                    act.wait_ge(sq_used, k - 1)
                act.activation(norm.sq[:, k % 2, :], core.x[:, k, :], ACT.Square).then_inc(sq_done, 1)
            core.banks.filled(act, "rms")
            act.activation(norm.rstd[:, :], core.ps("rms")[:, :], ACT.Sqrt, bias=core.c("eps6"))\
               .then_inc(core.banks.done("rms"), 1)
            act.drain().then_inc(root_done, 1)
            norm.scalar(act, 0, 0, lambda k: core.v("ln_in_b_2", k))

        @block.vector
        def _(dve):
            dve.wait_ge(root_done, 1)
            dve.reciprocal(norm.rstd[:, :], norm.rstd[:, :])
            dve.drain()
            for k in range(KD):
                dve.scalar_tensor_tensor(out=old[:, k, :], in0=core.x[:, k, :], scalar=core.v("final_norm_w", k),
                                         in1=norm.rstd[:, :], op0=ALU.mult, op1=ALU.mult)
            dve.drain()
            for k in range(KD):
                dve.tensor_copy(core.x[:, k, :].rearrange("p (n r c) -> p n r c", n=NBLK, c=QB), blocked(old[:, k, :]))\
                   .then_inc(norm.summand, 1)
            norm.vector(dve, 0, 0, lambda k: core.v("ln_in_g_2", k))


def layer_plan():

    def attention(kind, heads, lag, before=None):
        units = [(kind, h, n) for h in range(heads) for n in range(TT)]
        out = []
        for x in range(len(units) + lag + 1):
            if before and x < len(units) and x % TT == 0:
                out += before(x // TT)
            if x < len(units):
                out.append(("scores", *units[x]))
            if lag <= x < len(units) + lag:
                out.append(("turn", *units[x - lag]))
            if x > lag and (x - lag) % TT == 0:
                h = (x - lag) // TT - 1
                if kind == "df" and h:
                    out.append(("msq", "df", h - 1))
                out.append(("values", kind, h))
        return out + [("msq", "df", heads - 1)] * (kind == "df")

    plan = [("feat", "naq", m) for m in range(4)] + [("feat", "nak", m) for m in range(4)]
    plan += [("tok", "nav", t, hh) for hh in (0, 1) for t in range(TT)]
    plan += attention("na", NA_HEADS, 2)
    for w in ("dfq", "dfk"):
        for m in range(5):
            plan += [("feat", w, m)] * (m < 4) + [("swap", w, m - 1)] * (m > 0)
    plan += [("tok", "dfv", t, hh) for hh in (0, 1) for t in range(TT)]
    plan += attention("df", DF_HEADS, 3)
    plan += [("feat", "cq", m) for m in range(3)] + [("feat", "ckv", m) for m in range(2)] + [("kr",)]
    plan += [("msq", "q"), ("msq", "kv"), ("swap", "kr", 0)]
    plan += [("mv", t) for t in range(TT)]
    plan += attention("ml", MLA_HEADS, 2, lambda h: [("mq", h), ("mk", h), ("swap", "mq", h)])
    for b in range(3):
        plan += [("gate", b, m) for m in range(KD)] + [("branch", b, m) for m in range(KD)]
    plan += [("wo", m) for m in range(KD)] + [("norm", 0)]
    plan += [e for f in range(KF) for e in (("fg", f), ("fu", f))]
    return plan + [("fo", m) for m in range(KD)] + [("norm", 1)]


def numbered(events, wanted):
    chosen = [e for e in events if wanted(e)]
    return {e: n for n, e in enumerate(chosen)}, len(chosen)


def layers(core, ctx, out):
    core.stage = "layers_"
    nc, I = core.nc, core.ins
    sem = lambda n: core.sem(n, ctx)
    con2 = core.sb("con2", [P, NCON2], ctx)
    c2 = lambda n: con2[:, CON2[n][0]:CON2[n][0] + CON2[n][1]]
    x, x_hi, banks = core.x, core.x_hi, core.banks
    slabs, halves = core.pieces.narrowed(PIECES), core.halves.narrowed(HALVES)
    lv = core.sb("lv", [P, NLAYER], ctx)
    vec = lambda n, k=0: lv[:, LAYER[n][0] + k:LAYER[n][0] + k + 1]
    work = core.sb("work", [P, 24 * T], ctx)
    raw_at = lambda key: slabs.slot(key) * PIECE
    hi_at = lambda key: (PIECES + halves.slot(key)) * PIECE
    tiles = lambda a, n: work[:, a * T:(a + n) * T].rearrange("p (m t) -> p m t", t=T)
    proj = {n: tiles(4 * k, 4) for k, n in enumerate(("naq", "nak", "nav", "dfq", "dfk", "dfv"))}
    proj |= {"cq": tiles(0, 3), "ckv": tiles(3, 2), "kr": tiles(5, 1), "mv": tiles(8, 4), "mq": tiles(12, 2), "mk": tiles(14, 2)}
    merged, hidden = tiles(0, 8), tiles(0, KF)
    heads_out = core.sb("heads_out", [P, 3, 4, T], ctx)
    NP = 6
    p = core.sb("p", [P, NP, T], ctx)
    pt = core.sb("pt", [P, 2, TT, T], ctx)
    gates = pt[:, :, :, :].rearrange("p a b t -> p (a b) t")
    table = core.sb("table", [P, NA_HEADS, RUN], ctx)
    lamv = pt[:, 0, 0, 0:256].rearrange("p (a b n) -> p a b n", a=2, b=2)
    lam = core.sb("lam", [P, 8], ctx)
    side = table[:, :, :].rearrange("p h n -> p (h n)")[:, 0:2 * T].rearrange("p (a t) -> p a t", a=2)
    norm = Norm(core, ctx, 2, table[:, :, :].rearrange("p h n -> p (h n)")[:, 2 * T:4 * T].rearrange("p (a t) -> p a t", a=2), before=1)
    rot = norm.rstd

    plan = layer_plan()
    soft = [(*e[1:], j) for e in plan if e[0] == "scores" for j in range(1 + (e[1] == "df"))]
    NS = len(soft)
    soft_no = {s: n for n, s in enumerate(soft)}
    of_unit = lambda u: [soft_no[(*u, j)] for j in range(1 + (u[0] == "df"))]
    unit_no, UNITS = numbered(plan, lambda e: e[0] == "turn")
    head_no, HEADS_ALL = numbered(plan, lambda e: e[0] == "values")
    copy_no, COPIES = numbered(plan, lambda e: e[0] in ("feat", "tok", "kr", "mv", "mq", "mk"))
    swap_no, SWAPS = numbered(plan, lambda e: e[0] == "swap")
    scaled_no, SCALED = numbered(soft, lambda s: s[3] == 0)
    assert NS % NP == 0 and HEADS_ALL % 2 == 0
    SQUARES, LATENT = DF_HEADS + 5, 5
    negmax = core.sb("negmax", [P, NS], ctx)
    sums = core.sb("sums", [P, NS], ctx)
    recip = core.sb("recip", [P, NS], ctx)
    keys = []
    for e in plan:
        if e[0] == "scores":
            keys += [("scores", *e[1:], j) for j in range(1 + (e[1] == "df"))]
        else:
            keys += [("mean", e[1]), ("var", e[1])] if e[0] == "norm" else [e]
    banks.begin(keys, reps=LAYERS)

    def near(n):
        lo, hi = max(n - 1, 0), min(n + 1, NBLK - 1)
        return lo, hi - lo + 1

    W, G0 = "w_in_2", 3072 + QRANK + KVRANK + ROPE_D
    source = {(n, hh): (W, 0, D, 512 * k + 256 * hh, 256)
              for k, n in enumerate(("naq", "nak", "nav", "dfq", "dfk", "dfv")) for hh in (0, 1)}
    source |= {("cq", 0): (W, 0, D, 3072, 256), ("cq", 1): (W, 0, D, 3072 + 256, QRANK - 256),
               ("ckv", 0): (W, 0, D, 3072 + QRANK, KVRANK + ROPE_D)}
    source |= {("mla", 0): ("w_mla_2", 0, 3 * 768), ("mla", 1): ("w_mla_2", 3 * 768, 2 * D)}
    for b in range(3):
        source |= {("gate", b, c): (W, 0, D, G0 + b * D + 256 * c, 256) for c in range(4)}
        source |= {("branch", b, hh): ("w_branch_2", BR * b, BR, 512 * hh, 512) for hh in (0, 1)}
    source |= {("wo", c): ("w_out_2", 0, D, 256 * c, 256) for c in range(4)}
    source |= {("ffn", f): ("w_ffn_in_2", 0, D, 2 * P * f, 2 * P) for f in range(KF)}
    source |= {("fo", m, hh): ("w_ffn_out_2", FF // 2 * hh, FF // 2, P * m, P) for m in range(KD) for hh in (0, 1)}
    slabs.begin(list(source), reps=LAYERS)
    split_keys = [k for k in source if k[0] != "mla"]
    halves.begin(split_keys, reps=LAYERS)
    split_no = {k: n for n, k in enumerate(split_keys)}

    def slabs_of(e):
        if e[0] == "tok":
            return [(e[1], e[3])]
        if e[0] == "feat":
            return [(e[1], 0 if e[1] == "ckv" else e[2] // 2)]
        return {"gate": lambda: [("gate", e[1], e[2] // 2)], "branch": lambda: [("branch", e[1], e[2] // 4)],
                "wo": lambda: [("wo", e[1] // 2)], "fg": lambda: [("ffn", e[1])],
                "fo": lambda: [("fo", e[1], 0), ("fo", e[1], 1)]}.get(e[0], lambda: [])()

    due, placed = {}, 0
    for e in plan:
        for key in slabs_of(e):
            n = split_no[key]
            if n == placed and n + 1 < len(split_keys):
                placed += 1
                nxt = split_keys[n + 1]
                due.setdefault(("mq", 1) if nxt == ("gate", 0, 0) else e, []).append(nxt)
    assert sum(len(v) for v in due.values()) == len(split_keys) - 1

    def parts(key):
        _, _, rows, _, cols = source[key]
        k, out = rows // P, []
        for at in (hi_at(key), raw_at(key)):
            flat = core.ring[:, :, :].rearrange("p a b -> p (a b)")
            out.append(flat[:, at:at + k * cols].rearrange("p (k n) -> p k n", k=k))
        return out

    def whole(key, at):
        n = source[key][2] // P * source[key][4]
        return core.ring[:, :, :].rearrange("p a b -> p (a b)")[:, at:at + n]

    const_in, layer_done, params_in, table_in = sem("const_in"), sem("layer_done"), sem("params_in"), sem("table_in")
    lam_sums, lam_exps = sem("lam_sums"), sem("lam_exps")
    slab_round, heads_round, heads_split, merged_round, merged_split, hidden_round, hidden_split, joined = (
        sem(n) for n in ("slab_round", "heads_round", "heads_split", "merged_round", "merged_split", "hidden_round",
                         "hidden_split", "joined"))
    work_tile = lambda n: work[:, n * T:(n + 1) * T]
    heads_hi = lambda b, k: work_tile(8 + 4 * b + k)
    merged_hi = lambda m: work_tile(8 + m)

    def hidden_hi(f):
        if f < 12:
            return heads_out[:, f // 4, f % 4, :]
        return p[:, f - 12, :] if f < 12 + NP else pt[:, (f - 12 - NP) // TT, (f - 12 - NP) % TT, :]
    copied, rotated, max_done, exp_done, recip_done, scaled, combined, turned, head_done = (
        sem(n) for n in ("copied", "rotated", "max_done", "exp_done", "recip_done", "scaled", "combined", "turned", "head_done"))
    squared, root_done, latent_done, gate_done, branch_done, silu_done, hidden_done, out_done = (
        sem(n) for n in ("squared", "root_done", "latent_done", "gate_done", "branch_done", "silu_done", "hidden_done", "out_done"))

    def free_slot(eng, s, i):
        if s >= NP:
            banks.filled_too(eng, ("turn", *soft[s - NP][:3]), ("scores", *soft[s]), i)

    with nc.Block() as block:
        @block.sync
        def _(sp):
            sp.dma_start(con2[:, :], I["con2"]).then_inc(const_in, 16)
            with sp.Fori(0, LAYERS) as i:
                at = sp.snap(i, min_val=0, max_val=LAYERS - 1)
                sp.wait_ge(layer_done, i + 1)
                sp.dma_start(lv[:, :], I["layer_vec"][bass.ds(at, 1)].rearrange("a p n -> (a p) n")).then_inc(params_in, 16)
                sp.dma_start(pt[:, 0, 0, 0:256],
                             I["lam"][bass.ds(at, 1), :].broadcast_to([P, 256])).then_inc(params_in, 16)
                for r in range(ROWS):
                    lead = I["rpb"][bass.ds(at, 1), r * RPB_W:r * RPB_W + 1]
                    src = bass.AP(tensor=lead.tensor, offset=lead.offset, ap=[[1, QB], [RPB_H * RPB_W, NA_HEADS], [1, RUN]])
                    sp.dma_start(table[r * QB:(r + 1) * QB, :, :], src).then_inc(table_in, 16)
                for key, what in source.items():
                    slabs.vacant(sp, key, i)
                    flat = core.ring[:, :, :].rearrange("p a b -> p (a b)")
                    if key[0] == "mla":
                        name, c0, cols = what
                        sp.dma_start(flat[:, raw_at(key):raw_at(key) + cols],
                                     I[name][bass.ds(at, 1), :, c0:c0 + cols].rearrange("a p n -> p (a n)"))\
                          .then_inc(slabs.put(key), 16)
                        continue
                    name, r0, rows, c0, cols = what
                    sp.dma_start(whole(key, raw_at(key)).rearrange("p (k n) -> p k n", n=cols),
                                 I[name][bass.ds(at, 1), r0:r0 + rows, c0:c0 + cols].rearrange("a (k p) n -> p (a k) n", p=P))\
                      .then_inc(slabs.put(key), 16)
            sp.wait_ge(joined, KD)
            sp.dma_start(out.rearrange("(k p) n -> p k n", p=P), x[:, :, :]).then_inc(out_done, 16)
            sp.wait_ge(out_done, 16)

        @block.tensor
        def _(pe):
            pe.wait_ge(const_in, 16)
            xs = [x[:, k, :] for k in range(KD)]

            def layer(i):
                using, to_tell = [], []

                def need(*keys):
                    if using != list(keys):
                        for k in using:
                            to_tell.append(slabs.done(k))
                            if k[0] != "mla":
                                to_tell.append(halves.done(k))
                        using[:] = keys
                        for k in keys:
                            slabs.filled(pe, k, i) if k[0] == "mla" else halves.filled(pe, k, i)

                def chain(out, pairs, start=True, stop=True):
                    for k, (lhs, rhs) in enumerate(pairs):
                        last = pe.matmul(out, lhs, rhs, start=start and k == 0, stop=stop and k == len(pairs) - 1)
                        if to_tell and k < len(pairs) - 1:
                            last.then_inc(to_tell.pop(0), 1)
                    return last

                def emit(key, lhs, rhs, rows=P):
                    banks.vacant(pe, key, i)
                    chain(core.ps(key)[0:rows, :], list(zip(lhs, rhs))).then_inc(banks.put(key), 1)

                def three(lhs, lhs_lo, rhs, rhs_lo):
                    return [(r32(a), r32(b)) for k in range(len(lhs))
                            for a, b in ((lhs[k], rhs[k]), (lhs[k], rhs_lo[k]), (lhs_lo[k], rhs[k]))]

                def emit3(key, lhs, lhs_lo, rhs, rhs_lo, rows=P):
                    banks.vacant(pe, key, i)
                    chain(core.ps(key)[0:rows, :], three(lhs, lhs_lo, rhs, rhs_lo)).then_inc(banks.put(key), 1)

                def by_feature(key, slab, c0, rhs, rhs_lo, cols=P):
                    need(slab)
                    hi, lo = parts(slab)
                    n = hi.shape[1]
                    emit3(key, [hi[:, k, c0:c0 + cols] for k in range(n)], [lo[:, k, c0:c0 + cols] for k in range(n)],
                          rhs, rhs_lo, rows=cols)

                def scores(kind, h, n):
                    q = slice(n * P, (n + 1) * P)
                    if kind == "na":
                        if (h, n) == (0, 0):
                            pe.wait_ge(copied, i * COPIES + copy_no[("feat", "nak", 3)] + 1)
                        lo, nb = near(n)
                        r = slice((h % 2) * 64, (h % 2) * 64 + 64)
                        key = ("scores", kind, h, n, 0)
                        banks.vacant(pe, key, i)
                        pe.matmul(core.ps(key)[:, 0:nb * P], proj["naq"][r, h // 2, q],
                                  proj["nak"][r, h // 2, lo * P:(lo + nb) * P], start=True, stop=True)\
                            .then_inc(banks.put(key), 1)
                    elif kind == "df":
                        if (h, n) == (0, 0):
                            pe.wait_ge(rotated, i * SWAPS + swap_no[("swap", "dfk", 3)] + 1)
                        for j in (0, 1):
                            r = slice(j * 64, j * 64 + 64)
                            emit(("scores", kind, h, n, j), [proj["dfq"][r, h, q]], [proj["dfk"][r, h, :]])
                    else:
                        if n == 0:
                            pe.wait_ge(copied, i * COPIES + copy_no[("mk", h)] + 1)
                            pe.wait_ge(rotated, i * SWAPS + swap_no[("swap", "mq", h)] + 1)
                        emit(("scores", kind, h, n, 0), [proj["mq"][0:96, h % 2, q]], [proj["mk"][0:96, h % 2, :]])

                def turn(kind, h, n):
                    key, s = ("turn", kind, h, n), soft_no[(kind, h, n, 0)]
                    if kind == "df":
                        pe.wait_ge(combined, i * (DF_HEADS * TT) + h * TT + n + 1)
                    else:
                        pe.wait_ge(scaled, i * SCALED + scaled_no[(kind, h, n, 0)] + 1)
                    banks.vacant(pe, key, i)
                    for b in range(near(n)[1] if kind == "na" else TT):
                        last = pe.transpose(core.ps(key)[:, b * P:(b + 1) * P], p[:, s % NP, b * P:(b + 1) * P], core.c("ident"))
                    last.then_inc(banks.put(key), 1)

                def values(kind, h):
                    key = ("values", kind, h)
                    turned_pt = pt[:, head_no[key] % 2]
                    v = proj[{"na": "nav", "df": "dfv", "ml": "mv"}[kind]]
                    if h == 0:
                        pe.wait_ge(copied, i * COPIES + copy_no[{"na": ("tok", "nav", 3, 1), "df": ("tok", "dfv", 3, 1),
                                                                 "ml": ("mv", 3)}[kind]] + 1)
                    pe.wait_ge(turned, i * UNITS + unit_no[("turn", kind, h, TT - 1)] + 1)
                    if kind == "na":
                        banks.vacant(pe, key, i)
                        for n in range(NBLK):
                            lo, nb = near(n)
                            last = product(pe, core.ps(key)[0:64, n * P:(n + 1) * P],
                                           [v[:, j, h * 64:h * 64 + 64] for j in range(lo, lo + nb)],
                                           [turned_pt[:, j, n * P:(n + 1) * P] for j in range(lo, lo + nb)])
                        last.then_inc(banks.put(key), 1)
                    else:
                        w = P if kind == "df" else 64
                        emit(key, [v[:, j, h * w:(h + 1) * w] for j in range(TT)], [turned_pt[:, j, :] for j in range(TT)], rows=w)

                for e in plan:
                    kind = e[0]
                    if kind == "feat":
                        slab = slabs_of(e)[0]
                        by_feature(e, slab, (e[2] - 2 * slab[1]) * P, x_hi, xs)
                    elif kind == "tok":
                        need((e[1], e[3]))
                        hi, lo = parts((e[1], e[3]))
                        tok = slice(e[2] * P, (e[2] + 1) * P)
                        banks.vacant(pe, e, i)
                        chain(core.ps(e)[:, 0:256], three([x_hi[k][:, tok] for k in range(KD)], [xs[k][:, tok] for k in range(KD)],
                                                          [hi[:, k, :] for k in range(KD)], [lo[:, k, :] for k in range(KD)]))\
                            .then_inc(banks.put(e), 1)
                    elif kind == "kr":
                        by_feature(e, ("ckv", 0), KVRANK + ROPE_D - 96, x_hi, xs, cols=96)
                    elif kind == "swap":
                        of = {"kr": ("kr",), "mq": ("mq", e[2])}.get(e[1], ("feat", e[1], e[2]))
                        pe.wait_ge(copied, i * COPIES + copy_no[of] + 1)
                        rows, mat = (P, "dswap") if of[0] == "feat" else (96, "mswap")
                        src = proj[e[1]][0:rows, e[2] % (4 if of[0] == "feat" else 2), :]
                        emit(e, [c2(mat)[0:rows, 0:rows]], [src], rows=rows)
                    elif kind == "scores":
                        scores(*e[1:])
                    elif kind == "turn":
                        turn(*e[1:])
                    elif kind == "values":
                        values(*e[1:])
                    elif kind == "msq" and e[1] == "df":
                        pe.wait_ge(squared, i * SQUARES + e[2] + 1)
                        emit(e, [c2("mean_h")], [norm.sq[:, e[2] % 2, :]])
                    elif kind == "msq":
                        first, n, mat = (0, 3, "mean_q") if e[1] == "q" else (3, 2, "mean_kv")
                        pe.wait_ge(squared, i * SQUARES + DF_HEADS + first + n)
                        emit(e, [c2(mat)] * n, [p[:, first + j, :] for j in range(n)])
                    elif kind in ("mv", "mq", "mk"):
                        need(("mla", 0), ("mla", 1))
                        if e == ("mv", 0):
                            pe.wait_ge(latent_done, i * LATENT + LATENT)
                        flat = core.ring[:, :, :].rearrange("p a b -> p (a b)")
                        wq, wkv = (flat[:, raw_at(("mla", j)):raw_at(("mla", j)) + n].rearrange("p (k n) -> p k n", k=k)
                                   for j, n, k in ((0, 3 * 768, 3), (1, 2 * D, 2)))
                        if kind == "mv":
                            emit(e, [proj["ckv"][:, k, e[1] * P:(e[1] + 1) * P] for k in range(2)],
                                 [wkv[:, k, :].rearrange("p (h c) -> p h c", c=128)[:, :, 64:128] for k in range(2)])
                        elif kind == "mq":
                            emit(e, [wq[:, k, e[1] * 96:(e[1] + 1) * 96] for k in range(3)], [proj["cq"][:, k, :] for k in range(3)], rows=96)
                        else:
                            emit(e, [wkv[:, k, e[1] * P:e[1] * P + 64] for k in range(2)], [proj["ckv"][:, k, :] for k in range(2)], rows=64)
                    elif kind == "gate":
                        by_feature(e, slabs_of(e)[0], (e[2] % 2) * P, x_hi, xs)
                    elif kind == "branch":
                        if e[2] == 0:
                            pe.wait_ge(heads_split, i * 12 + 4 * e[1] + 4)
                        by_feature(e, slabs_of(e)[0], (e[2] % 4) * P, [heads_hi(e[1], k) for k in range(4)],
                                   [heads_out[:, e[1], k, :] for k in range(4)])
                    elif kind == "wo":
                        if e[1] == 0:
                            pe.wait_ge(merged_split, i * KD + KD)
                        by_feature(e, slabs_of(e)[0], (e[1] % 2) * P, [merged_hi(m) for m in range(KD)],
                                   [merged[:, m, :] for m in range(KD)])
                    elif kind == "norm":
                        if e[1] == 1:
                            need()
                        norm.tensor(pe, i, e[1], to_tell if e[1] == 1 else ())
                        if e[1] == 1:
                            pe.wait_ge(norm.ready, norm.at(i, 1, KD))
                    elif kind in ("fg", "fu"):
                        if e == ("fg", 0):
                            pe.wait_ge(norm.ready, norm.at(i, 0, KD))
                        by_feature(e, ("ffn", e[1]), P * (kind == "fu"), x_hi, xs)
                    else:
                        if e[1] == 0:
                            pe.wait_ge(hidden_split, i * KF + KF)
                        banks.vacant(pe, e, i)
                        for hh in (0, 1):
                            need(("fo", e[1], hh))
                            hi, lo = parts(("fo", e[1], hh))
                            n = KF // 2
                            last = chain(core.ps(e)[:, :], three([hi[:, k, :] for k in range(n)], [lo[:, k, :] for k in range(n)],
                                                                 [hidden_hi(hh * n + k) for k in range(n)],
                                                                 [hidden[:, hh * n + k, :] for k in range(n)]),
                                         start=hh == 0, stop=hh == 1)
                        last.then_inc(banks.put(e), 1)

            with pe.Fori(0, LAYERS) as i:
                layer(i)

        @block.scalar
        def _(act):
            act.drain().then_inc(layer_done, 1)

            def layer(i):
                act.wait_ge(lam_sums, i + 1)
                act.activation(lam[:, 2:4], lam[:, 0:2], ACT.Exp).then_inc(lam_exps, 1)
                act.wait_ge(params_in, i * 32 + 32)

                def round_slab(key):
                    slabs.filled(act, key, i)
                    halves.vacant(act, key, i)
                    act.activation(r32(whole(key, hi_at(key))), whole(key, raw_at(key)), ACT.Identity).then_inc(slab_round, 1)

                def round_hidden(f):
                    act.wait_ge(hidden_done, i * KF + f + 1)
                    act.activation(r32(hidden_hi(f)), hidden[:, f, :], ACT.Identity).then_inc(hidden_round, 1)

                round_slab(split_keys[0])

                def copy(e, dst, rows=P, scale=1.0, cols=T):
                    banks.filled(act, e, i)
                    act.activation(dst, core.ps(e)[0:rows, 0:cols], ACT.Identity, scale=scale).then_inc(banks.done(e), 1)
                    act.drain().then_inc(copied, 1)

                for e in plan:
                    kind = e[0]
                    if e == ("fo", 0):
                        round_hidden(KF - 1)
                    for key in due.get(e, ()):
                        round_slab(key)
                    if kind == "tok":
                        copy(e, proj[e[1]][:, e[2], 256 * e[3]:256 * e[3] + 256], cols=256)
                    elif kind == "feat":
                        copy(e, proj[e[1]][:, e[2], :], scale=0.125 if e[1] == "naq" else 1.0)
                        if e[1] in ("cq", "ckv"):
                            n = e[2] + (3 if e[1] == "ckv" else 0)
                            if n == 0:
                                banks.filled_too(act, ("turn", "df", DF_HEADS - 1, TT - 1), e, i)
                            act.activation(p[:, n, :], proj[e[1]][:, e[2], :], ACT.Square).then_inc(squared, 1)
                    elif kind == "kr":
                        copy(e, proj["kr"][0:96, 0, :], rows=96)
                    elif kind == "mv":
                        copy(e, proj["mv"][:, e[1], :])
                    elif kind in ("mq", "mk"):
                        if e[1] >= 2:
                            banks.filled_too(act, ("scores", "ml", e[1] - 2, TT - 1, 0), e, i)
                        rows = 96 if kind == "mq" else 64
                        copy(e, proj[kind][0:rows, e[1] % 2, :], rows=rows)
                    elif kind == "scores":
                        for s in of_unit(e[1:]):
                            act.wait_ge(max_done, i * NS + s + 1)
                            key = ("scores", *soft[s])
                            if e[1] == "na":
                                w = near(e[3])[1] * P
                                act.activation(p[:, s % NP, 0:w], p[:, s % NP, 0:w], ACT.Exp, bias=negmax[:, s:s + 1],
                                               accum_out=sums[:, s:s + 1])
                            else:
                                banks.filled(act, key, i)
                                free_slot(act, s, i)
                                if s - soft_no[("ml", 0, 0, 0)] in range(NP):
                                    banks.filled_too(act, ("msq", "kv"), key, i)
                                act.activation(p[:, s % NP, :], core.ps(key)[:, :], ACT.Exp, bias=negmax[:, s:s + 1],
                                               scale=SCALE[e[1]], accum_out=sums[:, s:s + 1]).then_inc(banks.done(key), 1)
                            act.drain().then_inc(exp_done, 1)
                    elif kind == "turn":
                        banks.filled(act, e, i)
                        lo, nb = near(e[3]) if e[1] == "na" else (0, TT)
                        hd = head_no[("values", e[1], e[2])]
                        if e[3] == 0 and hd >= 2:
                            banks.filled_too(act, [k for k, n in head_no.items() if n == hd - 2][0], e, i)
                        act.activation(pt[:, hd % 2, lo:lo + nb, e[3] * P:(e[3] + 1) * P],
                                       core.ps(e)[:, 0:nb * P].rearrange("p (b q) -> p b q", q=P), ACT.Identity)\
                           .then_inc(banks.done(e), 1)
                        act.drain().then_inc(turned, 1)
                    elif kind == "values" and e[1] == "df":
                        banks.filled(act, e, i)
                        if e[2] >= 2:
                            banks.filled_too(act, ("msq", "df", e[2] - 2), e, i)
                        act.activation(norm.sq[:, e[2] % 2, :], core.ps(e)[:, :], ACT.Square).then_inc(squared, 1)
                        act.activation(heads_out[:, 1, e[2], :], core.ps(e)[:, :], ACT.Identity).then_inc(banks.done(e), 1)
                    elif kind == "msq":
                        banks.filled(act, e, i)
                        dst = {"q": side[:, 0, :], "kv": side[:, 1, :]}.get(e[1], side[:, e[-1] % 2, :] if e[1] == "df" else None)
                        if e[1] == "df" and e[2] >= 2:
                            act.wait_ge(head_done, i * HEADS_ALL + head_no[("values", "df", e[2] - 2)] + 1)
                        if e[1] != "df":
                            act.wait_ge(head_done, i * HEADS_ALL + head_no[("values", "df", DF_HEADS - 1)] + 1)
                        act.activation(dst, core.ps(e)[:, :], ACT.Sqrt, bias=core.c("eps6")).then_inc(banks.done(e), 1)
                        act.drain().then_inc(root_done, 1)
                    elif kind == "gate":
                        n = e[1] * KD + e[2]
                        if e[2] == 0:
                            act.wait_ge(head_done, i * HEADS_ALL + HEADS_ALL)
                            if e[1]:
                                banks.filled_too(act, ("branch", e[1] - 1, 0), e, i)
                            for k in range(4):
                                act.activation(r32(heads_hi(e[1], k)), heads_out[:, e[1], k, :], ACT.Identity)\
                                   .then_inc(heads_round, 1)
                        banks.filled(act, e, i)
                        if e[1]:
                            act.wait_ge(branch_done, i * (3 * KD) + n - KD + 1)
                        elif e[2] == 0:
                            banks.filled_too(act, ("values", "ml", MLA_HEADS - 1), e, i)
                        act.activation(gates[:, e[2], :], core.ps(e)[:, :], ACT.Sigmoid, bias=vec("b_gate_2", n))\
                           .then_inc(banks.done(e), 1)
                        act.drain().then_inc(gate_done, 1)
                    elif kind == "norm":
                        norm.scalar(act, i, e[1], lambda k: vec("ln1_b_2" if e[1] == 0 else "ln2_b_2", k))
                    elif kind == "fg":
                        banks.filled(act, e, i)
                        if e[1] >= 2:
                            act.wait_ge(hidden_done, i * KF + e[1] - 1)
                        act.activation(side[:, e[1] % 2, :], core.ps(e)[:, :], ACT.Silu).then_inc(banks.done(e), 1)
                        act.drain().then_inc(silu_done, 1)
                        if e[1]:
                            round_hidden(e[1] - 1)
                    elif kind == "branch" and e[1] == 2:
                        act.wait_ge(branch_done, i * (3 * KD) + 2 * KD + e[2] + 1)
                        act.activation(r32(merged_hi(e[2])), merged[:, e[2], :], ACT.Identity).then_inc(merged_round, 1)
                act.drain().then_inc(layer_done, 1)

            with act.Fori(0, LAYERS) as i:
                layer(i)

        @block.vector
        def _(dve):
            dve.wait_ge(const_in, 16)

            def layer(i):
                dve.wait_ge(params_in, i * 32 + 32)
                dve.tensor_tensor(rot[:, 0:128].rearrange("p (a n) -> p a n", a=2), lamv[:, :, 0, :], lamv[:, :, 1, :], ALU.mult)
                dve.drain()
                dve.tensor_reduce(lam[:, 0:2], rot[:, 0:128].rearrange("p (a n) -> p a n", a=2), AX.X, ALU.add)
                dve.drain().then_inc(lam_sums, 1)
                dve.wait_ge(lam_exps, i + 1)
                dve.scalar_tensor_tensor(out=lam[:, 4:5], in0=lam[:, 3:4], scalar=lam[:, 2:3], in1=vec("lam_init"),
                                         op0=ALU.subtract, op1=ALU.subtract)
                dve.tensor_tensor(lam[:, 5:6], vec("diff_subln_g_2"), vec("one_less"), ALU.mult)
                dve.drain()

                def rest(tile, hi, rounded, count, done):
                    dve.wait_ge(rounded, count)
                    dve.tensor_tensor(r32(tile), tile, r32(hi), ALU.subtract).then_inc(done, 1)

                def rest_of_slab(key):
                    rest(whole(key, raw_at(key)), whole(key, hi_at(key)), slab_round, i * len(split_keys) + split_no[key] + 1,
                         halves.put(key))

                rest_of_slab(split_keys[0])
                recips, combines = [], []

                def maximum(u):
                    kind = u[0]
                    for s in of_unit(u):
                        key, col = ("scores", *soft[s]), negmax[:, s:s + 1]
                        banks.filled(dve, key, i)
                        if kind == "na":
                            _, h, n = u
                            lo, nb = near(n)
                            if (h, n) == (0, 0):
                                dve.wait_ge(table_in, i * (16 * ROWS) + 16 * ROWS)
                            free_slot(dve, s, i)
                            w = p[:, s % NP, 0:nb * P]
                            last = RUN - 1 - (lo - n + 1) * QB
                            bias = table[:, NA_HEADS - 1 - h, last:last + 1]
                            bias = bass.AP(tensor=bias.tensor, offset=bias.offset,
                                           ap=[list(bias.ap[0]), [-QB, nb], [-RPB_W, ROWS], [-1, QB]])
                            four = lambda ap: ap.rearrange("p (b r c) -> p b r c", b=nb, c=QB)
                            dve.tensor_tensor(four(w), four(core.ps(key)[:, 0:nb * P]), bias, ALU.add)\
                               .then_inc(banks.done(key), 1)
                            dve.drain()
                            mask = c2("near0" if n == 0 else "near2" if n == NBLK - 1 else "near1")
                            dve.tensor_tensor_reduce(w, w, mask, 1.0, NEG, ALU.add, ALU.max, col)
                            dve.drain()
                            dve.tensor_scalar(col, col, -1.0, None, ALU.mult)
                        else:
                            dve.tensor_reduce(col, core.ps(key)[:, :], AX.X, ALU.max)
                            dve.drain()
                            dve.tensor_scalar(col, col, -SCALE[kind], None, ALU.mult)
                        dve.drain().then_inc(max_done, 1)

                def invert(u):
                    for s in of_unit(u):
                        dve.wait_ge(exp_done, i * NS + s + 1)
                        dve.reciprocal(recip[:, s:s + 1], sums[:, s:s + 1])
                        dve.drain().then_inc(recip_done, 1)
                    if u[0] == "df":
                        dve.tensor_scalar(recip[:, s:s + 1], recip[:, s:s + 1], lam[:, 4:5], None, ALU.mult)
                        dve.drain()
                        combines.append(u)

                def combine(u):
                    a, b = of_unit(u)
                    dve.wait_ge(scaled, i * SCALED + scaled_no[(*u, 0)] + 1)
                    dve.scalar_tensor_tensor(out=p[:, a % NP, :], in0=p[:, b % NP, :], scalar=recip[:, b:b + 1],
                                             in1=p[:, a % NP, :], op0=ALU.mult, op1=ALU.add).then_inc(combined, 1)

                for e in plan:
                    kind = e[0]
                    if kind == "fo" and e[1] == 0:
                        rest(hidden[:, KF - 1, :], hidden_hi(KF - 1), hidden_round, i * KF + KF, hidden_split)
                    for key in due.get(e, ()):
                        rest_of_slab(key)
                    if kind == "gate" and e[2] == 0:
                        for k in range(4):
                            rest(heads_out[:, e[1], k, :], heads_hi(e[1], k), heads_round, i * 12 + 4 * e[1] + k + 1, heads_split)
                    if kind == "scores":
                        u = e[1:]
                        maximum(u)
                        before = list(combines)
                        if recips:
                            invert(recips.pop(0))
                        if before:
                            combine(combines.pop(0))
                        recips.append(u)
                    elif kind == "turn":
                        while e[1:] in recips:
                            invert(recips.pop(0))
                        while e[1:] in combines:
                            combine(combines.pop(0))
                    elif kind == "swap":
                        banks.filled(dve, e, i)
                        lo, hi, t = (0, P, "d") if e[1] in ("dfq", "dfk") else (64, 96, "m")
                        src = proj[e[1]][lo:hi, e[2] % (4 if t == "d" else 2), :]
                        dve.tensor_tensor(rot[lo:hi, :], core.ps(e)[lo:hi, :], c2(t + "sin")[lo:hi, :], ALU.mult)\
                           .then_inc(banks.done(e), 1)
                        dve.tensor_tensor(src, src, c2(t + "cos")[lo:hi, :], ALU.mult)
                        dve.drain()
                        for dst in ([proj["mk"][lo:hi, j, :] for j in (0, 1)] if e[1] == "kr" else [src]):
                            dve.tensor_tensor(dst, src, rot[lo:hi, :], ALU.add)
                        dve.drain().then_inc(rotated, 1)
                    elif kind == "values" and e[1] != "df":
                        banks.filled(dve, e, i)
                        h, b = e[2], 0 if e[1] == "na" else 2
                        dve.tensor_copy(heads_out[(h % 2) * 64:(h % 2) * 64 + 64, b, h // 2, :], core.ps(e)[0:64, :])\
                           .then_inc(banks.done(e), 1)
                        dve.drain().then_inc(head_done, 1)
                    elif kind == "msq":
                        n = {"q": DF_HEADS, "kv": DF_HEADS + 1}.get(e[1], e[-1])
                        dve.wait_ge(root_done, i * (DF_HEADS + 2) + n + 1)
                        root = side[:, n % 2, :]
                        dve.reciprocal(root, root)
                        dve.drain()
                        if e[1] == "df":
                            dst = heads_out[:, 1, e[2], :]
                            dve.scalar_tensor_tensor(out=dst, in0=dst, scalar=lam[:, 5:6], in1=root, op0=ALU.mult, op1=ALU.mult)
                            dve.drain().then_inc(head_done, 1)
                        else:
                            name, gain, k = ("cq", "mla_q_norm_g_2", 3) if e[1] == "q" else ("ckv", "mla_kv_norm_g_2", 2)
                            for j in range(k):
                                dst = proj[name][:, j, :]
                                dve.scalar_tensor_tensor(out=dst, in0=dst, scalar=vec(gain, j), in1=root, op0=ALU.mult, op1=ALU.mult)\
                                   .then_inc(latent_done, 1)
                    elif kind == "branch":
                        n = e[1] * KD + e[2]
                        dve.wait_ge(gate_done, i * (3 * KD) + n + 1)
                        banks.filled(dve, e, i)
                        dst = merged[:, e[2], :] if e[1] == 0 else rot[:, :]
                        dve.tensor_tensor(dst, core.ps(e)[:, :], gates[:, e[2], :], ALU.mult).then_inc(banks.done(e), 1)
                        dve.drain()
                        if e[1]:
                            dve.tensor_tensor(merged[:, e[2], :], merged[:, e[2], :], rot[:, :], ALU.add)
                            dve.drain()
                        dve.nop().then_inc(branch_done, 1)
                        if e[1] == 2:
                            for m in range(max(e[2] - 1, 0), e[2] + (e[2] == KD - 1)):
                                rest(merged[:, m, :], merged_hi(m), merged_round, i * KD + m + 1, merged_split)
                    elif kind in ("wo", "fo"):
                        banks.filled(dve, e, i)
                        dst = x[:, e[1], :]
                        dve.scalar_tensor_tensor(out=dst, in0=r32(dst), scalar=ALPHA, in1=core.ps(e)[:, :], op0=ALU.mult, op1=ALU.add)\
                           .then_inc(banks.done(e), 1)
                        dve.drain()
                        dve.scalar_tensor_tensor(out=dst, in0=r32(x_hi[e[1]]), scalar=ALPHA, in1=dst, op0=ALU.mult, op1=ALU.add)
                        dve.drain().then_inc(norm.summand, 1)
                    elif kind == "norm":
                        norm.vector(dve, i, e[1], lambda k: vec("ln1_g_2" if e[1] == 0 else "ln2_g_2", k))
                    elif kind == "fu":
                        dve.wait_ge(silu_done, i * KF + e[1] + 1)
                        banks.filled(dve, e, i)
                        dve.tensor_tensor(hidden[:, e[1], :], side[:, e[1] % 2, :], core.ps(e)[:, :], ALU.mult)\
                           .then_inc(banks.done(e), 1)
                        dve.drain().then_inc(hidden_done, 1)
                        if e[1]:
                            f = e[1] - 1
                            rest(hidden[:, f, :], hidden_hi(f), hidden_round, i * KF + f + 1, hidden_split)

            with dve.Fori(0, LAYERS) as i:
                layer(i)
            dve.drain()
            for k in range(KD):
                dve.tensor_tensor(x[:, k, :], r32(x[:, k, :]), r32(x_hi[k]), ALU.add).then_inc(joined, 1)

        @block.gpsimd
        def _(pool):
            with pool.Fori(0, LAYERS) as i:
                for s in range(NS):
                    kind, h, n, j = soft[s]
                    if j:
                        continue
                    pool.wait_ge(recip_done, i * NS + s + 1)
                    w = near(n)[1] * P if kind == "na" else T
                    pool.tensor_tensor(p[:, s % NP, 0:w], p[:, s % NP, 0:w], recip[:, s:s + 1].broadcast_to([P, w]), ALU.mult)\
                        .then_inc(scaled, 1)


class Shared:
    pass


def build_program(nc, ins, out):
    ctx = ExitStack()
    with ctx:
        core = Core(nc, ctx, ins)
        a = Shared()
        with ExitStack() as mix_ctx:
            a.xm = core.sb("xm", [P, KD, T + CTX], mix_ctx)
            a.y = core.sb("y", [P, TT, D], mix_ctx)
            a.c = core.sb("c_in", [P, KD, 2], mix_ctx)
            a.skip = core.sb("skip", [P, HEADS], mix_ctx)
            with ExitStack() as scan_ctx:
                a.xtok = core.sb("xtok", [P, TT + CT, D], scan_ctx)
                a.btok = core.sb("btok", [P, TT + CT, GROUPS * STATE], scan_ctx)
                a.bc = core.sb("bc", [P, 2 * GROUPS, T], scan_ctx)
                a.dt = core.sb("dt", [P, TT + CT, 2 * HEADS], scan_ctx)
                a.dta = core.sb("dta", [P, TT + CT, 2 * HEADS], scan_ctx)
                with ExitStack() as c1:
                    front(core, c1, a)
                with ExitStack() as c2:
                    scan(core, c2, a)
            with ExitStack() as c3:
                mixer(core, c3, a)
        with ExitStack() as moe_ctx:
            b = Shared()
            b.xf_tok = core.sb("xf_tok", [P, TT, 2, D], moe_ctx)
            b.pick = core.sb("pick", [P, TT, EXPERTS * CAP], moe_ctx)
            b.put = core.sb("put", [P, EXPERTS // 2, T], moe_ctx)
            with ExitStack() as c4:
                router(core, c4, b)
            with ExitStack() as c5:
                experts(core, c5, b)
        x_hi = core.sb("x_hi", [P, 5, T])
        flat = core.ring[:, :, :].rearrange("p a b -> p (a b)")
        at = (PIECES + HALVES) * PIECE
        core.x_hi = [x_hi[:, k, :] for k in range(5)] + [flat[:, at + k * T:at + (k + 1) * T] for k in range(3)]
        with ExitStack() as c6:
            entry(core, c6)
        with ExitStack() as c7:
            layers(core, c7, out)



def _permuted_tokens():
    t = np.arange(T).reshape(ROWS, NBLK, QB)
    return t.transpose(1, 0, 2).reshape(-1)


def _rope(half):
    inv = np.exp((-np.log(np.float32(500000.0)) * np.arange(half, dtype=np.float32) / np.float32(half)).astype(np.float32))
    ang = _permuted_tokens().astype(np.float32)[None, :] * inv.astype(np.float32)[:, None]
    return np.cos(ang).astype(np.float32), np.sin(ang).astype(np.float32)


def _rope_tables(first, half, period):
    cos, sin, swap = np.ones((P, T), np.float32), np.zeros((P, T), np.float32), np.zeros((P, P), np.float32)
    c, s = _rope(half)
    for at in range(first, P, period):
        if at + 2 * half > P:
            break
        for j in range(half):
            lo, hi = at + j, at + half + j
            cos[lo] = cos[hi] = c[j]
            sin[lo] = sin[hi] = s[j]
            swap[hi, lo] = -1.0
            swap[lo, hi] = 1.0
    return cos, sin, swap


def _near_masks():
    out = np.full((3, ROWS, QB, 3, ROWS, QB), NEG, np.float32)
    for k, n in enumerate((0, 1, NBLK - 1)):
        for c in range(QB):
            w0 = min(max(QB * n + c - WIN // 2, 0), GRID - WIN)
            for j in range(3):
                for c2 in range(QB):
                    if w0 <= QB * (n - 1 + j) + c2 < w0 + WIN:
                        out[k, :, c, j, :, c2] = 0.0
    return out.reshape(3, P, 3 * P)


def _constants():
    lower = np.tril(np.ones((P, P), np.float32))
    dcos, dsin, dswap = _rope_tables(0, 8, 64)
    mcos, msin, mswap = _rope_tables(64, 16, 64)
    near = _near_masks()
    ones = np.ones((P, P), np.float32)
    parts = {
        "ident": np.eye(P), "ones": ones, "mean_d": ones / D,
        "tri_f": lower.T, "tri_b": lower, "mask_f": np.where(lower.T > 0, 0.0, NEG), "mask_b": np.where(lower > 0, 0.0, NEG),
        "eps6": ones[:, :1] * EPS, "eps5": ones[:, :1] * LN_EPS,
        "slot": np.tile(np.arange(1, CAP + 1)[None, :], (P, 1)),
    }
    second = {
        "dcos": dcos, "dsin": dsin, "mcos": mcos, "msin": msin, "dswap": dswap, "mswap": mswap,
        "mean_q": ones / QRANK, "mean_kv": ones / KVRANK, "mean_h": ones / P,
        "near0": near[0][:, P:], "near1": near[1], "near2": near[2][:, :2 * P],
    }
    return parts, second


def _pack(parts):
    at, where = 0, {}
    for name, a in parts.items():
        where[name] = (at, a.shape[1])
        at += a.shape[1]
    return where, at


_FIRST, _SECOND = _constants()
CON, NCON = _pack(_FIRST)
CON2, NCON2 = _pack(_SECOND)

_VECS = [("ada_b", 48), ("norm1_w", 8), ("norm2_w", 8), ("final_norm_w", 8), ("conv_w", 48), ("conv_b", 16),
         ("ssd_norm_w", 8), ("ln_in_g_2", 8), ("ln_in_b_2", 8)]
_LAYER = [("ln1_g_2", 8), ("ln1_b_2", 8), ("ln2_g_2", 8), ("ln2_b_2", 8), ("b_gate_2", 24), ("diff_subln_g_2", 1),
          ("mla_q_norm_g_2", 3), ("mla_kv_norm_g_2", 2), ("lam_init", 1), ("one_less", 1)]


def _places(columns):
    at, where = 0, {}
    for name, n in columns:
        where[name] = (at, n)
        at += n
    return where, at


VEC, NVEC = _places(_VECS)
LAYER, NLAYER = _places(_LAYER)


def lay_out(x):
    f = lambda n: np.ascontiguousarray(np.asarray(x[n]))
    cols = lambda v: np.ascontiguousarray(v.reshape(-1, P).T)
    g = {
        "xT": np.ascontiguousarray(f("x")[0].T), "ctxT": np.ascontiguousarray(f("ctx")[0].T),
        "cT": np.ascontiguousarray(np.stack([f("c")[0], f("c_ctx")], axis=1)),
        "ada_w": f("ada_w")[0], "w_in": f("w_in")[0], "w_pa": f("w_pa")[0], "w_pb": f("w_pb")[0], "w_o": f("w_o")[0],
        "wsT": np.ascontiguousarray(f("w_s")[0].transpose(0, 2, 1)),
        "rowsA": np.concatenate([f("dt_bias")[0].reshape(-1), f("a_log")[0].reshape(-1), f("d_skip")[0]]),
        "rowsB": np.concatenate([f("sgu_ln_w")[0], f("sgu_ln_b")[0], f("b_s")[0].reshape(-1)]),
    }
    for n in ("w_in_2", "w_out_2", "w_ffn_out_2"):
        g[n] = f(n)
    g["w_ffn_in_2"] = f("w_ffn_in_2").reshape(LAYERS, D, 2, KF, P).transpose(0, 1, 3, 2, 4).reshape(LAYERS, D, 2 * FF)
    g["w_branch_2"] = f("w_branch_2").reshape(LAYERS, 3 * BR, D)
    tiled = lambda w: w.reshape(LAYERS, -1, P, w.shape[2]).transpose(0, 2, 1, 3).reshape(LAYERS, P, -1)
    g["w_mla_2"] = np.concatenate([tiled(f("w_mla_qb_2")), tiled(f("w_mla_kvb_2"))], axis=2)
    rpb = f("na_rpb_2").reshape(LAYERS, -1)
    edge = np.zeros((LAYERS, RPB_PAD), np.float32)
    g["rpb"] = np.concatenate([edge, rpb, edge], axis=1)[:, ::-1]
    g["lam"] = f("diff_lambda_2").reshape(LAYERS, 256)
    lam_init = [0.8 - 0.6 * float(np.exp(-0.3 * l)) for l in range(LAYERS)]
    extra = {"lam_init": lam_init, "one_less": [1.0 - v for v in lam_init]}
    g["layer_vec"] = np.stack([np.concatenate(
        [np.full((P, 1), extra[n][l], np.float32) if n in extra else cols(f(n)[l]) for n, _ in _LAYER], axis=1)
        for l in range(LAYERS)])
    for n in ("router_w", "w_gate", "w_up", "w_down"):
        g[n] = f(n)[0]
    g["vec"] = np.concatenate([cols(f(n)) for n, _ in _VECS], axis=1)
    g["con"] = np.concatenate([np.asarray(v, np.float32) for v in _FIRST.values()], axis=1)
    g["con2"] = np.concatenate([np.asarray(v, np.float32) for v in _SECOND.values()], axis=1)
    return {k: np.ascontiguousarray(v, dtype=v.dtype) for k, v in g.items()}


def kernel(**inputs):
    import concourse.bacc as bacc
    from concourse.bass_utils import run_bass_kernel_spmd

    nc = bacc.Bacc("TRN2", target_bir_lowering=False, num_devices=1)
    arrays = {"in_" + n: a for n, a in lay_out(inputs).items()}
    ins = {n[3:]: nc.dram_tensor(n, list(a.shape), mybir.dt.from_np(a.dtype), kind="ExternalInput").ap()
           for n, a in arrays.items()}
    out = nc.dram_tensor("out", [D, T], F32, kind="ExternalOutput").ap()
    build_program(nc, ins, out)
    result = run_bass_kernel_spmd(nc, [arrays], core_ids=[0])
    y = np.empty((1, T, D), np.float32)
    y[0, _permuted_tokens()] = result.results[0]["out"].T
    return y
```

```python
from contextlib import ExitStack

import numpy as np

import concourse.bass as bass
from concourse import mybir

F32 = mybir.dt.float32
ALU = mybir.AluOpType
ACT = mybir.ActivationFunctionType
AX = mybir.AxisListType

P = 128
D = 1024
KD = D // P
T = 512
TT = T // P
CTX = 256
CT = CTX // P
SLAB = 4352
SLOTS = 3
RAW, HIGH = 9, 4
PIECE, PIECES, HALVES = 2304, 3, 2
BANKS = 8
NEG = -1.0e30

HEADS, HDIM, GROUPS, STATE = 16, 64, 4, 128
HPG = HEADS // GROUPS
XBC = D + 2 * GROUPS * STATE
NSCAN = XBC + 2 * HEADS
EPS = 1e-6
EXPERTS, CAP = 16, 64

LAYERS = 2
GRID = 64
ROWS = T // GRID
QB = 16
NBLK = GRID // QB
WIN = 16
RPB_W = 2 * WIN - 1
RPB_H = 15
RUN = (ROWS - 1) * RPB_W + 3 * QB
RPB_PAD = 16
NA_HEADS, DF_HEADS, MLA_HEADS = 8, 4, 8
BR = 512
FF = 2816
KF = FF // P
QRANK, KVRANK, ROPE_D = 384, 256, 32
ALPHA = 4.0 ** 0.25
SCALE = {"df": 64 ** -0.5, "ml": 96 ** -0.5}
LN_EPS = 1e-5


class Ring:

    def __init__(self, full, free, step, given=0):
        self.given = given
        self.full, self.free, self.step, self.n = full, free, step, len(full)
        self.base, self.pos = [0] * self.n, 0
        self.reps = 0

    def reached(self):
        return [b + self.reps * c for b, c in zip(self.base, self.count)]

    def part(self, first, last):
        ring = Ring(self.full[first:last], self.free[first:last], self.step, self.given)
        ring.base = (self.reached() if self.reps else self.base)[first:last]
        return ring

    def joined(self, *parts):
        self.base = [b for ring in parts for b in ring.reached()]
        self.pos, self.reps = 0, 0

    def begin(self, keys, reps=1):
        if self.reps:
            self.base = [b + self.reps * c for b, c in zip(self.base, self.count)]
            self.pos = (self.pos + len(self.use)) % self.n
        self.reps, self.count, self.use = reps, [0] * self.n, {}
        for k, key in enumerate(keys):
            slot = (self.pos + k) % self.n
            assert key not in self.use, key
            self.use[key] = (slot, self.base[slot] + self.count[slot])
            self.count[slot] += 1

    def slot(self, key):
        return self.use[key][0]

    def filled(self, eng, key, i=0):
        slot, before = self.use[key]
        eng.wait_ge(self.full[slot], i * (self.step * self.count[slot]) + self.step * (before + 1))

    def filled_too(self, eng, key, later, i=0):
        if self.use[key][0] != self.use[later][0]:
            self.filled(eng, key, i)

    def vacant(self, eng, key, i=0):
        slot, before = self.use[key]
        if before + self.given:
            eng.wait_ge(self.free[slot], i * self.count[slot] + before + self.given)

    def put(self, key):
        return self.full[self.use[key][0]]

    def done(self, key):
        return self.free[self.use[key][0]]


TWINS = {}


def r32(ap):
    return bass.AP(tensor=TWINS[ap.tensor.name], offset=ap.offset, ap=[list(d) for d in ap.ap])


def bcast_rows(v, n):
    return v.rearrange("(a n) -> a n", a=1).broadcast_to([P, n])


def w_tiles(w, r0, rows, c0, cols):
    return w[r0:r0 + rows, c0:c0 + cols].rearrange("(k p) n -> p k n", p=P)


class Core:

    def __init__(self, nc, ctx, ins):
        self.nc, self.ctx, self.ins = nc, ctx, ins
        self.stage = ""
        self.ring = self.sb("ring", [P, SLOTS, SLAB])
        self.slabs = Ring([self.sem(f"slab_full{i}") for i in range(SLOTS)],
                          [self.sem(f"slab_read{i}") for i in range(SLOTS)], 16)
        self.bank = [ctx.enter_context(nc.psum_tensor(f"bank{i}", [P, 512], F32)) for i in range(BANKS)]
        self.banks = Ring([self.sem(f"bank_full{i}") for i in range(BANKS)],
                          [self.sem(f"bank_read{i}") for i in range(BANKS)], 1)
        self.pieces = Ring([self.sem(f"piece_full{i}") for i in range(RAW)],
                           [self.sem(f"piece_read{i}") for i in range(RAW)], 16, given=1)
        self.halves = Ring([self.sem(f"split_done{i}") for i in range(HIGH)],
                           [self.sem(f"split_read{i}") for i in range(HIGH)], 1, given=1)
        self.norm_sems = [self.sem("norm_" + n) for n in
                          ("summed", "centred", "squared", "square_read", "root", "scaled", "rounded", "ready")]
        self.vec = self.sb("vec", [P, NVEC])
        self.con = self.sb("con", [P, NCON])
        self.x = self.sb("x", [P, KD, T])
        self.mod = self.sb("mod", [P, 48, 2])

    def sb(self, name, shape, ctx=None):
        with self.nc.sbuf_tensor(self.stage + name, shape, F32) as buf:
            pass
        TWINS[buf.name] = (ctx or self.ctx).enter_context(
            self.nc.sbuf_tensor(self.stage + name + "_r", shape, mybir.dt.float32r))
        return buf

    def sem(self, name, ctx=None):
        return (ctx or self.ctx).enter_context(self.nc.semaphore(self.stage + name))

    def v(self, name, i=0, n=1):
        a = VEC[name][0] + i
        return self.vec[:, a:a + n]

    def c(self, name, rows=P):
        a, n = CON[name][:2]
        return self.con[0:rows, a:a + n]

    def ps(self, key):
        return self.bank[self.banks.slot(key)]

    def slab(self, key, k, n):
        return self.ring[:, self.slabs.slot(key), 0:k * n].rearrange("p (k n) -> p k n", k=k)


def load_slab(core, sp, key, src, i=0, at=0):
    _, k, n = src.shape
    core.slabs.vacant(sp, key, i)
    dst = core.ring[:, core.slabs.slot(key), at:at + k * n].rearrange("p (k n) -> p k n", k=k)
    sp.dma_start(dst, src).then_inc(core.slabs.put(key), 16)


def product(pe, out, lhs, rhs, read=None):
    n = len(lhs)
    for k in range(n):
        last = pe.matmul(out, lhs[k], rhs[k], start=k == 0, stop=k == n - 1)
        if k == 0 and read is not None:
            last.then_inc(read, 1)
    return last


def front(core, ctx, a):
    core.stage = "front_"
    nc, I = core.nc, core.ins
    TA = T + CTX
    NM = XBC // P
    sem = lambda n: core.sem(n, ctx)
    pad = core.sb("pad", [P, 2, TA + 3], ctx)
    conv = core.sb("conv", [P, 2, TA + 1], ctx)
    act_x = core.sb("act_x", [P, 2, TA], ctx)
    sq = core.sb("sq", [P, 2, TA], ctx)
    rstd = core.sb("rstd", [P, TA], ctx)
    scale1 = core.sb("scale1", [P, KD, 2], ctx)
    dtw = core.sb("dtw", [P, 6, CT + TT, 2 * HEADS], ctx)
    raw, mag, ex, one_ex, ln_ex, rest = (dtw[:, k] for k in range(6))
    rows = core.sb("rowsA", [P, 5 * HEADS], ctx)
    dt_bias, a_neg = rows[:, 0:2 * HEADS], rows[:, 2 * HEADS:4 * HEADS]
    const_in, x_in, pad_zero = sem("const_in"), sem("x_in"), sem("pad_zero")
    c_silu = sem("c_silu")
    sq_done, sq_used, root_done = sem("sq_done"), sem("sq_used"), sem("root_done")
    scaled, xm_done = sem("scaled"), sem("xm_done")
    dt_dve, dt_act = sem("dt_dve"), sem("dt_act")
    pad_done, conv_done, act_done = sem("pad_done"), sem("conv_done"), sem("act_done")

    ada = [("ada", s) for s in range(4)]
    xbc = [("xbc", s) for s in range(4)]
    core.slabs.begin(ada + ["dtw"] + xbc)
    keys = ["rms_l", "rms_c"] + ada + ["dt"]
    for m in range(NM):
        keys += [("xl", m)] + ([("xc", m)] if m < 12 else [])
        if m >= 1 and m - 1 < 12:
            keys += [("tl", m - 1), ("tc", m - 1)]
    core.banks.begin(keys)

    with nc.Block() as block:
        @block.sync
        def _(sp):
            sp.dma_start(core.con[:, :], I["con"]).then_inc(const_in, 16)
            sp.dma_start(core.vec[:, :], I["vec"]).then_inc(const_in, 16)
            sp.dma_start(a.c[:, :, :], I["cT"].rearrange("(k p) n -> p k n", p=P)).then_inc(const_in, 16)
            sp.dma_start(a.xm[:, :, 0:T], I["xT"].rearrange("(k p) n -> p k n", p=P)).then_inc(x_in, 16)
            sp.dma_start(a.xm[:, :, T:TA], I["ctxT"].rearrange("(k p) n -> p k n", p=P)).then_inc(x_in, 16)
            sp.dma_start(rows[:, :], bcast_rows(I["rowsA"], 5 * HEADS)).then_inc(const_in, 16)
            for s in range(4):
                load_slab(core, sp, ("ada", s), w_tiles(I["ada_w"], 0, D, 512 * s, 512))
            load_slab(core, sp, "dtw", w_tiles(I["w_in"], 0, D, XBC, 2 * HEADS))
            for s in range(4):
                load_slab(core, sp, ("xbc", s), w_tiles(I["w_in"], 0, D, 512 * s, 512))

        @block.tensor
        def _(pe):
            pe.wait_ge(const_in, 64)
            core.banks.vacant(pe, "rms_l")
            core.banks.vacant(pe, "rms_c")
            for k in range(KD):
                pe.wait_ge(sq_done, k + 1)
                last = pe.matmul(core.ps("rms_l")[:, :], core.c("mean_d"), sq[:, k % 2, 0:T],
                                 start=k == 0, stop=k == KD - 1)
                if k == KD - 1:
                    last.then_inc(core.banks.put("rms_l"), 1)
                last = pe.matmul(core.ps("rms_c")[:, 0:CTX], core.c("mean_d"), sq[:, k % 2, T:TA],
                                 start=k == 0, stop=k == KD - 1)
                if k < KD - 1:
                    last.then_inc(sq_used, 1)
            last.then_inc(core.banks.put("rms_c"), 1)
            pe.wait_ge(c_silu, 1)
            for s in range(4):
                core.slabs.filled(pe, ("ada", s))
                core.banks.vacant(pe, ("ada", s))
                w = core.slab(("ada", s), KD, 512)
                for m in range(4):
                    last = product(pe, core.ps(("ada", s))[:, 2 * m:2 * m + 2],
                                   [w[:, k, m * P:(m + 1) * P] for k in range(KD)],
                                   [a.c[:, k, :] for k in range(KD)],
                                   core.slabs.done(("ada", s - 1)) if s and m == 0 else None)
                last.then_inc(core.banks.put(("ada", s)), 1)
            pe.wait_ge(xm_done, 2 * KD)
            core.slabs.filled(pe, "dtw")
            core.banks.vacant(pe, "dt")
            w = core.slab("dtw", KD, 2 * HEADS)
            for t in range(TT + CT):
                last = product(pe, core.ps("dt")[:, t * 32:t * 32 + 32],
                               [a.xm[:, k, t * P:(t + 1) * P] for k in range(KD)],
                               [w[:, k, :] for k in range(KD)],
                               core.slabs.done(("ada", 3)) if t == 0 else None)
            last.then_inc(core.banks.put("dt"), 1)

            def turn(m):
                pe.wait_ge(act_done, m + 1)
                src = act_x[:, m % 2]
                for name, t0, n in (("tl", 0, TT), ("tc", TT, CT)):
                    core.banks.vacant(pe, (name, m))
                    for t in range(n):
                        last = pe.transpose(core.ps((name, m))[:, t * P:(t + 1) * P],
                                            src[:, (t0 + t) * P:(t0 + t + 1) * P], core.c("ident"))
                    last.then_inc(core.banks.put((name, m)), 1)

            for m in range(NM):
                read = None
                if m % 4 == 0:
                    core.slabs.filled(pe, ("xbc", m // 4))
                    read = core.slabs.done(("xbc", m // 4 - 1) if m else "dtw")
                w = core.slab(("xbc", m // 4), KD, 512)
                cut = [w[:, k, (m % 4) * P:(m % 4 + 1) * P] for k in range(KD)]
                core.banks.vacant(pe, ("xl", m))
                last = product(pe, core.ps(("xl", m))[:, :], cut, [a.xm[:, k, 0:T] for k in range(KD)], read)
                last.then_inc(core.banks.put(("xl", m)), 1)
                if m < 12:
                    core.banks.vacant(pe, ("xc", m))
                    last = product(pe, core.ps(("xc", m))[:, 0:CTX], cut, [a.xm[:, k, T:TA] for k in range(KD)])
                    last.then_inc(core.banks.put(("xc", m)), 1)
                if m >= 1 and m - 1 < 12:
                    turn(m - 1)
            pe.drain().then_inc(core.slabs.done(("xbc", 3)), 1)

        @block.scalar
        def _(act):
            act.wait_ge(x_in, 32)
            for k in range(KD):
                if k >= 2:
                    act.wait_ge(sq_used, k - 1)
                act.activation(sq[:, k % 2, :], a.xm[:, k, :], ACT.Square).then_inc(sq_done, 1)
            act.wait_ge(const_in, 64)
            core.banks.filled(act, "rms_l")
            core.banks.filled(act, "rms_c")
            act.activation(rstd[:, 0:T], core.ps("rms_l")[:, :], ACT.Sqrt,
                           bias=core.c("eps6")).then_inc(core.banks.done("rms_l"), 1)
            act.activation(rstd[:, T:TA], core.ps("rms_c")[:, 0:CTX], ACT.Sqrt,
                           bias=core.c("eps6")).then_inc(core.banks.done("rms_c"), 1)
            act.drain().then_inc(root_done, 1)
            act.activation(a.c[:, :, :], a.c[:, :, :], ACT.Silu).then_inc(c_silu, 1)
            for k in range(KD):
                for j, (lo, hi) in enumerate(((0, T), (T, TA))):
                    act.wait_ge(scaled, 2 * k + j + 1)
                    act.activation(a.xm[:, k, lo:hi], a.xm[:, k, lo:hi], ACT.Identity,
                                   bias=core.mod[:, k, j:j + 1]).then_inc(xm_done, 1)
            act.wait_ge(dt_dve, 1)
            act.activation(mag, raw, ACT.Abs).then_inc(dt_act, 1)
            act.wait_ge(dt_act, 1)
            act.activation(ex, mag, ACT.Exp, scale=-1.0)
            act.activation(a_neg, a_neg, ACT.Exp).then_inc(dt_act, 1)
            act.wait_ge(dt_dve, 2)
            act.activation(ln_ex, one_ex, ACT.Ln).then_inc(dt_act, 1)

            def silu(m):
                act.wait_ge(conv_done, m + 1)
                if m >= 12:
                    act.activation(a.bc[:, m - 8, :], conv[:, m % 2, 0:T], ACT.Silu, bias=core.v("conv_b", m))\
                       .then_inc(act_done, 1)
                    return
                if m >= 2:
                    core.banks.filled(act, ("tc", m - 2))
                act.activation(act_x[:, m % 2, 0:T], conv[:, m % 2, 0:T], ACT.Silu, bias=core.v("conv_b", m))
                act.activation(act_x[:, m % 2, T:TA], conv[:, m % 2, T + 1:TA + 1], ACT.Silu,
                               bias=core.v("conv_b", m))
                act.drain().then_inc(act_done, 1)
                if m >= 8:
                    act.activation(a.bc[:, m - 8, :], act_x[:, m % 2, 0:T], ACT.Identity)

            act.wait_ge(pad_zero, 1)
            for m in range(NM):
                core.banks.filled(act, ("xl", m))
                if m >= 2:
                    act.wait_ge(conv_done, m - 1)
                act.activation(pad[:, m % 2, 1:T + 1], core.ps(("xl", m))[:, :], ACT.Identity)\
                   .then_inc(core.banks.done(("xl", m)), 1)
                if m < 12:
                    core.banks.filled(act, ("xc", m))
                    act.activation(pad[:, m % 2, T + 2:TA + 2], core.ps(("xc", m))[:, 0:CTX], ACT.Identity)\
                       .then_inc(core.banks.done(("xc", m)), 1)
                act.drain().then_inc(pad_done, 1)
                if m >= 1:
                    silu(m - 1)
            silu(NM - 1)

        @block.vector
        def _(dve):
            dve.wait_ge(const_in, 64)
            for s in range(4):
                core.banks.filled(dve, ("ada", s))
                bias = core.v("ada_b", 4 * s, 4).unsqueeze(2).broadcast_to([P, 4, 2])
                dve.tensor_tensor(core.mod[:, 4 * s:4 * s + 4, :],
                                  core.ps(("ada", s))[:, 0:8].rearrange("p (m j) -> p m j", j=2), bias,
                                  ALU.add).then_inc(core.banks.done(("ada", s)), 1)
            dve.drain()
            dve.tensor_scalar(scale1[:, :, :], core.mod[:, KD:2 * KD, :], 1.0, None, ALU.add)
            dve.drain()
            dve.tensor_tensor(scale1[:, :, :], scale1[:, :, :],
                              core.v("norm1_w", 0, KD).unsqueeze(2).broadcast_to([P, KD, 2]), ALU.mult)
            dve.wait_ge(root_done, 1)
            dve.reciprocal(rstd[:, :], rstd[:, :])
            dve.drain()
            for k in range(KD):
                for j, (lo, hi) in enumerate(((0, T), (T, TA))):
                    dve.scalar_tensor_tensor(out=a.xm[:, k, lo:hi], in0=a.xm[:, k, lo:hi],
                                             scalar=scale1[:, k, j:j + 1], in1=rstd[:, lo:hi],
                                             op0=ALU.mult, op1=ALU.mult).then_inc(scaled, 1)
            core.banks.filled(dve, "dt")
            bias = dt_bias.unsqueeze(1).broadcast_to([P, CT + TT, 2 * HEADS])
            dve.tensor_tensor(raw, core.ps("dt")[:, 0:192].rearrange("p (t h) -> p t h", h=2 * HEADS), bias,
                              ALU.add).then_inc(core.banks.done("dt"), 1)
            dve.drain().then_inc(dt_dve, 1)
            dve.wait_ge(dt_act, 2)
            dve.tensor_scalar(one_ex, ex, 1.0, None, ALU.add)
            dve.drain().then_inc(dt_dve, 1)
            dve.tensor_scalar(rest, one_ex, -1.0, None, ALU.add)
            dve.drain()
            dve.tensor_tensor(rest, ex, rest, ALU.subtract)
            dve.reciprocal(mag, one_ex)
            dve.drain()
            dve.tensor_tensor(rest, rest, mag, ALU.mult)
            dve.wait_ge(dt_act, 3)
            dve.drain()
            dve.tensor_tensor(rest, rest, ln_ex, ALU.add)
            dve.drain()
            dve.scalar_tensor_tensor(out=a.dt[:, :, :], in0=raw, scalar=0.0, in1=rest, op0=ALU.max, op1=ALU.add)
            dve.drain()
            dve.scalar_tensor_tensor(out=a.dta[:, :, :], in0=a.dt[:, :, :], scalar=-1.0,
                                     in1=a_neg.unsqueeze(1).broadcast_to([P, CT + TT, 2 * HEADS]),
                                     op0=ALU.mult, op1=ALU.mult)

            def tokens(m):
                dst, col = (a.xtok, m) if m < 8 else (a.btok, m - 8)
                for name, t0, n in (("tl", 0, TT), ("tc", TT, CT)):
                    core.banks.filled(dve, (name, m))
                    last = dve.tensor_copy(dst[:, t0:t0 + n, col * P:(col + 1) * P],
                                           core.ps((name, m))[:, 0:n * P].rearrange("p (t f) -> p t f", f=P))
                    last.then_inc(core.banks.done((name, m)), 1)

            for m in range(NM):
                dve.wait_ge(pad_done, m + 1)
                if m >= 2:
                    dve.wait_ge(act_done, m - 1)
                n = TA + 1 if m < 12 else T
                src, dst = pad[:, m % 2], conv[:, m % 2, 0:n]
                dve.tensor_scalar(dst, src[:, 0:n], core.v("conv_w", m), None, ALU.mult)
                dve.drain()
                for tap in (1, 2):
                    dve.scalar_tensor_tensor(out=dst, in0=src[:, tap:n + tap], scalar=core.v("conv_w", NM * tap + m),
                                             in1=dst, op0=ALU.mult, op1=ALU.add)
                    if tap == 1:
                        dve.drain()
                dve.drain().then_inc(conv_done, 1)
                if m >= 2 and m - 2 < 12:
                    tokens(m - 2)

        @block.gpsimd
        def _(pool):
            pool.memset(pad[:, :, :], 0.0).then_inc(pad_zero, 1)
            pool.wait_ge(const_in, 64)
            pool.tensor_copy(a.skip[:, :], rows[:, 4 * HEADS:5 * HEADS])


def scan(core, ctx, a):
    core.stage = "scan_"
    nc = core.nc
    sem = lambda n: core.sem(n, ctx)
    NT, H2 = TT + CT, 2 * HEADS
    acum = core.sb("acum", [P, NT, H2], ctx)
    grow = core.sb("grow", [P, NT, H2], ctx)
    total = core.sb("total", [P, NT, H2], ctx)
    toend = core.sb("toend", [P, NT, H2], ctx)
    spare = core.x[:, :, :].rearrange("p m t -> p (m t)")
    cb = spare[:, 0:TT * GROUPS * P].rearrange("p (t n) -> p t n", t=TT)
    xdt, xend = spare[:, 2 * D:3 * D], spare[:, 3 * D:4 * D]
    h = core.sb("h", [P, 2, D], ctx)
    NSEG = 6
    seg = core.sb("seg", [P, NSEG, HPG * P], ctx)
    part = core.sb("part", [P, D], ctx)
    acum_done, exp_done, cb_done, toend_done = sem("acum_done"), sem("exp_done"), sem("cb_done"), sem("toend_done")
    seg_done, decay_done, mt_done, mt_used = sem("seg_done"), sem("decay_done"), sem("mt_done"), sem("mt_used")
    xdt_done, xend_done = sem("xdt_done"), sem("xend_done")
    h_done, part_done, part_used = sem("h_done"), sem("part_done"), sem("part_used")

    ctx_steps = [(d, TT + (k if d == 0 else CT - 1 - k), False) for k in range(CT) for d in (0, 1)]
    lat_steps = [(d, k if d == 0 else TT - 1 - k, True) for k in range(TT) for d in (0, 1)]
    steps = ctx_steps + lat_steps
    outs = [u for u, s in enumerate(steps) if s[2]]
    feeds = [u for u, s in enumerate(steps) if u < len(steps) - 2]
    G = range(GROUPS)
    keys = ["sums"] + [("cb", t) for t in range(TT)]
    first = outs[0]

    def seg_keys(u):
        return [("seg", u, g) for g in G]

    keys += [k for u in range(first) for k in (("st", u, 0), ("st", u, 1))] + seg_keys(first)
    for u in outs:
        if u + 1 in outs:
            keys += seg_keys(u + 1)
        keys += [("off", u, 0), ("off", u, 1)]
        if u in feeds:
            keys += [("st", u, 0), ("st", u, 1)]
        keys += [("diag", u, 0), ("diag", u, 1)]
    core.slabs.begin(MIXER_SLABS)
    core.banks.begin(keys)
    order = {u: n for n, u in enumerate(outs)}
    feed_no = {u: n for n, u in enumerate(feeds)}
    per_head = lambda ap: ap.unsqueeze(2).broadcast_to([P, HEADS, HDIM])
    by_head = lambda ap: ap.rearrange("p (h f) -> p h f", f=HDIM)

    with nc.Block() as block:
        @block.sync
        def _(sp):
            for key in MIXER_SLABS[:SLOTS]:
                load_slab(core, sp, key, mixer_slabs(core)[key])

        @block.tensor
        def _(pe):
            core.banks.vacant(pe, "sums")
            sums = core.ps("sums")
            for d, tri in enumerate(("tri_f", "tri_b")):
                pe.matmul(sums[:, d * 96:d * 96 + 96], core.c(tri), a.dta[:, :, d * HEADS:(d + 1) * HEADS],
                          start=True, stop=True)
            pe.matmul(sums[:, 192:384], core.c("ones"), a.dta[:, :, :], start=True, stop=True)\
              .then_inc(core.banks.put("sums"), 1)
            for t in range(TT):
                core.banks.vacant(pe, ("cb", t))
                for g in G:
                    last = pe.matmul(core.ps(("cb", t))[:, g * P:(g + 1) * P], a.bc[:, g, t * P:(t + 1) * P],
                                     a.bc[:, GROUPS + g, t * P:(t + 1) * P], start=True, stop=True)
                last.then_inc(core.banks.put(("cb", t)), 1)

            def state(u):
                t = steps[u][1]
                pe.wait_ge(xend_done, feed_no[u] + 1)
                for half in (0, 1):
                    core.banks.vacant(pe, ("st", u, half))
                    for g in (2 * half, 2 * half + 1):
                        last = pe.matmul(core.ps(("st", u, half))[:, (g % 2) * 256:(g % 2) * 256 + 256],
                                         a.btok[:, t, g * P:(g + 1) * P], xend[:, g * 256:(g + 1) * 256],
                                         start=True, stop=True)
                    last.then_inc(core.banks.put(("st", u, half)), 1)

            def sums_of(u):
                d, t, _ = steps[u]
                for g in G:
                    core.banks.vacant(pe, ("seg", u, g))
                    for r in range(HPG):
                        col = d * HEADS + g * HPG + r
                        last = pe.matmul(core.ps(("seg", u, g))[:, r * P:(r + 1) * P],
                                         a.dta[:, t, col:col + 1].broadcast_to([P, P]),
                                         core.c("tri_b" if d else "tri_f"), start=True, stop=True)
                    last.then_inc(core.banks.put(("seg", u, g)), 1)

            for u in range(first):
                state(u)
            sums_of(first)
            for u in outs:
                d, t, _ = steps[u]
                if u + 1 in outs:
                    sums_of(u + 1)
                pe.wait_ge(h_done, u - 1)
                for half in (0, 1):
                    core.banks.vacant(pe, ("off", u, half))
                    for g in (2 * half, 2 * half + 1):
                        last = pe.matmul(core.ps(("off", u, half))[:, (g % 2) * 256:(g % 2) * 256 + 256],
                                         a.bc[:, GROUPS + g, t * P:(t + 1) * P], h[:, d, g * 256:(g + 1) * 256],
                                         start=True, stop=True)
                    last.then_inc(core.banks.put(("off", u, half)), 1)
                if u in feeds:
                    state(u)
                pe.wait_ge(xdt_done, order[u] + 1)
                for half in (0, 1):
                    core.banks.vacant(pe, ("diag", u, half))
                    for g in (2 * half, 2 * half + 1):
                        n = order[u] * GROUPS + g
                        pe.wait_ge(mt_done, n + 1)
                        for r in range(HPG):
                            hd = g * HPG + r
                            last = pe.matmul(core.ps(("diag", u, half))[:, (hd % 8) * HDIM:(hd % 8 + 1) * HDIM],
                                             seg[:, n % NSEG, r * P:(r + 1) * P], xdt[:, hd * HDIM:(hd + 1) * HDIM],
                                             start=True, stop=True)
                            if r == HPG - 1 and g % 2 == 0:
                                last.then_inc(mt_used, 1)
                    last.then_inc(core.banks.put(("diag", u, half)), 1)

        @block.scalar
        def _(act):
            act.wait_ge(acum_done, 1)
            act.activation(grow[:, :, :], acum[:, :, :], ACT.Exp)
            act.activation(total[:, :, :], total[:, :, :], ACT.Exp)
            act.activation(toend[:, :, :], toend[:, :, :], ACT.Exp)
            act.drain().then_inc(exp_done, 1)
            for t in range(TT):
                core.banks.filled(act, ("cb", t))
                act.activation(cb[:, t, :], core.ps(("cb", t))[:, :], ACT.Identity)\
                   .then_inc(core.banks.done(("cb", t)), 1)
            act.drain().then_inc(cb_done, 1)
            for n in range(len(outs) * GROUPS):
                act.wait_ge(seg_done, n + 1)
                act.activation(seg[:, n % NSEG, :], seg[:, n % NSEG, :], ACT.Exp).then_inc(decay_done, 1)

        @block.vector
        def _(dve):
            core.banks.filled(dve, "sums")
            sums = core.ps("sums")
            for d in (0, 1):
                dve.tensor_copy(acum[:, :, d * HEADS:(d + 1) * HEADS],
                                sums[:, d * 96:d * 96 + 96].rearrange("p (t h) -> p t h", h=HEADS))
            dve.tensor_copy(total[:, :, :], sums[:, 192:384].rearrange("p (t h) -> p t h", h=H2))\
               .then_inc(core.banks.done("sums"), 1)
            dve.drain()
            dve.tensor_tensor(toend[:, :, :], total[:, :, :], acum[:, :, :], ALU.subtract)
            dve.drain().then_inc(acum_done, 1)
            dve.wait_ge(exp_done, 1)
            dve.tensor_tensor(toend[:, :, :], toend[:, :, :], a.dt[:, :, :], ALU.mult)
            dve.drain().then_inc(toend_done, 1)

            def carry(u):
                d, t, _ = steps[u]
                if u >= 2:
                    if u in outs:
                        core.banks.filled(dve, ("off", u, 1))
                    dve.tensor_tensor(by_head(h[:, d, :]), by_head(h[:, d, :]),
                                      per_head(total[:, t, d * HEADS:(d + 1) * HEADS]), ALU.mult)
                    dve.drain()
                for half in (0, 1):
                    core.banks.filled(dve, ("st", u, half))
                    dst, src = h[:, d, half * 512:half * 512 + 512], core.ps(("st", u, half))[:, :]
                    last = dve.tensor_tensor(dst, dst, src, ALU.add) if u >= 2 else dve.tensor_copy(dst, src)
                    last.then_inc(core.banks.done(("st", u, half)), 1)
                dve.drain().then_inc(h_done, 1)

            def segments(u):
                d, t, _ = steps[u]
                for g in G:
                    n = order[u] * GROUPS + g
                    core.banks.filled(dve, ("seg", u, g))
                    if n >= NSEG:
                        old = n - NSEG
                        if old % 2 == 0:
                            dve.wait_ge(mt_used, old // 2 + 1)
                        else:
                            core.banks.filled(dve, ("diag", outs[old // GROUPS], (old % GROUPS) // 2))
                    for r in range(HPG):
                        col = d * HEADS + g * HPG + r
                        last = dve.scalar_tensor_tensor(
                            out=seg[:, n % NSEG, r * P:(r + 1) * P], in0=core.ps(("seg", u, g))[:, r * P:(r + 1) * P],
                            scalar=acum[:, t, col:col + 1], in1=core.c("mask_b" if d else "mask_f"),
                            op0=ALU.subtract, op1=ALU.add)
                    last.then_inc(core.banks.done(("seg", u, g)), 1)
                    dve.drain().then_inc(seg_done, 1)

            def scaled_x(u):
                d, t, _ = steps[u]
                if order[u]:
                    core.banks.filled(dve, ("diag", u - 1, 1))
                dve.tensor_tensor(by_head(xdt[:, :]), by_head(a.xtok[:, t, :]),
                                  per_head(a.dt[:, t, d * HEADS:(d + 1) * HEADS]), ALU.mult).then_inc(xdt_done, 1)

            for u in range(first):
                carry(u)
            segments(first)
            for u in outs:
                d, t, _ = steps[u]
                scaled_x(u)
                if u in feeds:
                    carry(u)
                if u + 1 in outs:
                    segments(u + 1)
                if order[u]:
                    dve.wait_ge(part_used, order[u])
                for half in (0, 1):
                    lo = half * 512
                    core.banks.filled(dve, ("off", u, half))
                    dve.tensor_tensor(by_head(part[:, :])[:, 8 * half:8 * half + 8],
                                      by_head(core.ps(("off", u, half))[:, :]),
                                      per_head(grow[:, t, d * HEADS:(d + 1) * HEADS])[:, 8 * half:8 * half + 8],
                                      ALU.mult).then_inc(core.banks.done(("off", u, half)), 1)
                    core.banks.filled(dve, ("diag", u, half))
                    dve.drain()
                    dve.tensor_tensor(part[:, lo:lo + 512], part[:, lo:lo + 512], core.ps(("diag", u, half))[:, :],
                                      ALU.add).then_inc(core.banks.done(("diag", u, half)), 1)
                dve.drain().then_inc(part_done, 1)

        @block.gpsimd
        def _(pool):
            def to_end(u):
                d, t, _ = steps[u]
                n = feed_no[u]
                if n:
                    core.banks.filled(pool, ("st", feeds[n - 1], 1))
                pool.tensor_tensor(by_head(xend[:, :]), by_head(a.xtok[:, t, :]),
                                   per_head(toend[:, t, d * HEADS:(d + 1) * HEADS]), ALU.mult).then_inc(xend_done, 1)

            def decays(u):
                t = steps[u][1]
                for g in G:
                    n = order[u] * GROUPS + g
                    pool.wait_ge(decay_done, n + 1)
                    cbg = cb[:, t, g * P:(g + 1) * P].unsqueeze(1).broadcast_to([P, HPG, P])
                    m = seg[:, n % NSEG, :].rearrange("p (r i) -> p r i", i=P)
                    pool.tensor_tensor(m, m, cbg, ALU.mult).then_inc(mt_done, 1)

            def add_part(u):
                t = steps[u][1]
                pool.wait_ge(part_done, order[u] + 1)
                pool.tensor_tensor(a.y[:, t, :], a.y[:, t, :], part[:, :], ALU.add).then_inc(part_used, 1)

            pool.wait_ge(toend_done, 1)
            for u in range(first):
                to_end(u)
            for t in range(TT):
                pool.tensor_tensor(by_head(a.y[:, t, :]), by_head(a.xtok[:, t, :]), per_head(a.skip[:, :]), ALU.mult)
            pool.drain()
            pool.wait_ge(cb_done, 1)
            for u in outs:
                t = steps[u][1]
                if u in feeds:
                    to_end(u)
                decays(u)
                if order[u]:
                    add_part(u - 1)
            add_part(outs[-1])


MERGE_SLABS = [(n, hh) for hh in (0, 1) for n in ("ga", "pa", "gb", "pb")]
MIXER_SLABS = [("z", 0), ("z", 1), ("v", 0), ("v", 1), ("u", 0), ("u", 1)] + [("ada", s) for s in range(4, 12)] \
    + MERGE_SLABS + [("wo", 0), ("wo", 1)]


def mixer_slabs(core):
    I = core.ins
    Z0, V0, U0 = NSCAN, NSCAN + 2 * D, NSCAN + D
    GA, GB = NSCAN + 3 * D, NSCAN + 4 * D
    source = {("z", s): w_tiles(I["w_in"], 0, D, Z0 + 512 * s, 512) for s in (0, 1)}
    source |= {("v", s): w_tiles(I["w_in"], 0, D, V0 + 512 * s, 512) for s in (0, 1)}
    source |= {("u", s): w_tiles(I["w_in"], 0, D, U0 + 512 * s, 512) for s in (0, 1)}
    source |= {("ada", s): w_tiles(I["ada_w"], 0, D, 512 * s, 512) for s in range(4, 12)}
    source |= {("ga", s): w_tiles(I["w_in"], 0, D, GA + 512 * s, 512) for s in (0, 1)}
    source |= {("gb", s): w_tiles(I["w_in"], 0, D, GB + 512 * s, 512) for s in (0, 1)}
    source |= {("pa", s): w_tiles(I["w_pa"], 0, D, 512 * s, 512) for s in (0, 1)}
    source |= {("pb", s): w_tiles(I["w_pb"], 0, D, 512 * s, 512) for s in (0, 1)}
    source |= {("wo", s): w_tiles(I["w_o"], 0, D, 512 * s, 512) for s in (0, 1)}
    return source


def mixer(core, ctx, a):
    core.stage = "mixer_"
    nc, I = core.nc, core.ins
    sem = lambda n: core.sem(n, ctx)
    v = core.sb("v", [P, TT, D], ctx)
    u = core.sb("u", [P, KD, T], ctx)
    yt = core.sb("yt", [P, KD, T], ctx)
    ws = core.sb("ws", [P, KD, P], ctx)
    gate = core.sb("gate", [P, 4, T], ctx)
    rows = core.sb("rowsB", [P, 2 * D + KD * P], ctx)
    ln_w, ln_b, b_s = rows[:, 0:D], rows[:, D:2 * D], rows[:, 2 * D:]
    zs = core.sb("zs", [P, 2, 512], ctx)
    tmp = core.sb("tmp", [P, 2, T], ctx)
    ssq = core.sb("ssq", [P, TT, GROUPS], ctx)
    bn = core.sb("bn", [P, TT, 2, 6], ctx)
    mv = core.sb("mv", [P, TT, 2], ctx)
    merged = v[:, :, :].rearrange("p t n -> p (t n)").rearrange("p (m t) -> p m t", t=T)
    zs_done, zs_used, y_done = sem("zs_done"), sem("zs_used"), sem("y_done")
    v_done, v_ready, u_done, root2_done, mv_done = sem("v_done"), sem("v_ready"), sem("u_done"), sem("root2_done"), sem("mv_done")
    sgu_done, yt_done, gate_done, merged_done = sem("sgu_done"), sem("yt_done"), sem("gate_done"), sem("merged_done")
    rows_in, res_in, gated = sem("rows_in"), sem("res_in"), sem("gated")
    v_norm, merged_a = sem("v_norm"), sem("merged_a")

    source = mixer_slabs(core)
    tok = [(t, hh) for hh in (0, 1) for t in range(TT)]
    merge_tiles = [(n, m) for n, hh in MERGE_SLABS for m in range(4 * hh, 4 * hh + 4)]
    core.banks.begin([("z", *k) for k in tok] + [("v", *k) for k in tok] + [("u", m) for m in range(KD)]
                     + [("ada", s) for s in range(4, 12)]
                     + [("yt", m) for m in range(KD)] + [("mx", g) for g in range(KD)]
                     + merge_tiles + [("wo", m) for m in range(KD)])
    tile_no = {k: n for n, k in enumerate(merge_tiles)}
    with nc.Block() as block:
        @block.sync
        def _(sp):
            sp.dma_start(ws[:, :, :], I["wsT"].rearrange("g j i -> j g i")).then_inc(rows_in, 16)
            sp.dma_start(rows[:, :], bcast_rows(I["rowsB"], 2 * D + KD * P)).then_inc(rows_in, 16)
            for n, key in enumerate(MIXER_SLABS[SLOTS:]):
                load_slab(core, sp, key, source[key])
                if n == 0:
                    sp.dma_start(core.x[:, :, :], I["xT"].rearrange("(k p) n -> p k n", p=P)).then_inc(res_in, 16)

        @block.tensor
        def _(pe):
            prev = None

            def begin(key):
                nonlocal prev
                core.slabs.filled(pe, key)
                read, prev = (core.slabs.done(prev) if prev else None), key
                return read

            def by_feature(name, s, src, m0=0):
                read = begin((name, s))
                w = core.slab((name, s), KD, 512)
                for m in range(4):
                    key = (name, 4 * s + m)
                    core.banks.vacant(pe, key)
                    product(pe, core.ps(key)[:, :], [w[:, k, m * P:(m + 1) * P] for k in range(KD)],
                            [src[:, k, 0:T] for k in range(KD)], read if m == 0 else None)\
                        .then_inc(core.banks.put(key), 1)

            for name in ("z", "v"):
                for s in (0, 1):
                    read = begin((name, s))
                    w = core.slab((name, s), KD, 512)
                    for t in range(TT):
                        key = (name, t, s)
                        core.banks.vacant(pe, key)
                        product(pe, core.ps(key)[:, :], [a.xm[:, k, t * P:(t + 1) * P] for k in range(KD)],
                                [w[:, k, :] for k in range(KD)], read if t == 0 else None)\
                            .then_inc(core.banks.put(key), 1)
            for s in (0, 1):
                by_feature("u", s, a.xm)
            for s in range(4, 12):
                read = begin(("ada", s))
                core.banks.vacant(pe, ("ada", s))
                w = core.slab(("ada", s), KD, 512)
                for m in range(4):
                    last = product(pe, core.ps(("ada", s))[:, 2 * m:2 * m + 2],
                                   [w[:, k, m * P:(m + 1) * P] for k in range(KD)],
                                   [a.c[:, k, :] for k in range(KD)], read if m == 0 else None)
                last.then_inc(core.banks.put(("ada", s)), 1)
            pe.wait_ge(y_done, 1)
            for m in range(KD):
                core.banks.vacant(pe, ("yt", m))
                for t in range(TT):
                    last = pe.transpose(core.ps(("yt", m))[:, t * P:(t + 1) * P], a.y[:, t, m * P:(m + 1) * P],
                                        core.c("ident"))
                last.then_inc(core.banks.put(("yt", m)), 1)
            pe.wait_ge(rows_in, 32)
            pe.wait_ge(v_ready, TT)
            for g in range(KD):
                core.banks.vacant(pe, ("mx", g))
                for c in range(TT):
                    last = pe.matmul(core.ps(("mx", g))[:, c * P:(c + 1) * P], v[:, c, g * P:(g + 1) * P],
                                     ws[:, g, :], start=True, stop=True)
                last.then_inc(core.banks.put(("mx", g)), 1)
            for hh in (0, 1):
                by_feature("ga", hh, a.xm)
                pe.wait_ge(yt_done, KD)
                by_feature("pa", hh, yt)
                by_feature("gb", hh, a.xm)
                pe.wait_ge(sgu_done, KD)
                by_feature("pb", hh, u)
            pe.wait_ge(merged_done, KD)
            for s in (0, 1):
                by_feature("wo", s, merged)
            pe.drain().then_inc(core.slabs.done(("wo", 1)), 1)

        @block.scalar
        def _(act):
            for n, (t, hh) in enumerate(tok):
                core.banks.filled(act, ("z", t, hh))
                if n >= 2:
                    act.wait_ge(zs_used, n - 1)
                act.activation(zs[:, n % 2, :], core.ps(("z", t, hh))[:, :], ACT.Silu)\
                   .then_inc(core.banks.done(("z", t, hh)), 1)
                act.drain().then_inc(zs_done, 1)
            for n, (t, hh) in enumerate(tok):
                core.banks.filled(act, ("v", t, hh))
                act.activation(v[:, t, hh * 512:hh * 512 + 512], core.ps(("v", t, hh))[:, :], ACT.Gelu_apprx_tanh)\
                   .then_inc(core.banks.done(("v", t, hh)), 1)
                act.drain().then_inc(v_done, 1)
            for m in range(KD):
                core.banks.filled(act, ("u", m))
                act.activation(u[:, m, :], core.ps(("u", m))[:, :], ACT.Gelu_apprx_tanh)\
                   .then_inc(core.banks.done(("u", m)), 1)
            act.drain().then_inc(u_done, 1)
            act.wait_ge(gated, 2 * TT)
            for t in range(TT):
                for g in range(GROUPS):
                    act.activation(tmp[:, 0, 0:256], a.y[:, t, g * 256:(g + 1) * 256], ACT.Square,
                                   accum_out=ssq[:, t, g:g + 1])
                    act.drain()
            act.activation(ssq[:, :, :], ssq[:, :, :], ACT.Sqrt, scale=1.0 / 256, bias=core.c("eps6"))
            act.wait_ge(mv_done, 1)
            act.activation(mv[:, :, 1:2], mv[:, :, 1:2], ACT.Sqrt, bias=core.c("eps6"))
            act.drain().then_inc(root2_done, 1)
            for m in range(KD):
                core.banks.filled(act, ("yt", m))
                act.activation(yt[:, m, :], core.ps(("yt", m))[:, :], ACT.Identity,
                               scale=core.v("ssd_norm_w", m)).then_inc(core.banks.done(("yt", m)), 1)
                act.drain().then_inc(yt_done, 1)
            k = 0
            for hh in (0, 1):
                for name in ("ga", "gb"):
                    if k:
                        act.wait_ge(merged_a, 4 * k)
                    for m in range(4 * hh, 4 * hh + 4):
                        core.banks.filled(act, (name, m))
                        act.activation(gate[:, m % 4, :], core.ps((name, m))[:, :], ACT.Sigmoid)\
                           .then_inc(core.banks.done((name, m)), 1)
                        act.drain().then_inc(gate_done, 1)
                    k += 1

        @block.vector
        def _(dve):
            for n, (t, hh) in enumerate(tok):
                dve.wait_ge(zs_done, n + 1)
                dst = a.y[:, t, hh * 512:hh * 512 + 512]
                dve.tensor_tensor(dst, dst, zs[:, n % 2, :], ALU.mult).then_inc(zs_used, 1)
                dve.drain().then_inc(gated, 1)
            for n, (t, hh) in enumerate(tok):
                dve.wait_ge(v_done, n + 1)
                dve.bn_stats(bn[:, t, hh, :], v[:, t, hh * 512:hh * 512 + 512])
            dve.drain()
            for t in range(TT):
                dve.bn_aggr(mv[:, t, :], bn[:, t, :, :].rearrange("p a b -> p (a b)"))
            dve.drain().then_inc(mv_done, 1)
            for s in range(4, 12):
                core.banks.filled(dve, ("ada", s))
                bias = core.v("ada_b", 4 * s, 4).unsqueeze(2).broadcast_to([P, 4, 2])
                dve.tensor_tensor(core.mod[:, 4 * s:4 * s + 4, :],
                                  core.ps(("ada", s))[:, 0:8].rearrange("p (m j) -> p m j", j=2), bias,
                                  ALU.add).then_inc(core.banks.done(("ada", s)), 1)
            dve.wait_ge(root2_done, 1)
            dve.reciprocal(ssq[:, :, :], ssq[:, :, :])
            dve.reciprocal(mv[:, :, 1:2], mv[:, :, 1:2])
            dve.drain()
            for t in range(TT):
                dst = a.y[:, t, :].rearrange("p (g f) -> p g f", g=GROUPS)
                dve.tensor_tensor(dst, dst, ssq[:, t, :].unsqueeze(2).broadcast_to([P, GROUPS, 256]), ALU.mult)
            dve.drain().then_inc(y_done, 1)
            for t in range(TT):
                dve.tensor_scalar(v[:, t, :], v[:, t, :], mv[:, t, 0:1], mv[:, t, 1:2], ALU.subtract, ALU.mult)
                dve.drain().then_inc(v_norm, 1)
            dve.wait_ge(u_done, 1)
            for g in range(KD):
                core.banks.filled(dve, ("mx", g))
                mixed = tmp[:, 1, :]
                dve.tensor_tensor(mixed.rearrange("p (c i) -> p c i", i=P),
                                  core.ps(("mx", g))[:, :].rearrange("p (c i) -> p c i", i=P),
                                  b_s[:, g * P:(g + 1) * P].unsqueeze(1).broadcast_to([P, TT, P]), ALU.add)\
                   .then_inc(core.banks.done(("mx", g)), 1)
                dve.drain()
                dve.tensor_tensor(u[:, g, :], u[:, g, :], mixed, ALU.mult)
                dve.drain().then_inc(sgu_done, 1)
            k = 0
            for hh in (0, 1):
                for name in ("pa", "pb"):
                    for m in range(4 * hh, 4 * hh + 4):
                        dve.wait_ge(gate_done, k + 1)
                        core.banks.filled(dve, (name, m))
                        k += 1
                        if name == "pa":
                            dve.tensor_tensor(merged[:, m, :], core.ps((name, m))[:, :], gate[:, m % 4, :], ALU.mult)\
                               .then_inc(core.banks.done((name, m)), 1)
                            dve.drain().then_inc(merged_a, 1)
                        else:
                            dve.tensor_tensor(tmp[:, 1, :], core.ps((name, m))[:, :], gate[:, m % 4, :], ALU.mult)\
                               .then_inc(core.banks.done((name, m)), 1)
                            dve.drain().then_inc(merged_a, 1)
                            dve.tensor_tensor(merged[:, m, :], merged[:, m, :], tmp[:, 1, :], ALU.add)
                            dve.drain().then_inc(merged_done, 1)
            dve.wait_ge(res_in, 16)
            for m in range(KD):
                core.banks.filled(dve, ("wo", m))
                dve.scalar_tensor_tensor(out=core.x[:, m, :], in0=core.ps(("wo", m))[:, :],
                                         scalar=core.mod[:, 2 * KD + m, 0:1], in1=core.x[:, m, :],
                                         op0=ALU.mult, op1=ALU.add).then_inc(core.banks.done(("wo", m)), 1)

        @block.gpsimd
        def _(pool):
            pool.wait_ge(rows_in, 32)
            for t in range(TT):
                pool.wait_ge(v_norm, t + 1)
                pool.tensor_tensor(v[:, t, :], v[:, t, :], ln_w, ALU.mult)
                pool.drain()
                pool.tensor_tensor(v[:, t, :], v[:, t, :], ln_b, ALU.add)
                pool.drain().then_inc(v_ready, 1)


GU = 6
PIECE_SIZE = KD // 2 * 512
IN_RING = SLOTS * SLAB // PIECE_SIZE
GU_PIECES = [(n, hh, e, kk) for e in (0, 1) for hh in (0, 1) for n in ("g", "u") for kk in (0, 1)]


def piece_source(I, key, at):
    n, hh, _, kk = key
    w = {"g": I["w_gate"], "u": I["w_up"], "d": I["w_down"]}[n]
    return w[bass.ds(at, 1), D // 2 * kk:D // 2 * (kk + 1), 512 * hh:512 * hh + 512].rearrange("a (k p) n -> p (a k) n", p=P)


def router(core, ctx, b):
    core.stage = "router_"
    nc, I = core.nc, core.ins
    sem = lambda n: core.sem(n, ctx)
    xf = core.sb("xf", [P, KD, T], ctx)
    gates = core.sb("gates", [P, TT, EXPERTS * CAP], ctx)
    sq = core.sb("sq", [P, 2, T], ctx)
    rstd = core.sb("rstd", [P, T], ctx)
    scale2 = core.sb("scale2", [P, KD], ctx)
    rw = core.sb("rw", [P, KD, EXPERTS], ctx)
    aff = core.sb("aff", [P, TT, EXPERTS], ctx)
    top = core.sb("top", [P, TT], ctx)
    den = core.sb("den", [P, TT], ctx)
    pos = core.sb("pos", [P, TT, EXPERTS], ctx)
    mask = core.sb("mask", [P, TT, EXPERTS], ctx)
    work = core.sb("work", [EXPERTS, T], ctx)
    best = core.sb("best", [EXPERTS, 8], ctx)
    names = ["rw_in", "sq_done", "sq_used", "root_done", "scaled", "xf_done", "top_done", "exp_done", "aff_done",
             "mask_done", "masked_done", "pick_done", "gates_done"]
    rw_in, sq_done, sq_used, root_done, scaled, xf_done, top_done, exp_done, aff_done, mask_done, masked_done, \
        pick_done, gates_done = (sem(n) for n in names)
    PAIRS = EXPERTS // 2
    core.slabs.begin([])
    core.banks.begin(["rms", "logits"] + [("xt", t, hh) for t in range(TT) for hh in (0, 1)]
                     + ["aff", "mask", "pos"] + [("put", p) for p in range(PAIRS)])
    with nc.Block() as block:
        @block.sync
        def _(sp):
            sp.dma_start(rw[:, :, :], w_tiles(I["router_w"], 0, D, 0, EXPERTS)).then_inc(rw_in, 16)
            for slot, key in enumerate(GU_PIECES[:GU]):
                dst = core.ring[:, :, :].rearrange("p a b -> p (a b)")[:, slot * PIECE_SIZE:(slot + 1) * PIECE_SIZE]
                sp.dma_start(dst.rearrange("p (k n) -> p k n", k=KD // 2), piece_source(I, key, key[2]))\
                  .then_inc(core.pieces.full[slot], 16)

        @block.tensor
        def _(pe):
            core.banks.vacant(pe, "rms")
            for k in range(KD):
                pe.wait_ge(sq_done, k + 1)
                last = pe.matmul(core.ps("rms")[:, :], core.c("mean_d"), sq[:, k % 2, :], start=k == 0, stop=k == KD - 1)
                if k < KD - 1:
                    last.then_inc(sq_used, 1)
            last.then_inc(core.banks.put("rms"), 1)
            pe.wait_ge(xf_done, KD)
            pe.wait_ge(rw_in, 16)
            core.banks.vacant(pe, "logits")
            for t in range(TT):
                last = product(pe, core.ps("logits")[:, t * EXPERTS:(t + 1) * EXPERTS],
                               [xf[:, k, t * P:(t + 1) * P] for k in range(KD)], [rw[:, k, :] for k in range(KD)])
            last.then_inc(core.banks.put("logits"), 1)
            for t in range(TT):
                for hh in (0, 1):
                    core.banks.vacant(pe, ("xt", t, hh))
                    for m in range(4):
                        last = pe.transpose(core.ps(("xt", t, hh))[:, m * P:(m + 1) * P],
                                            xf[:, 4 * hh + m, t * P:(t + 1) * P], core.c("ident"))
                    last.then_inc(core.banks.put(("xt", t, hh)), 1)
            pe.wait_ge(aff_done, 1)
            core.banks.vacant(pe, "aff")
            for t in range(TT):
                last = pe.transpose(core.ps("aff")[0:EXPERTS, t * P:(t + 1) * P], aff[:, t, :], core.c("ident"))
            last.then_inc(core.banks.put("aff"), 1)
            pe.wait_ge(mask_done, 1)
            core.banks.vacant(pe, "mask")
            for t in range(TT):
                last = pe.transpose(core.ps("mask")[:, t * EXPERTS:(t + 1) * EXPERTS], work[:, t * P:(t + 1) * P],
                                    core.c("ident")[0:EXPERTS, 0:EXPERTS])
            last.then_inc(core.banks.put("mask"), 1)
            pe.wait_ge(masked_done, 1)
            core.banks.vacant(pe, "pos")
            for t in range(TT):
                last = product(pe, core.ps("pos")[:, t * EXPERTS:(t + 1) * EXPERTS],
                               [core.c("ones")] * t + [core.c("tri_f")], [mask[:, j, :] for j in range(t + 1)])
            last.then_inc(core.banks.put("pos"), 1)
            pe.wait_ge(gates_done, TT)
            for p in range(PAIRS):
                core.banks.vacant(pe, ("put", p))
                for t in range(TT):
                    last = pe.transpose(core.ps(("put", p))[:, t * P:(t + 1) * P], gates[:, t, p * P:(p + 1) * P],
                                        core.c("ident"))
                last.then_inc(core.banks.put(("put", p)), 1)

        @block.scalar
        def _(act):
            for k in range(KD):
                if k >= 2:
                    act.wait_ge(sq_used, k - 1)
                act.activation(sq[:, k % 2, :], core.x[:, k, :], ACT.Square).then_inc(sq_done, 1)
            core.banks.filled(act, "rms")
            act.activation(rstd[:, :], core.ps("rms")[:, :], ACT.Sqrt, bias=core.c("eps6"))\
               .then_inc(core.banks.done("rms"), 1)
            act.drain().then_inc(root_done, 1)
            for k in range(KD):
                act.wait_ge(scaled, k + 1)
                act.activation(xf[:, k, :], xf[:, k, :], ACT.Identity, bias=core.mod[:, 3 * KD + k, 0:1])\
                   .then_inc(xf_done, 1)
            act.wait_ge(top_done, 1)
            for t in range(TT):
                act.activation(aff[:, t, :], aff[:, t, :], ACT.Exp, bias=top[:, t:t + 1], accum_out=den[:, t:t + 1])
            act.drain().then_inc(exp_done, 1)
            for t in range(TT):
                for hh in (0, 1):
                    core.banks.filled(act, ("xt", t, hh))
                    act.activation(b.xf_tok[:, t, hh * 512:hh * 512 + 512], core.ps(("xt", t, hh))[:, :], ACT.Identity)\
                       .then_inc(core.banks.done(("xt", t, hh)), 1)
            for p in range(PAIRS):
                core.banks.filled(act, ("put", p))
                act.activation(b.put[:, p, :], core.ps(("put", p))[:, :], ACT.Identity)\
                   .then_inc(core.banks.done(("put", p)), 1)

        @block.vector
        def _(dve):
            dve.tensor_scalar(scale2[:, :], core.mod[:, 4 * KD:5 * KD, 0], 1.0, None, ALU.add)
            dve.drain()
            dve.tensor_tensor(scale2[:, :], scale2[:, :], core.v("norm2_w", 0, KD), ALU.mult)
            dve.wait_ge(root_done, 1)
            dve.reciprocal(rstd[:, :], rstd[:, :])
            dve.drain()
            for k in range(KD):
                dve.scalar_tensor_tensor(out=xf[:, k, :], in0=core.x[:, k, :], scalar=scale2[:, k:k + 1],
                                         in1=rstd[:, :], op0=ALU.mult, op1=ALU.mult).then_inc(scaled, 1)
            core.banks.filled(dve, "logits")
            dve.tensor_copy(aff[:, :, :], core.ps("logits")[:, 0:TT * EXPERTS].rearrange("p (t e) -> p t e", e=EXPERTS))\
               .then_inc(core.banks.done("logits"), 1)
            dve.drain()
            dve.tensor_reduce(top[:, :], aff[:, :, :], AX.X, ALU.max)
            dve.drain()
            dve.tensor_scalar(top[:, :], top[:, :], -1.0, None, ALU.mult)
            dve.drain().then_inc(top_done, 1)
            dve.wait_ge(exp_done, 1)
            dve.reciprocal(den[:, :], den[:, :])
            dve.drain()
            dve.tensor_tensor(aff[:, :, :], aff[:, :, :], den[:, :].unsqueeze(2).broadcast_to([P, TT, EXPERTS]), ALU.mult)
            dve.drain().then_inc(aff_done, 1)
            core.banks.filled(dve, "aff")
            dve.tensor_copy(work[:, :], core.ps("aff")[0:EXPERTS, :]).then_inc(core.banks.done("aff"), 1)
            for _ in range(CAP // 8):
                dve.drain()
                dve.max(best[:, :], work[:, :])
                dve.drain()
                dve.match_replace(work[:, :], best[:, :], work[:, :], -1.0)
            dve.drain()
            dve.tensor_scalar(work[:, :], work[:, :], 0.0, None, ALU.is_lt)
            dve.drain().then_inc(mask_done, 1)
            core.banks.filled(dve, "mask")
            dve.tensor_copy(mask[:, :, :], core.ps("mask")[:, 0:TT * EXPERTS].rearrange("p (t e) -> p t e", e=EXPERTS))\
               .then_inc(core.banks.done("mask"), 1)
            dve.drain().then_inc(masked_done, 1)
            core.banks.filled(dve, "pos")
            dve.tensor_tensor(pos[:, :, :], core.ps("pos")[:, 0:TT * EXPERTS].rearrange("p (t e) -> p t e", e=EXPERTS),
                              mask[:, :, :], ALU.mult).then_inc(core.banks.done("pos"), 1)
            dve.drain()
            over = lambda ap: ap.unsqueeze(2).broadcast_to([P, EXPERTS, CAP])
            for t in range(TT):
                dve.tensor_tensor(b.pick[:, t, :].rearrange("p (e s) -> p e s", s=CAP),
                                  core.c("slot").unsqueeze(1).broadcast_to([P, EXPERTS, CAP]), over(pos[:, t, :]),
                                  ALU.is_equal).then_inc(pick_done, 1)

        @block.gpsimd
        def _(pool):
            pool.wait_ge(aff_done, 1)
            for t in range(TT):
                pool.wait_ge(pick_done, t + 1)
                pool.tensor_tensor(gates[:, t, :].rearrange("p (e s) -> p e s", s=CAP),
                                   b.pick[:, t, :].rearrange("p (e s) -> p e s", s=CAP),
                                   aff[:, t, :].unsqueeze(2).broadcast_to([P, EXPERTS, CAP]), ALU.mult)\
                    .then_inc(gates_done, 1)


def experts(core, ctx, b):
    core.stage = "experts_"
    nc, I = core.nc, core.ins
    sem = lambda n: core.sem(n, ctx)
    PAIRS = EXPERTS // 2
    HK = KD // 2
    SIZE, LEAD = PIECE_SIZE, 3
    xg = core.sb("xg", [P, KD, 2, 2 * CAP], ctx)
    ht = core.sb("ht", [P, KD * CAP], ctx)
    hid = core.sb("hid", [CAP, 2, D], ctx)
    up = core.sb("up", [CAP, 512], ctx)
    part = core.sb("part", [CAP, 2, 512], ctx)
    y = core.sb("yslot", [P, D], ctx)
    high = core.sb("high", [P, HIGH + RAW - IN_RING, SIZE], ctx)
    raw_flat = core.ring[:, :, :].rearrange("p a b -> p (a b)")
    gu_raw, d_raw, halves = core.pieces.part(0, GU), core.pieces.part(GU, RAW), core.halves
    gu_banks, d_banks, xg_banks, sc_banks = (core.banks.part(2 * n, 2 * n + 2) for n in range(4))
    gu = [(n, hh, e) for e in (0, 1) for hh in (0, 1) for n in ("g", "u")]
    gu_pieces = GU_PIECES
    down = [("ht", 0), ("d", 0, 0), ("d", 1, 0), ("ht", 1), ("d", 0, 1), ("d", 1, 1)]
    d_pieces = [(*k, kk) for k in down if k[0] == "d" for kk in (0, 1)]
    xg_keys = [0, 1]
    gu_raw.begin(gu_pieces, reps=PAIRS)
    d_raw.begin(d_pieces, reps=PAIRS)
    halves.begin(gu_pieces, reps=PAIRS)
    gu_banks.begin(gu, reps=PAIRS)
    d_banks.begin(down, reps=PAIRS)
    xg_banks.begin(xg_keys, reps=PAIRS)
    sc_banks.begin(list(range(KD)), reps=PAIRS)
    at_slot = lambda n: high[:, HIGH + n - IN_RING, :] if n >= IN_RING else raw_flat[:, n * SIZE:(n + 1) * SIZE]
    raw = lambda key: at_slot(GU + d_raw.slot(key) if key[0] == "d" else gu_raw.slot(key))
    hi = lambda key: high[:, halves.slot(key), :]
    gu_ps = lambda e: core.bank[gu_banks.slot(e)]
    d_ps = lambda e: core.bank[2 + d_banks.slot(e)]
    xg_ps = lambda key: core.bank[4 + xg_banks.slot(key)]
    sc_ps = lambda m: core.bank[6 + sc_banks.slot(m)]
    xg_round, xg_done, slab_round, part_done, folded, silu_done, hid_done, ht_done, y_done = (
        sem(n) for n in ("xg_round", "xg_done", "slab_round", "part_done", "folded", "silu_done", "hid_done", "ht_done", "y_done"))
    gu_no = {e: n for n, e in enumerate(gu)}
    FOLDS = len(gu)

    plan = [(("g", 0, 0), 0), (("d", 0, 1), -1), (("u", 0, 0), 0), (("d", 1, 1), -1), (("g", 1, 0), 0), (("scatter",), -1),
            (("u", 1, 0), 0), (("g", 0, 1), 0), (("ht", 0), 0), (("u", 0, 1), 0), (("d", 0, 0), 0), (("g", 1, 1), 0),
            (("d", 1, 0), 0), (("u", 1, 1), 0), (("gather",), 1), (("ht", 1), 0)]
    rest_of_last = [(("d", 0, 1), -1), (("d", 1, 1), -1), (("scatter",), -1)]

    def ahead(split, n, i, last):
        if n < len(gu_pieces):
            split(n, i)
        elif not last:
            split(n - len(gu_pieces), i + 1)

    def pairs(eng, event, snap=lambda v, top: v):
        fixed = lambda v, top: v
        for e, off in plan:
            if off != -1:
                event(e, off, fixed, False)
        with eng.Fori(1, PAIRS - 1) as i:
            for e, off in plan:
                event(e, i + off if off else i, snap, False)
        for e, off in plan:
            if off != 1:
                event(e, PAIRS - 1 + off, fixed, True)
        for e, off in rest_of_last:
            event(e, PAIRS + off, fixed, True)

    def load(eng, kinds):
        def event(e, i, snap, last):
            if e[0] not in kinds:
                return
            n, hh, x = e
            at = snap(2 * i + x, EXPERTS - 1)
            for kk in (0, 1):
                key = (*e, kk)
                if type(i) is int and i == 0 and key in GU_PIECES[:GU]:
                    continue
                ring = d_raw if n == "d" else gu_raw
                ring.vacant(eng, key, i)
                eng.dma_start(raw(key).rearrange("p (k n) -> p k n", k=HK), piece_source(I, key, at))\
                   .then_inc(ring.put(key), 16)

        pairs(eng, event, lambda v, top: eng.snap(v, min_val=0, max_val=top))

    with nc.Block() as block:
        @block.sync
        def _(sp):
            load(sp, ("g", "u"))

        @block.tensor
        def _(pe):
            for free in gu_raw.free + d_raw.free + halves.free:
                pe.nop().then_inc(free, 1)
            to_tell = []

            def tell(mm):
                if to_tell:
                    mm.then_inc(to_tell.pop(0), 1)

            def event(e, i, snap, last):
                if e[0] == "gather":
                    col = snap(i * P, (PAIRS - 1) * P)
                    for key in xg_keys:
                        xg_banks.vacant(pe, key, i)
                        for m in range(4):
                            mm = product(pe, xg_ps(key)[:, m * P:(m + 1) * P],
                                         [b.xf_tok[:, t, (4 * key + m) * P:(4 * key + m + 1) * P] for t in range(TT)],
                                         [b.pick[:, t, bass.ds(col, P)] for t in range(TT)])
                        mm.then_inc(xg_banks.put(key), 1)
                elif e[0] == "scatter":
                    at = snap(i, PAIRS - 1)
                    pe.wait_ge(y_done, 4 * i + 4)
                    for m in range(KD):
                        sc_banks.vacant(pe, m, i)
                        pe.matmul(sc_ps(m)[:, :], y[:, m * P:(m + 1) * P], b.put[:, bass.ds(at, 1), :]
                                  .rearrange("p a n -> p (a n)"), start=True, stop=True).then_inc(sc_banks.put(m), 1)
                elif e[0] == "ht":
                    d_banks.vacant(pe, e, i)
                    pe.wait_ge(hid_done, 4 * i + 2 * e[1] + 2)
                    for k in range(KD):
                        mm = pe.matmul(d_ps(e)[:, k * CAP:(k + 1) * CAP], hid[:, e[1], k * P:(k + 1) * P],
                                       core.c("ident")[0:CAP, 0:CAP], start=True, stop=True)
                        if k < KD - 1:
                            tell(mm)
                    mm.then_inc(d_banks.put(e), 1)
                elif e[0] == "d":
                    d_banks.vacant(pe, e, i)
                    if e[1] == 0:
                        pe.wait_ge(ht_done, 2 * i + e[2] + 1)
                    for kk in (0, 1):
                        key = (*e, kk)
                        d_raw.filled(pe, key, i)
                        w = raw(key).rearrange("p (k n) -> p k n", k=HK)
                        for k in range(HK):
                            row = HK * kk + k
                            mm = pe.matmul(d_ps(e)[0:CAP, :], ht[:, row * CAP:(row + 1) * CAP], w[:, k, :],
                                           start=row == 0, stop=row == KD - 1)
                            if row < KD - 1:
                                tell(mm)
                        to_tell.append(d_raw.done(key))
                    mm.then_inc(d_banks.put(e), 1)
                else:
                    gu_banks.vacant(pe, e, i)
                    if e == ("g", 0, 0):
                        pe.wait_ge(xg_done, 2 * i + 2)
                    for kk in (0, 1):
                        key = (*e, kk)
                        halves.filled(pe, key, i)
                        w_hi, w_lo = (w.rearrange("p (k n) -> p k n", k=HK) for w in (hi(key), raw(key)))
                        for k in range(HK):
                            row = HK * kk + k
                            for low, w in enumerate((w_hi, w_lo)):
                                mm = pe.matmul(gu_ps(e)[:, :], r32(xg[:, row, e[2], :]), r32(w[:, k, :]),
                                               start=row == 0 and not low, stop=row == KD - 1 and low == 1)
                                if row < KD - 1 or not low:
                                    tell(mm)
                        to_tell.extend([gu_raw.done(key), halves.done(key)])
                    mm.then_inc(gu_banks.put(e), 1)

            event(("gather",), 0, lambda v, top: v, False)
            pairs(pe, event, lambda v, top: pe.snap(v, min_val=0, max_val=top))
            while to_tell:
                pe.wait_ge(y_done, 4 * PAIRS)
                pe.nop().then_inc(to_tell.pop(0), 1)

        @block.scalar
        def _(act):
            def round_piece(n, i):
                key = gu_pieces[n]
                gu_raw.filled(act, key, i)
                halves.vacant(act, key, i)
                act.activation(r32(hi(key)), raw(key), ACT.Identity).then_inc(slab_round, 1)

            def event(e, i, snap, last):
                if e[0] == "gather":
                    for key in xg_keys:
                        xg_banks.filled(act, key, i)
                        act.activation(r32(xg[:, 4 * key:4 * key + 4, :, 0:CAP]),
                                       xg_ps(key)[:, :].rearrange("p (m e s) -> p m e s", m=4, e=2), ACT.Identity)\
                           .then_inc(xg_round, 1)
                elif e[0] == "ht":
                    d_banks.filled(act, e, i)
                    act.activation(ht[:, :], d_ps(e)[:, :], ACT.Identity).then_inc(d_banks.done(e), 1)
                    act.drain().then_inc(ht_done, 1)
                elif e[0] == "d":
                    d_banks.filled(act, e, i)
                    act.activation(y[CAP * e[2]:CAP * e[2] + CAP, 512 * e[1]:512 * e[1] + 512], d_ps(e)[0:CAP, :], ACT.Identity)\
                       .then_inc(d_banks.done(e), 1)
                    act.drain().then_inc(y_done, 1)
                elif e[0] in ("g", "u"):
                    n = gu_no[e]
                    urgent = e[:2] == ("u", 1)
                    for kk in (0, 1)[:1 if urgent else 2]:
                        ahead(round_piece, 2 * n + kk + LEAD, i, last)
                    gu_banks.filled(act, e, i)
                    if n >= 2:
                        act.wait_ge(folded, FOLDS * i + n - 1)
                    act.activation(part[:, n % 2, :], gu_ps(e)[CAP:P, :], ACT.Identity).then_inc(part_done, 1)
                    if e[0] == "u":
                        act.wait_ge(folded, FOLDS * i + n)
                        dst = hid[:, e[2], 512 * e[1]:512 * e[1] + 512]
                        act.activation(dst, dst, ACT.Silu).then_inc(silu_done, 1)
                    if urgent:
                        ahead(round_piece, 2 * n + 1 + LEAD, i, last)

            for n in range(LEAD):
                round_piece(n, 0)
            event(("gather",), 0, None, False)
            pairs(act, event)

        @block.vector
        def _(dve):
            def rest_of_piece(n, i):
                key = gu_pieces[n]
                dve.wait_ge(slab_round, len(gu_pieces) * i + n + 1)
                dve.tensor_tensor(r32(raw(key)), raw(key), r32(hi(key)), ALU.subtract).then_inc(halves.put(key), 1)

            def event(e, i, snap, last):
                if e[0] == "gather":
                    for key in xg_keys:
                        dve.wait_ge(xg_round, 2 * i + key + 1)
                        dve.tensor_tensor(r32(xg[:, 4 * key:4 * key + 4, :, CAP:2 * CAP]),
                                          xg_ps(key)[:, :].rearrange("p (m e s) -> p m e s", m=4, e=2),
                                          r32(xg[:, 4 * key:4 * key + 4, :, 0:CAP]), ALU.subtract)\
                           .then_inc(xg_banks.done(key), 1)
                        dve.drain().then_inc(xg_done, 1)
                elif e[0] == "scatter":
                    for m in range(KD):
                        sc_banks.filled(dve, m, i)
                        dve.scalar_tensor_tensor(out=core.x[:, m, :], in0=sc_ps(m)[:, :],
                                                 scalar=core.mod[:, 5 * KD + m, 0:1], in1=core.x[:, m, :],
                                                 op0=ALU.mult, op1=ALU.add).then_inc(sc_banks.done(m), 1)
                elif e[0] in ("g", "u"):
                    n = gu_no[e]
                    urgent = e[:2] == ("u", 1)
                    for kk in (0, 1)[:1 if urgent else 2]:
                        ahead(rest_of_piece, 2 * n + kk + LEAD, i, last)
                    dve.wait_ge(part_done, FOLDS * i + n + 1)
                    gate = hid[:, e[2], 512 * e[1]:512 * e[1] + 512]
                    dve.tensor_tensor(gate if e[0] == "g" else up[:, :], gu_ps(e)[0:CAP, :], part[:, n % 2, :], ALU.add)\
                       .then_inc(gu_banks.done(e), 1)
                    dve.drain().then_inc(folded, 1)
                    if e[0] == "u":
                        dve.wait_ge(silu_done, 4 * i + n // 2 + 1)
                        dve.tensor_tensor(gate, gate, up[:, :], ALU.mult)
                        dve.drain().then_inc(hid_done, 1)
                    if urgent:
                        ahead(rest_of_piece, 2 * n + 1 + LEAD, i, last)

            for n in range(LEAD):
                rest_of_piece(n, 0)
            event(("gather",), 0, None, False)
            pairs(dve, event)

        @block.gpsimd
        def _(pool):
            load(pool, ("d",))
    core.banks.joined(gu_banks, d_banks, xg_banks, sc_banks)
    core.pieces.joined(gu_raw, d_raw)


def blocked(ap):
    return ap.rearrange("p (r n c) -> p n r c", n=NBLK, c=QB)


class Norm:

    def __init__(self, core, ctx, per, sq, before=0):
        self.core, self.per, self.sq, self.before = core, per, sq, before
        self.rstd = core.sb("norm_rstd", [P, T], ctx)
        self.summed, self.centred, self.squared, self.square_read, self.root, self.scaled, self.rounded, self.ready = core.norm_sems

    def at(self, i, n, k, each=KD):
        return i * (self.per * each) + (self.before + n) * each + k

    def tensor(self, pe, i, n, told=()):
        core, banks = self.core, self.core.banks
        banks.vacant(pe, ("mean", n), i)
        pe.wait_ge(self.summed, self.at(i, n, 1, 1))
        pe.matmul(core.ps(("mean", n))[:, :], core.c("mean_d"), self.rstd[:, :], start=True, stop=True)\
            .then_inc(banks.put(("mean", n)), 1)
        banks.vacant(pe, ("var", n), i)
        for k in range(KD):
            pe.wait_ge(self.squared, self.at(i, n, k + 1))
            last = pe.matmul(core.ps(("var", n))[:, :], core.c("mean_d"), self.sq[:, k % 2, :],
                             start=k == 0, stop=k == KD - 1)
            if k < KD - 1:
                last.then_inc(self.square_read, 1)
        last.then_inc(banks.put(("var", n)), 1)
        for sem in told:
            pe.nop().then_inc(sem, 1)

    def summand(self, dve, k):
        dve.drain()
        if k:
            dve.tensor_tensor(self.rstd[:, :], self.core.x[:, 0, :] if k == 1 else self.rstd[:, :], self.core.x[:, k, :], ALU.add)
        if k == KD - 1:
            dve.drain().then_inc(self.summed, 1)

    def vector(self, dve, i, n, gain, shift):
        core, banks = self.core, self.core.banks
        banks.filled(dve, ("mean", n), i)
        for k in range(KD):
            last = dve.tensor_tensor(core.x[:, k, :], core.x[:, k, :], core.ps(("mean", n))[:, :], ALU.subtract)
            if k == KD - 1:
                last.then_inc(banks.done(("mean", n)), 1)
                dve.drain().then_inc(self.centred, 1)
            else:
                last.then_inc(self.centred, 1)
        dve.wait_ge(self.root, self.at(i, n, 1, 1))
        dve.reciprocal(self.rstd[:, :], self.rstd[:, :])
        dve.drain()
        for k in range(KD):
            dve.scalar_tensor_tensor(out=core.x[:, k, :], in0=core.x[:, k, :], scalar=gain(k),
                                     in1=self.rstd[:, :], op0=ALU.mult, op1=ALU.mult).then_inc(self.scaled, 1)
            if k >= 2:
                self.rest(dve, i, n, k - 2, shift)
        self.rest(dve, i, n, KD - 2, shift)
        self.rest(dve, i, n, KD - 1, shift)

    def rest(self, dve, i, n, k, shift):
        x = self.core.x[:, k, :]
        dve.wait_ge(self.rounded, self.at(i, n, k + 1))
        dve.scalar_tensor_tensor(out=r32(x), in0=x, scalar=shift(k), in1=r32(self.core.x_hi[k]),
                                 op0=ALU.add, op1=ALU.subtract).then_inc(self.ready, 1)

    def scalar(self, act, i, n, shift):
        core, banks = self.core, self.core.banks
        for k in range(KD):
            act.wait_ge(self.centred, self.at(i, n, k + 1))
            if k >= 2:
                act.wait_ge(self.square_read, self.at(i, n, k - 1, KD - 1))
            act.activation(self.sq[:, k % 2, :], core.x[:, k, :], ACT.Square).then_inc(self.squared, 1)
        banks.filled(act, ("var", n), i)
        act.activation(self.rstd[:, :], core.ps(("var", n))[:, :], ACT.Sqrt, bias=core.c("eps5"))\
           .then_inc(banks.done(("var", n)), 1)
        act.drain().then_inc(self.root, 1)
        for k in range(KD):
            act.wait_ge(self.scaled, self.at(i, n, k + 1))
            act.activation(r32(core.x_hi[k]), core.x[:, k, :], ACT.Identity, bias=shift(k)).then_inc(self.rounded, 1)


def entry(core, ctx):
    core.stage = "entry_"
    nc = core.nc
    sem = lambda n: core.sem(n, ctx)
    norm = Norm(core, ctx, 1, core.sb("norm_sq", [P, 2, T], ctx))
    old = core.sb("old", [P, KD, T], ctx)
    sq_done, sq_used, root_done = sem("sq_done"), sem("sq_used"), sem("root_done")
    core.slabs.begin([])
    core.banks.begin(["rms", ("mean", 0), ("var", 0)])
    with nc.Block() as block:
        @block.tensor
        def _(pe):
            core.banks.vacant(pe, "rms")
            for k in range(KD):
                pe.wait_ge(sq_done, k + 1)
                last = pe.matmul(core.ps("rms")[:, :], core.c("mean_d"), norm.sq[:, k % 2, :], start=k == 0, stop=k == KD - 1)
                if k < KD - 1:
                    last.then_inc(sq_used, 1)
            last.then_inc(core.banks.put("rms"), 1)
            norm.tensor(pe, 0, 0)

        @block.scalar
        def _(act):
            for k in range(KD):
                if k >= 2:
                    act.wait_ge(sq_used, k - 1)
                act.activation(norm.sq[:, k % 2, :], core.x[:, k, :], ACT.Square).then_inc(sq_done, 1)
            core.banks.filled(act, "rms")
            act.activation(norm.rstd[:, :], core.ps("rms")[:, :], ACT.Sqrt, bias=core.c("eps6"))\
               .then_inc(core.banks.done("rms"), 1)
            act.drain().then_inc(root_done, 1)
            norm.scalar(act, 0, 0, lambda k: core.v("ln_in_b_2", k))

        @block.vector
        def _(dve):
            dve.wait_ge(root_done, 1)
            dve.reciprocal(norm.rstd[:, :], norm.rstd[:, :])
            dve.drain()
            for k in range(KD):
                dve.scalar_tensor_tensor(out=old[:, k, :], in0=core.x[:, k, :], scalar=core.v("final_norm_w", k),
                                         in1=norm.rstd[:, :], op0=ALU.mult, op1=ALU.mult)
            dve.drain()
            for k in range(KD):
                dve.tensor_copy(core.x[:, k, :].rearrange("p (n r c) -> p n r c", n=NBLK, c=QB), blocked(old[:, k, :]))
                norm.summand(dve, k)
            norm.vector(dve, 0, 0, lambda k: core.v("ln_in_g_2", k), lambda k: core.v("ln_in_b_2", k))


def layer_plan():

    def attention(kind, heads, lag, before=None):
        units = [(kind, h, n) for h in range(heads) for n in range(TT)]
        out = []
        for x in range(len(units) + lag + 1):
            if before and x < len(units) and x % TT == 0:
                out += before(x // TT)
            if x < len(units):
                out.append(("scores", *units[x]))
            if lag <= x < len(units) + lag:
                out.append(("turn", *units[x - lag]))
            if x > lag and (x - lag) % TT == 0:
                h = (x - lag) // TT - 1
                if kind == "df" and h:
                    out.append(("msq", "df", h - 1))
                out.append(("values", kind, h))
        return out + [("msq", "df", heads - 1)] * (kind == "df")

    plan = [("feat", "naq", m) for m in range(4)] + [("feat", "nak", m) for m in range(4)]
    plan += [("tok", "nav", t, hh) for hh in (0, 1) for t in range(TT)]
    plan += attention("na", NA_HEADS, 3)
    for w in ("dfq", "dfk"):
        for m in range(5):
            plan += [("feat", w, m)] * (m < 4) + [("swap", w, m - 1)] * (m > 0)
    plan += [("tok", "dfv", t, hh) for hh in (0, 1) for t in range(TT)]
    plan += attention("df", DF_HEADS, 3)
    plan += [("feat", "cq", m) for m in range(3)] + [("feat", "ckv", m) for m in range(2)] + [("kr",)]
    plan += [("msq", "q"), ("msq", "kv"), ("swap", "kr", 0)]
    plan += [("mv", t) for t in range(TT)]
    plan += attention("ml", MLA_HEADS, 3, lambda h: [("mq", h), ("mk", h), ("swap", "mq", h)])
    for b in range(3):
        plan += [("gate", b, m) for m in range(KD)] + [("branch", b, m) for m in range(KD)]
    plan += [("wo", m) for m in range(KD)] + [("norm", 0)]
    plan += [e for f in range(KF) for e in (("fg", f), ("fu", f))]
    return plan + [("fo", m) for m in range(KD)] + [("norm", 1)]


def numbered(events, wanted):
    chosen = [e for e in events if wanted(e)]
    return {e: n for n, e in enumerate(chosen)}, len(chosen)


def layers(core, ctx, out):
    core.stage = "layers_"
    nc, I = core.nc, core.ins
    sem = lambda n: core.sem(n, ctx)
    con2 = core.sb("con2", [P, NCON2], ctx)
    c2 = lambda n: con2[:, CON2[n][0]:CON2[n][0] + CON2[n][1]]
    x, x_hi, banks = core.x, core.x_hi, core.banks
    slabs, halves = core.pieces.part(0, PIECES), core.halves.part(0, HALVES)
    lv = core.sb("lv", [P, NLAYER], ctx)
    vec = lambda n, k=0: lv[:, LAYER[n][0] + k:LAYER[n][0] + k + 1]
    work = core.sb("work", [P, 24 * T], ctx)
    raw_at = lambda key: slabs.slot(key) * PIECE
    hi_at = lambda key: (PIECES + halves.slot(key)) * PIECE
    tiles = lambda a, n: work[:, a * T:(a + n) * T].rearrange("p (m t) -> p m t", t=T)
    proj = {n: tiles(4 * k, 4) for k, n in enumerate(("naq", "nak", "nav", "dfq", "dfk", "dfv"))}
    proj |= {"cq": tiles(0, 3), "ckv": tiles(3, 2), "kr": tiles(5, 1), "mv": tiles(8, 4), "mq": tiles(12, 2), "mk": tiles(14, 2)}
    merged, hidden = tiles(0, 8), tiles(0, KF)
    heads_out = core.sb("heads_out", [P, 3, 4, T], ctx)
    NP = 6
    p = core.sb("p", [P, NP, T], ctx)
    pt = core.sb("pt", [P, 2, TT, T], ctx)
    gates = pt[:, :, :, :].rearrange("p a b t -> p (a b) t")
    table = core.sb("table", [P, NA_HEADS, RUN], ctx)
    lamv = pt[:, 0, 0, 0:256].rearrange("p (a b n) -> p a b n", a=2, b=2)
    lam = core.sb("lam", [P, 8], ctx)
    side = table[:, :, :].rearrange("p h n -> p (h n)")[:, 0:2 * T].rearrange("p (a t) -> p a t", a=2)
    norm = Norm(core, ctx, 2, table[:, :, :].rearrange("p h n -> p (h n)")[:, 2 * T:4 * T].rearrange("p (a t) -> p a t", a=2), before=1)
    rot = norm.rstd

    plan = layer_plan()
    soft = [(*e[1:], j) for e in plan if e[0] == "scores" for j in range(1 + (e[1] == "df"))]
    NS = len(soft)
    soft_no = {s: n for n, s in enumerate(soft)}
    of_unit = lambda u: [soft_no[(*u, j)] for j in range(1 + (u[0] == "df"))]
    unit_no, UNITS = numbered(plan, lambda e: e[0] == "turn")
    head_no, HEADS_ALL = numbered(plan, lambda e: e[0] == "values")
    copy_no, COPIES = numbered(plan, lambda e: e[0] in ("feat", "tok", "kr", "mv", "mq", "mk"))
    swap_no, SWAPS = numbered(plan, lambda e: e[0] == "swap")
    scaled_no, SCALED = numbered(soft, lambda s: s[3] == 0)
    assert NS % NP == 0 and HEADS_ALL % 2 == 0
    SQUARES, LATENT = DF_HEADS + 5, 5
    negmax = core.sb("negmax", [P, NS], ctx)
    sums = core.sb("sums", [P, NS], ctx)
    recip = core.sb("recip", [P, NS], ctx)
    keys = []
    for e in plan:
        if e[0] == "scores":
            keys += [("scores", *e[1:], j) for j in range(1 + (e[1] == "df"))]
        else:
            keys += [("mean", e[1]), ("var", e[1])] if e[0] == "norm" else [e]
    banks.begin(keys, reps=LAYERS)

    def near(n):
        lo, hi = max(n - 1, 0), min(n + 1, NBLK - 1)
        return lo, hi - lo + 1

    W, G0 = "w_in_2", 3072 + QRANK + KVRANK + ROPE_D
    source = {(n, hh): (W, 0, D, 512 * k + 256 * hh, 256)
              for k, n in enumerate(("naq", "nak", "nav", "dfq", "dfk", "dfv")) for hh in (0, 1)}
    source |= {("cq", 0): (W, 0, D, 3072, 256), ("cq", 1): (W, 0, D, 3072 + 256, QRANK - 256),
               ("ckv", 0): (W, 0, D, 3072 + QRANK, KVRANK + ROPE_D)}
    source |= {("mla", 0): ("w_mla_2", 0, 3 * 768), ("mla", 1): ("w_mla_2", 3 * 768, 2 * D)}
    for b in range(3):
        source |= {("gate", b, c): (W, 0, D, G0 + b * D + 256 * c, 256) for c in range(4)}
        source |= {("branch", b, hh): ("w_branch_2", BR * b, BR, 512 * hh, 512) for hh in (0, 1)}
    source |= {("wo", c): ("w_out_2", 0, D, 256 * c, 256) for c in range(4)}
    source |= {("ffn", f): ("w_ffn_in_2", 0, D, 2 * P * f, 2 * P) for f in range(KF)}
    source |= {("fo", m, hh): ("w_ffn_out_2", FF // 2 * hh, FF // 2, P * m, P) for m in range(KD) for hh in (0, 1)}
    slabs.begin(list(source), reps=LAYERS)
    split_keys = [k for k in source if k[0] != "mla"]
    halves.begin(split_keys, reps=LAYERS)
    split_no = {k: n for n, k in enumerate(split_keys)}

    def slabs_of(e):
        if e[0] == "tok":
            return [(e[1], e[3])]
        if e[0] == "feat":
            return [(e[1], 0 if e[1] == "ckv" else e[2] // 2)]
        return {"gate": lambda: [("gate", e[1], e[2] // 2)], "branch": lambda: [("branch", e[1], e[2] // 4)],
                "wo": lambda: [("wo", e[1] // 2)], "fg": lambda: [("ffn", e[1])],
                "fo": lambda: [("fo", e[1], 0), ("fo", e[1], 1)]}.get(e[0], lambda: [])()

    due, placed = {}, 0
    for e in plan:
        for key in slabs_of(e):
            n = split_no[key]
            if n == placed and n + 1 < len(split_keys):
                placed += 1
                nxt = split_keys[n + 1]
                due.setdefault(("mq", 1) if nxt == ("gate", 0, 0) else e, []).append(nxt)
    assert sum(len(v) for v in due.values()) == len(split_keys) - 1

    def parts(key):
        _, _, rows, _, cols = source[key]
        k, out = rows // P, []
        for at in (hi_at(key), raw_at(key)):
            flat = core.ring[:, :, :].rearrange("p a b -> p (a b)")
            out.append(flat[:, at:at + k * cols].rearrange("p (k n) -> p k n", k=k))
        return out

    flat = core.ring[:, :, :].rearrange("p a b -> p (a b)")

    def whole(key, at):
        n = source[key][2] // P * source[key][4]
        return core.ring[:, :, :].rearrange("p a b -> p (a b)")[:, at:at + n]

    const_in, layer_done, params_in, table_in = sem("const_in"), sem("layer_done"), sem("params_in"), sem("table_in")
    lam_sums, lam_exps = sem("lam_sums"), sem("lam_exps")
    slab_round, heads_round, heads_split, merged_round, merged_split, hidden_round, hidden_split, joined = (
        sem(n) for n in ("slab_round", "heads_round", "heads_split", "merged_round", "merged_split", "hidden_round",
                         "hidden_split", "joined"))
    work_tile = lambda n: work[:, n * T:(n + 1) * T]
    heads_hi = lambda b, k: work_tile(8 + 4 * b + k)
    merged_hi = lambda m: work_tile(8 + m)

    def hidden_hi(f):
        if f < 12:
            return heads_out[:, f // 4, f % 4, :]
        return p[:, f - 12, :] if f < 12 + NP else pt[:, (f - 12 - NP) // TT, (f - 12 - NP) % TT, :]
    copied, rotated, max_done, exp_done, recip_done, scaled, combined, turned, head_done = (
        sem(n) for n in ("copied", "rotated", "max_done", "exp_done", "recip_done", "scaled", "combined", "turned", "head_done"))
    squared, root_done, latent_done, gate_done, branch_done, silu_done, hidden_done, out_done = (
        sem(n) for n in ("squared", "root_done", "latent_done", "gate_done", "branch_done", "silu_done", "hidden_done", "out_done"))

    def free_slot(eng, s, i):
        if s >= NP:
            banks.filled_too(eng, ("turn", *soft[s - NP][:3]), ("scores", *soft[s]), i)

    with nc.Block() as block:
        @block.sync
        def _(sp):
            with sp.Fori(0, LAYERS) as i:
                at = sp.snap(i, min_val=0, max_val=LAYERS - 1)

                def piece(key):
                    slabs.vacant(sp, key, i)
                    name, c0, cols = source[key][0], source[key][-2], source[key][-1]
                    if key[0] == "mla":
                        src = I[name][bass.ds(at, 1), :, c0:c0 + cols].rearrange("a p n -> p (a n)")
                        sp.dma_start(flat[:, raw_at(key):raw_at(key) + cols], src).then_inc(slabs.put(key), 16)
                        return
                    r0, rows = source[key][1:3]
                    src = I[name][bass.ds(at, 1), r0:r0 + rows, c0:c0 + cols].rearrange("a (k p) n -> p (a k) n", p=P)
                    sp.dma_start(whole(key, raw_at(key)).rearrange("p (k n) -> p k n", n=cols), src)\
                      .then_inc(slabs.put(key), 16)

                keys = list(source)
                for key in keys[:PIECES - 1]:
                    piece(key)
                sp.wait_ge(layer_done, i + 1)
                sp.dma_start(lv[:, :], I["layer_vec"][bass.ds(at, 1)].rearrange("a p n -> (a p) n")).then_inc(params_in, 16)
                sp.dma_start(pt[:, 0, 0, 0:256],
                             I["lam"][bass.ds(at, 1), :].broadcast_to([P, 256])).then_inc(params_in, 16)
                for r in range(ROWS):
                    lead = I["rpb"][bass.ds(at, 1), r * RPB_W:r * RPB_W + 1]
                    src = bass.AP(tensor=lead.tensor, offset=lead.offset, ap=[[1, QB], [RPB_H * RPB_W, NA_HEADS], [1, RUN]])
                    sp.dma_start(table[r * QB:(r + 1) * QB, :, :], src).then_inc(table_in, 16)
                for key in keys[PIECES - 1:]:
                    piece(key)
            sp.wait_ge(joined, KD)
            sp.dma_start(out.rearrange("(k p) n -> p k n", p=P), x[:, :, :]).then_inc(out_done, 16)
            sp.wait_ge(out_done, 16)

        @block.tensor
        def _(pe):
            xs = [x[:, k, :] for k in range(KD)]

            def layer(i):
                using, to_tell = [], []

                def need(*keys):
                    if using != list(keys):
                        for k in using:
                            to_tell.append(slabs.done(k))
                            if k[0] != "mla":
                                to_tell.append(halves.done(k))
                        using[:] = keys
                        for k in keys:
                            slabs.filled(pe, k, i) if k[0] == "mla" else halves.filled(pe, k, i)

                def chain(out, pairs, start=True, stop=True, fresh=None):
                    for k, (lhs, rhs) in enumerate(pairs):
                        if fresh is not None and k % 3 == 0:
                            pe.wait_ge(norm.ready, norm.at(i, fresh, k // 3 + 1))
                        last = pe.matmul(out, lhs, rhs, start=start and k == 0, stop=stop and k == len(pairs) - 1)
                        if to_tell and k < len(pairs) - 1:
                            last.then_inc(to_tell.pop(0), 1)
                    return last

                def emit(key, lhs, rhs, rows=P):
                    banks.vacant(pe, key, i)
                    chain(core.ps(key)[0:rows, :], list(zip(lhs, rhs))).then_inc(banks.put(key), 1)

                def three(lhs, lhs_lo, rhs, rhs_lo):
                    return [(r32(a), r32(b)) for k in range(len(lhs))
                            for a, b in ((lhs[k], rhs[k]), (lhs[k], rhs_lo[k]), (lhs_lo[k], rhs[k]))]

                def emit3(key, lhs, lhs_lo, rhs, rhs_lo, rows=P):
                    banks.vacant(pe, key, i)
                    fresh = {("feat", "naq", 0): -1, ("fg", 0): 0}.get(key)
                    chain(core.ps(key)[0:rows, :], three(lhs, lhs_lo, rhs, rhs_lo), fresh=fresh).then_inc(banks.put(key), 1)

                def by_feature(key, slab, c0, rhs, rhs_lo, cols=P):
                    need(slab)
                    hi, lo = parts(slab)
                    n = hi.shape[1]
                    emit3(key, [hi[:, k, c0:c0 + cols] for k in range(n)], [lo[:, k, c0:c0 + cols] for k in range(n)],
                          rhs, rhs_lo, rows=cols)

                def scores(kind, h, n):
                    q = slice(n * P, (n + 1) * P)
                    if kind == "na":
                        if (h, n) == (0, 0):
                            pe.wait_ge(copied, i * COPIES + copy_no[("feat", "nak", 3)] + 1)
                        lo, nb = near(n)
                        r = slice((h % 2) * 64, (h % 2) * 64 + 64)
                        key = ("scores", kind, h, n, 0)
                        banks.vacant(pe, key, i)
                        pe.matmul(core.ps(key)[:, 0:nb * P], proj["naq"][r, h // 2, q],
                                  proj["nak"][r, h // 2, lo * P:(lo + nb) * P], start=True, stop=True)\
                            .then_inc(banks.put(key), 1)
                    elif kind == "df":
                        if (h, n) == (0, 0):
                            pe.wait_ge(rotated, i * SWAPS + swap_no[("swap", "dfk", 3)] + 1)
                        for j in (0, 1):
                            r = slice(j * 64, j * 64 + 64)
                            emit(("scores", kind, h, n, j), [proj["dfq"][r, h, q]], [proj["dfk"][r, h, :]])
                    else:
                        if n == 0:
                            pe.wait_ge(copied, i * COPIES + copy_no[("mk", h)] + 1)
                            pe.wait_ge(rotated, i * SWAPS + swap_no[("swap", "mq", h)] + 1)
                        emit(("scores", kind, h, n, 0), [proj["mq"][0:96, h % 2, q]], [proj["mk"][0:96, h % 2, :]])

                def turn(kind, h, n):
                    key, s = ("turn", kind, h, n), soft_no[(kind, h, n, 0)]
                    if kind == "df":
                        pe.wait_ge(combined, i * (DF_HEADS * TT) + h * TT + n + 1)
                    else:
                        pe.wait_ge(scaled, i * SCALED + scaled_no[(kind, h, n, 0)] + 1)
                    banks.vacant(pe, key, i)
                    for b in range(near(n)[1] if kind == "na" else TT):
                        last = pe.transpose(core.ps(key)[:, b * P:(b + 1) * P], p[:, s % NP, b * P:(b + 1) * P], core.c("ident"))
                    last.then_inc(banks.put(key), 1)

                def values(kind, h):
                    key = ("values", kind, h)
                    turned_pt = pt[:, head_no[key] % 2]
                    v = proj[{"na": "nav", "df": "dfv", "ml": "mv"}[kind]]
                    if h == 0:
                        pe.wait_ge(copied, i * COPIES + copy_no[{"na": ("tok", "nav", 3, 1), "df": ("tok", "dfv", 3, 1),
                                                                 "ml": ("mv", 3)}[kind]] + 1)
                    pe.wait_ge(turned, i * UNITS + unit_no[("turn", kind, h, TT - 1)] + 1)
                    if kind == "na":
                        banks.vacant(pe, key, i)
                        for n in range(NBLK):
                            lo, nb = near(n)
                            last = product(pe, core.ps(key)[0:64, n * P:(n + 1) * P],
                                           [v[:, j, h * 64:h * 64 + 64] for j in range(lo, lo + nb)],
                                           [turned_pt[:, j, n * P:(n + 1) * P] for j in range(lo, lo + nb)])
                        last.then_inc(banks.put(key), 1)
                    else:
                        w = P if kind == "df" else 64
                        emit(key, [v[:, j, h * w:(h + 1) * w] for j in range(TT)], [turned_pt[:, j, :] for j in range(TT)], rows=w)

                for e in plan:
                    kind = e[0]
                    if kind == "feat":
                        slab = slabs_of(e)[0]
                        by_feature(e, slab, (e[2] - 2 * slab[1]) * P, x_hi, xs)
                    elif kind == "tok":
                        need((e[1], e[3]))
                        hi, lo = parts((e[1], e[3]))
                        tok = slice(e[2] * P, (e[2] + 1) * P)
                        banks.vacant(pe, e, i)
                        chain(core.ps(e)[:, 0:256], three([x_hi[k][:, tok] for k in range(KD)], [xs[k][:, tok] for k in range(KD)],
                                                          [hi[:, k, :] for k in range(KD)], [lo[:, k, :] for k in range(KD)]))\
                            .then_inc(banks.put(e), 1)
                    elif kind == "kr":
                        by_feature(e, ("ckv", 0), KVRANK + ROPE_D - 96, x_hi, xs, cols=96)
                    elif kind == "swap":
                        if e == ("swap", "dfq", 0):
                            pe.wait_ge(const_in, 16)
                        of = {"kr": ("kr",), "mq": ("mq", e[2])}.get(e[1], ("feat", e[1], e[2]))
                        pe.wait_ge(copied, i * COPIES + copy_no[of] + 1)
                        rows, mat = (P, "dswap") if of[0] == "feat" else (96, "mswap")
                        src = proj[e[1]][0:rows, e[2] % (4 if of[0] == "feat" else 2), :]
                        emit(e, [c2(mat)[0:rows, 0:rows]], [src], rows=rows)
                    elif kind == "scores":
                        scores(*e[1:])
                    elif kind == "turn":
                        turn(*e[1:])
                    elif kind == "values":
                        values(*e[1:])
                    elif kind == "msq" and e[1] == "df":
                        pe.wait_ge(squared, i * SQUARES + e[2] + 1)
                        emit(e, [c2("mean_h")], [norm.sq[:, e[2] % 2, :]])
                    elif kind == "msq":
                        first, n, mat = (0, 3, "mean_q") if e[1] == "q" else (3, 2, "mean_kv")
                        pe.wait_ge(squared, i * SQUARES + DF_HEADS + first + n)
                        emit(e, [c2(mat)] * n, [p[:, first + j, :] for j in range(n)])
                    elif kind in ("mv", "mq", "mk"):
                        need(("mla", 0), ("mla", 1))
                        if e == ("mv", 0):
                            pe.wait_ge(latent_done, i * LATENT + LATENT)
                        flat = core.ring[:, :, :].rearrange("p a b -> p (a b)")
                        wq, wkv = (flat[:, raw_at(("mla", j)):raw_at(("mla", j)) + n].rearrange("p (k n) -> p k n", k=k)
                                   for j, n, k in ((0, 3 * 768, 3), (1, 2 * D, 2)))
                        if kind == "mv":
                            emit(e, [proj["ckv"][:, k, e[1] * P:(e[1] + 1) * P] for k in range(2)],
                                 [wkv[:, k, :].rearrange("p (h c) -> p h c", c=128)[:, :, 64:128] for k in range(2)])
                        elif kind == "mq":
                            emit(e, [wq[:, k, e[1] * 96:(e[1] + 1) * 96] for k in range(3)], [proj["cq"][:, k, :] for k in range(3)], rows=96)
                        else:
                            emit(e, [wkv[:, k, e[1] * P:e[1] * P + 64] for k in range(2)], [proj["ckv"][:, k, :] for k in range(2)], rows=64)
                    elif kind == "gate":
                        by_feature(e, slabs_of(e)[0], (e[2] % 2) * P, x_hi, xs)
                    elif kind == "branch":
                        if e[2] == 0:
                            pe.wait_ge(heads_split, i * 12 + 4 * e[1] + 4)
                        by_feature(e, slabs_of(e)[0], (e[2] % 4) * P, [heads_hi(e[1], k) for k in range(4)],
                                   [heads_out[:, e[1], k, :] for k in range(4)])
                    elif kind == "wo":
                        if e[1] == 0:
                            pe.wait_ge(merged_split, i * KD + KD)
                        by_feature(e, slabs_of(e)[0], (e[1] % 2) * P, [merged_hi(m) for m in range(KD)],
                                   [merged[:, m, :] for m in range(KD)])
                    elif kind == "norm":
                        if e[1] == 1:
                            need()
                        norm.tensor(pe, i, e[1], to_tell if e[1] == 1 else ())
                    elif kind in ("fg", "fu"):
                        by_feature(e, ("ffn", e[1]), P * (kind == "fu"), x_hi, xs)
                    else:
                        if e[1] == 0:
                            pe.wait_ge(hidden_split, i * KF + KF)
                        banks.vacant(pe, e, i)
                        for hh in (0, 1):
                            need(("fo", e[1], hh))
                            hi, lo = parts(("fo", e[1], hh))
                            n = KF // 2
                            last = chain(core.ps(e)[:, :], three([hi[:, k, :] for k in range(n)], [lo[:, k, :] for k in range(n)],
                                                                 [hidden_hi(hh * n + k) for k in range(n)],
                                                                 [hidden[:, hh * n + k, :] for k in range(n)]),
                                         start=hh == 0, stop=hh == 1)
                        last.then_inc(banks.put(e), 1)

            with pe.Fori(0, LAYERS) as i:
                layer(i)

        @block.scalar
        def _(act):

            def layer(i):

                def round_slab(key):
                    slabs.filled(act, key, i)
                    halves.vacant(act, key, i)
                    act.activation(r32(whole(key, hi_at(key))), whole(key, raw_at(key)), ACT.Identity).then_inc(slab_round, 1)

                def round_hidden(f):
                    act.wait_ge(hidden_done, i * KF + f + 1)
                    act.activation(r32(hidden_hi(f)), hidden[:, f, :], ACT.Identity).then_inc(hidden_round, 1)

                round_slab(split_keys[0])
                act.wait_ge(lam_sums, i + 1)
                act.activation(lam[:, 2:4], lam[:, 0:2], ACT.Exp).then_inc(lam_exps, 1)
                act.wait_ge(params_in, i * 32 + 32)

                def copy(e, dst, rows=P, scale=1.0, cols=T):
                    banks.filled(act, e, i)
                    act.activation(dst, core.ps(e)[0:rows, 0:cols], ACT.Identity, scale=scale).then_inc(banks.done(e), 1)
                    act.drain().then_inc(copied, 1)

                for e in plan:
                    kind = e[0]
                    if e == ("fo", 0):
                        round_hidden(KF - 1)
                    for key in due.get(e, ()):
                        round_slab(key)
                    if kind == "tok":
                        copy(e, proj[e[1]][:, e[2], 256 * e[3]:256 * e[3] + 256], cols=256)
                    elif kind == "feat":
                        copy(e, proj[e[1]][:, e[2], :], scale=0.125 if e[1] == "naq" else 1.0)
                        if e[1] in ("cq", "ckv"):
                            n = e[2] + (3 if e[1] == "ckv" else 0)
                            if n == 0:
                                banks.filled_too(act, ("turn", "df", DF_HEADS - 1, TT - 1), e, i)
                            act.activation(p[:, n, :], proj[e[1]][:, e[2], :], ACT.Square).then_inc(squared, 1)
                    elif kind == "kr":
                        copy(e, proj["kr"][0:96, 0, :], rows=96)
                    elif kind == "mv":
                        copy(e, proj["mv"][:, e[1], :])
                    elif kind in ("mq", "mk"):
                        if e[1] >= 2:
                            banks.filled_too(act, ("scores", "ml", e[1] - 2, TT - 1, 0), e, i)
                        rows = 96 if kind == "mq" else 64
                        copy(e, proj[kind][0:rows, e[1] % 2, :], rows=rows)
                    elif kind == "scores":
                        for s in of_unit(e[1:]):
                            act.wait_ge(max_done, i * NS + s + 1)
                            key = ("scores", *soft[s])
                            if e[1] == "na":
                                w = near(e[3])[1] * P
                                act.activation(p[:, s % NP, 0:w], p[:, s % NP, 0:w], ACT.Exp, bias=negmax[:, s:s + 1],
                                               accum_out=sums[:, s:s + 1])
                            else:
                                banks.filled(act, key, i)
                                free_slot(act, s, i)
                                if s - soft_no[("ml", 0, 0, 0)] in range(NP):
                                    banks.filled_too(act, ("msq", "kv"), key, i)
                                act.activation(p[:, s % NP, :], core.ps(key)[:, :], ACT.Exp, bias=negmax[:, s:s + 1],
                                               scale=SCALE[e[1]], accum_out=sums[:, s:s + 1]).then_inc(banks.done(key), 1)
                            act.drain().then_inc(exp_done, 1)
                    elif kind == "turn":
                        banks.filled(act, e, i)
                        lo, nb = near(e[3]) if e[1] == "na" else (0, TT)
                        hd = head_no[("values", e[1], e[2])]
                        if e[3] == 0 and hd >= 2:
                            banks.filled_too(act, [k for k, n in head_no.items() if n == hd - 2][0], e, i)
                        act.activation(pt[:, hd % 2, lo:lo + nb, e[3] * P:(e[3] + 1) * P],
                                       core.ps(e)[:, 0:nb * P].rearrange("p (b q) -> p b q", q=P), ACT.Identity)\
                           .then_inc(banks.done(e), 1)
                        act.drain().then_inc(turned, 1)
                    elif kind == "values" and e[1] == "df":
                        banks.filled(act, e, i)
                        if e[2] >= 2:
                            banks.filled_too(act, ("msq", "df", e[2] - 2), e, i)
                        act.activation(norm.sq[:, e[2] % 2, :], core.ps(e)[:, :], ACT.Square).then_inc(squared, 1)
                        act.activation(heads_out[:, 1, e[2], :], core.ps(e)[:, :], ACT.Identity).then_inc(banks.done(e), 1)
                    elif kind == "msq":
                        banks.filled(act, e, i)
                        dst = {"q": side[:, 0, :], "kv": side[:, 1, :]}.get(e[1], side[:, e[-1] % 2, :] if e[1] == "df" else None)
                        if e[1] == "df" and e[2] >= 2:
                            act.wait_ge(head_done, i * HEADS_ALL + head_no[("values", "df", e[2] - 2)] + 1)
                        if e[1] != "df":
                            act.wait_ge(head_done, i * HEADS_ALL + head_no[("values", "df", DF_HEADS - 1)] + 1)
                        act.activation(dst, core.ps(e)[:, :], ACT.Sqrt, bias=core.c("eps6")).then_inc(banks.done(e), 1)
                        act.drain().then_inc(root_done, 1)
                    elif kind == "gate":
                        n = e[1] * KD + e[2]
                        if e[2] == 0:
                            act.wait_ge(head_done, i * HEADS_ALL + HEADS_ALL)
                            if e[1]:
                                banks.filled_too(act, ("branch", e[1] - 1, 0), e, i)
                            for k in range(4):
                                act.activation(r32(heads_hi(e[1], k)), heads_out[:, e[1], k, :], ACT.Identity)\
                                   .then_inc(heads_round, 1)
                        banks.filled(act, e, i)
                        if e[1]:
                            act.wait_ge(branch_done, i * (3 * KD) + n - KD + 1)
                        elif e[2] == 0:
                            banks.filled_too(act, ("values", "ml", MLA_HEADS - 1), e, i)
                        act.activation(gates[:, e[2], :], core.ps(e)[:, :], ACT.Sigmoid, bias=vec("b_gate_2", n))\
                           .then_inc(banks.done(e), 1)
                        act.drain().then_inc(gate_done, 1)
                    elif kind == "norm":
                        norm.scalar(act, i, e[1], lambda k: vec("ln1_b_2" if e[1] == 0 else "ln2_b_2", k))
                    elif kind == "fg":
                        banks.filled(act, e, i)
                        if e[1] >= 2:
                            act.wait_ge(hidden_done, i * KF + e[1] - 1)
                        act.activation(side[:, e[1] % 2, :], core.ps(e)[:, :], ACT.Silu).then_inc(banks.done(e), 1)
                        act.drain().then_inc(silu_done, 1)
                        if e[1]:
                            round_hidden(e[1] - 1)
                    elif kind == "branch" and e[1] == 2:
                        act.wait_ge(branch_done, i * (3 * KD) + 2 * KD + e[2] + 1)
                        act.activation(r32(merged_hi(e[2])), merged[:, e[2], :], ACT.Identity).then_inc(merged_round, 1)

            with act.Fori(0, LAYERS) as i:
                layer(i)

        @block.vector
        def _(dve):
            dve.wait_ge(const_in, 16)
            dve.nop().then_inc(layer_done, 1)

            def layer(i):
                def rest(tile, hi, rounded, count, done):
                    dve.wait_ge(rounded, count)
                    dve.tensor_tensor(r32(tile), tile, r32(hi), ALU.subtract).then_inc(done, 1)

                def rest_of_slab(key):
                    rest(whole(key, raw_at(key)), whole(key, hi_at(key)), slab_round, i * len(split_keys) + split_no[key] + 1,
                         halves.put(key))

                rest_of_slab(split_keys[0])
                dve.wait_ge(params_in, i * 32 + 32)
                dve.tensor_tensor(rot[:, 0:128].rearrange("p (a n) -> p a n", a=2), lamv[:, :, 0, :], lamv[:, :, 1, :], ALU.mult)
                dve.drain()
                dve.tensor_reduce(lam[:, 0:2], rot[:, 0:128].rearrange("p (a n) -> p a n", a=2), AX.X, ALU.add)
                dve.drain().then_inc(lam_sums, 1)
                dve.wait_ge(lam_exps, i + 1)
                dve.scalar_tensor_tensor(out=lam[:, 4:5], in0=lam[:, 3:4], scalar=lam[:, 2:3], in1=vec("lam_init"),
                                         op0=ALU.subtract, op1=ALU.subtract)
                dve.tensor_tensor(lam[:, 5:6], vec("diff_subln_g_2"), vec("one_less"), ALU.mult)
                dve.drain()

                recips, combines = [], []

                def maximum(u):
                    kind = u[0]
                    for s in of_unit(u):
                        key, col = ("scores", *soft[s]), negmax[:, s:s + 1]
                        banks.filled(dve, key, i)
                        if kind == "na":
                            _, h, n = u
                            lo, nb = near(n)
                            if (h, n) == (0, 0):
                                dve.wait_ge(table_in, i * (16 * ROWS) + 16 * ROWS)
                            free_slot(dve, s, i)
                            w = p[:, s % NP, 0:nb * P]
                            last = RUN - 1 - (lo - n + 1) * QB
                            bias = table[:, NA_HEADS - 1 - h, last:last + 1]
                            bias = bass.AP(tensor=bias.tensor, offset=bias.offset,
                                           ap=[list(bias.ap[0]), [-QB, nb], [-RPB_W, ROWS], [-1, QB]])
                            four = lambda ap: ap.rearrange("p (b r c) -> p b r c", b=nb, c=QB)
                            dve.tensor_tensor(four(w), four(core.ps(key)[:, 0:nb * P]), bias, ALU.add)\
                               .then_inc(banks.done(key), 1)
                            dve.drain()
                            mask = c2("near0" if n == 0 else "near2" if n == NBLK - 1 else "near1")
                            dve.tensor_tensor_reduce(w, w, mask, 1.0, NEG, ALU.add, ALU.max, col)
                            dve.drain()
                            dve.tensor_scalar(col, col, -1.0, None, ALU.mult)
                        else:
                            dve.tensor_reduce(col, core.ps(key)[:, :], AX.X, ALU.max)
                            dve.drain()
                            dve.tensor_scalar(col, col, -SCALE[kind], None, ALU.mult)
                        dve.drain().then_inc(max_done, 1)

                def invert(u):
                    for s in of_unit(u):
                        dve.wait_ge(exp_done, i * NS + s + 1)
                        dve.reciprocal(recip[:, s:s + 1], sums[:, s:s + 1])
                        dve.drain().then_inc(recip_done, 1)
                    if u[0] == "df":
                        dve.tensor_scalar(recip[:, s:s + 1], recip[:, s:s + 1], lam[:, 4:5], None, ALU.mult)
                        dve.drain()
                        combines.append(u)

                def combine(u):
                    a, b = of_unit(u)
                    dve.wait_ge(scaled, i * SCALED + scaled_no[(*u, 0)] + 1)
                    dve.scalar_tensor_tensor(out=p[:, a % NP, :], in0=p[:, b % NP, :], scalar=recip[:, b:b + 1],
                                             in1=p[:, a % NP, :], op0=ALU.mult, op1=ALU.add).then_inc(combined, 1)

                for e in plan:
                    kind = e[0]
                    if kind == "fo" and e[1] == 0:
                        rest(hidden[:, KF - 1, :], hidden_hi(KF - 1), hidden_round, i * KF + KF, hidden_split)
                    for key in due.get(e, ()):
                        rest_of_slab(key)
                    if kind == "gate" and e[2] == 0:
                        for k in range(4):
                            rest(heads_out[:, e[1], k, :], heads_hi(e[1], k), heads_round, i * 12 + 4 * e[1] + k + 1, heads_split)
                    if kind == "scores":
                        u = e[1:]
                        maximum(u)
                        before = list(combines)
                        if recips:
                            invert(recips.pop(0))
                        if before:
                            combine(combines.pop(0))
                        recips.append(u)
                    elif kind == "turn":
                        while e[1:] in recips:
                            invert(recips.pop(0))
                        while e[1:] in combines:
                            combine(combines.pop(0))
                    elif kind == "swap":
                        banks.filled(dve, e, i)
                        lo, hi, t = (0, P, "d") if e[1] in ("dfq", "dfk") else (64, 96, "m")
                        src = proj[e[1]][lo:hi, e[2] % (4 if t == "d" else 2), :]
                        dve.tensor_tensor(rot[lo:hi, :], core.ps(e)[lo:hi, :], c2(t + "sin")[lo:hi, :], ALU.mult)\
                           .then_inc(banks.done(e), 1)
                        dve.tensor_tensor(src, src, c2(t + "cos")[lo:hi, :], ALU.mult)
                        dve.drain()
                        for dst in ([proj["mk"][lo:hi, j, :] for j in (0, 1)] if e[1] == "kr" else [src]):
                            dve.tensor_tensor(dst, src, rot[lo:hi, :], ALU.add)
                        dve.drain().then_inc(rotated, 1)
                    elif kind == "values" and e[1] != "df":
                        banks.filled(dve, e, i)
                        h, b = e[2], 0 if e[1] == "na" else 2
                        dve.tensor_copy(heads_out[(h % 2) * 64:(h % 2) * 64 + 64, b, h // 2, :], core.ps(e)[0:64, :])\
                           .then_inc(banks.done(e), 1)
                        dve.drain().then_inc(head_done, 1)
                    elif kind == "msq":
                        n = {"q": DF_HEADS, "kv": DF_HEADS + 1}.get(e[1], e[-1])
                        dve.wait_ge(root_done, i * (DF_HEADS + 2) + n + 1)
                        root = side[:, n % 2, :]
                        dve.reciprocal(root, root)
                        dve.drain()
                        if e[1] == "df":
                            dst = heads_out[:, 1, e[2], :]
                            dve.scalar_tensor_tensor(out=dst, in0=dst, scalar=lam[:, 5:6], in1=root, op0=ALU.mult, op1=ALU.mult)
                            dve.drain().then_inc(head_done, 1)
                        else:
                            name, gain, k = ("cq", "mla_q_norm_g_2", 3) if e[1] == "q" else ("ckv", "mla_kv_norm_g_2", 2)
                            for j in range(k):
                                dst = proj[name][:, j, :]
                                dve.scalar_tensor_tensor(out=dst, in0=dst, scalar=vec(gain, j), in1=root, op0=ALU.mult, op1=ALU.mult)\
                                   .then_inc(latent_done, 1)
                    elif kind == "branch":
                        n = e[1] * KD + e[2]
                        dve.wait_ge(gate_done, i * (3 * KD) + n + 1)
                        banks.filled(dve, e, i)
                        dst = merged[:, e[2], :] if e[1] == 0 else rot[:, :]
                        dve.tensor_tensor(dst, core.ps(e)[:, :], gates[:, e[2], :], ALU.mult).then_inc(banks.done(e), 1)
                        dve.drain()
                        if e[1]:
                            dve.tensor_tensor(merged[:, e[2], :], merged[:, e[2], :], rot[:, :], ALU.add)
                            dve.drain()
                        dve.nop().then_inc(branch_done, 1)
                        if e[1] == 2:
                            for m in range(max(e[2] - 1, 0), e[2] + (e[2] == KD - 1)):
                                rest(merged[:, m, :], merged_hi(m), merged_round, i * KD + m + 1, merged_split)
                    elif kind in ("wo", "fo"):
                        banks.filled(dve, e, i)
                        dst = x[:, e[1], :]
                        dve.scalar_tensor_tensor(out=dst, in0=r32(dst), scalar=ALPHA, in1=core.ps(e)[:, :], op0=ALU.mult, op1=ALU.add)\
                           .then_inc(banks.done(e), 1)
                        dve.drain()
                        dve.scalar_tensor_tensor(out=dst, in0=r32(x_hi[e[1]]), scalar=ALPHA, in1=dst, op0=ALU.mult, op1=ALU.add)
                        norm.summand(dve, e[1])
                    elif kind == "norm":
                        norm.vector(dve, i, e[1], lambda k: vec("ln1_g_2" if e[1] == 0 else "ln2_g_2", k),
                                    lambda k: vec("ln1_b_2" if e[1] == 0 else "ln2_b_2", k))
                    elif kind == "fu":
                        dve.wait_ge(silu_done, i * KF + e[1] + 1)
                        banks.filled(dve, e, i)
                        dve.tensor_tensor(hidden[:, e[1], :], side[:, e[1] % 2, :], core.ps(e)[:, :], ALU.mult)\
                           .then_inc(banks.done(e), 1)
                        dve.drain().then_inc(hidden_done, 1)
                        if e[1]:
                            f = e[1] - 1
                            rest(hidden[:, f, :], hidden_hi(f), hidden_round, i * KF + f + 1, hidden_split)

            with dve.Fori(0, LAYERS) as i:
                layer(i)
                dve.drain().then_inc(layer_done, 1)
            dve.drain()
            for k in range(KD):
                dve.tensor_tensor(x[:, k, :], r32(x[:, k, :]), r32(x_hi[k]), ALU.add).then_inc(joined, 1)

        @block.gpsimd
        def _(pool):
            pool.dma_start(con2[:, :], I["con2"]).then_inc(const_in, 16)
            with pool.Fori(0, LAYERS) as i:
                for s in range(NS):
                    kind, h, n, j = soft[s]
                    if j:
                        continue
                    pool.wait_ge(recip_done, i * NS + s + 1)
                    w = near(n)[1] * P if kind == "na" else T
                    pool.tensor_tensor(p[:, s % NP, 0:w], p[:, s % NP, 0:w], recip[:, s:s + 1].broadcast_to([P, w]), ALU.mult)\
                        .then_inc(scaled, 1)


class Shared:
    pass


def build_program(nc, ins, out):
    ctx = ExitStack()
    with ctx:
        core = Core(nc, ctx, ins)
        a = Shared()
        with ExitStack() as mix_ctx:
            a.xm = core.sb("xm", [P, KD, T + CTX], mix_ctx)
            a.y = core.sb("y", [P, TT, D], mix_ctx)
            a.c = core.sb("c_in", [P, KD, 2], mix_ctx)
            a.skip = core.sb("skip", [P, HEADS], mix_ctx)
            with ExitStack() as scan_ctx:
                a.xtok = core.sb("xtok", [P, TT + CT, D], scan_ctx)
                a.btok = core.sb("btok", [P, TT + CT, GROUPS * STATE], scan_ctx)
                a.bc = core.sb("bc", [P, 2 * GROUPS, T], scan_ctx)
                a.dt = core.sb("dt", [P, TT + CT, 2 * HEADS], scan_ctx)
                a.dta = core.sb("dta", [P, TT + CT, 2 * HEADS], scan_ctx)
                with ExitStack() as c1:
                    front(core, c1, a)
                with ExitStack() as c2:
                    scan(core, c2, a)
            with ExitStack() as c3:
                mixer(core, c3, a)
        with ExitStack() as moe_ctx:
            b = Shared()
            b.xf_tok = core.sb("xf_tok", [P, TT, D], moe_ctx)
            b.pick = core.sb("pick", [P, TT, EXPERTS * CAP], moe_ctx)
            b.put = core.sb("put", [P, EXPERTS // 2, T], moe_ctx)
            with ExitStack() as c4:
                router(core, c4, b)
            with ExitStack() as c5:
                experts(core, c5, b)
        x_hi = core.sb("x_hi", [P, 5, T])
        flat = core.ring[:, :, :].rearrange("p a b -> p (a b)")
        at = (PIECES + HALVES) * PIECE
        core.x_hi = [x_hi[:, k, :] for k in range(5)] + [flat[:, at + k * T:at + (k + 1) * T] for k in range(3)]
        with ExitStack() as c6:
            entry(core, c6)
        with ExitStack() as c7:
            layers(core, c7, out)



def _permuted_tokens():
    t = np.arange(T).reshape(ROWS, NBLK, QB)
    return t.transpose(1, 0, 2).reshape(-1)


def _rope(half):
    inv = np.exp((-np.log(np.float32(500000.0)) * np.arange(half, dtype=np.float32) / np.float32(half)).astype(np.float32))
    ang = _permuted_tokens().astype(np.float32)[None, :] * inv.astype(np.float32)[:, None]
    return np.cos(ang).astype(np.float32), np.sin(ang).astype(np.float32)


def _rope_tables(first, half, period):
    cos, sin, swap = np.ones((P, T), np.float32), np.zeros((P, T), np.float32), np.zeros((P, P), np.float32)
    c, s = _rope(half)
    for at in range(first, P, period):
        if at + 2 * half > P:
            break
        for j in range(half):
            lo, hi = at + j, at + half + j
            cos[lo] = cos[hi] = c[j]
            sin[lo] = sin[hi] = s[j]
            swap[hi, lo] = -1.0
            swap[lo, hi] = 1.0
    return cos, sin, swap


def _near_masks():
    out = np.full((3, ROWS, QB, 3, ROWS, QB), NEG, np.float32)
    for k, n in enumerate((0, 1, NBLK - 1)):
        for c in range(QB):
            w0 = min(max(QB * n + c - WIN // 2, 0), GRID - WIN)
            for j in range(3):
                for c2 in range(QB):
                    if w0 <= QB * (n - 1 + j) + c2 < w0 + WIN:
                        out[k, :, c, j, :, c2] = 0.0
    return out.reshape(3, P, 3 * P)


def _constants():
    lower = np.tril(np.ones((P, P), np.float32))
    dcos, dsin, dswap = _rope_tables(0, 8, 64)
    mcos, msin, mswap = _rope_tables(64, 16, 64)
    near = _near_masks()
    ones = np.ones((P, P), np.float32)
    parts = {
        "ident": np.eye(P), "ones": ones, "mean_d": ones / D,
        "tri_f": lower.T, "tri_b": lower, "mask_f": np.where(lower.T > 0, 0.0, NEG), "mask_b": np.where(lower > 0, 0.0, NEG),
        "eps6": ones[:, :1] * EPS, "eps5": ones[:, :1] * LN_EPS,
        "slot": np.tile(np.arange(1, CAP + 1)[None, :], (P, 1)),
    }
    second = {
        "dcos": dcos, "dsin": dsin, "mcos": mcos, "msin": msin, "dswap": dswap, "mswap": mswap,
        "mean_q": ones / QRANK, "mean_kv": ones / KVRANK, "mean_h": ones / P,
        "near0": near[0][:, P:], "near1": near[1], "near2": near[2][:, :2 * P],
    }
    return parts, second


def _pack(parts):
    at, where = 0, {}
    for name, a in parts.items():
        where[name] = (at, a.shape[1])
        at += a.shape[1]
    return where, at


_FIRST, _SECOND = _constants()
CON, NCON = _pack(_FIRST)
CON2, NCON2 = _pack(_SECOND)

_VECS = [("ada_b", 48), ("norm1_w", 8), ("norm2_w", 8), ("final_norm_w", 8), ("conv_w", 48), ("conv_b", 16),
         ("ssd_norm_w", 8), ("ln_in_g_2", 8), ("ln_in_b_2", 8)]
_LAYER = [("ln1_g_2", 8), ("ln1_b_2", 8), ("ln2_g_2", 8), ("ln2_b_2", 8), ("b_gate_2", 24), ("diff_subln_g_2", 1),
          ("mla_q_norm_g_2", 3), ("mla_kv_norm_g_2", 2), ("lam_init", 1), ("one_less", 1)]


def _places(columns):
    at, where = 0, {}
    for name, n in columns:
        where[name] = (at, n)
        at += n
    return where, at


VEC, NVEC = _places(_VECS)
LAYER, NLAYER = _places(_LAYER)


def lay_out(x):
    f = lambda n: np.ascontiguousarray(np.asarray(x[n]))
    cols = lambda v: np.ascontiguousarray(v.reshape(-1, P).T)
    g = {
        "xT": np.ascontiguousarray(f("x")[0].T), "ctxT": np.ascontiguousarray(f("ctx")[0].T),
        "cT": np.ascontiguousarray(np.stack([f("c")[0], f("c_ctx")], axis=1)),
        "ada_w": f("ada_w")[0], "w_in": f("w_in")[0], "w_pa": f("w_pa")[0], "w_pb": f("w_pb")[0], "w_o": f("w_o")[0],
        "wsT": np.ascontiguousarray(f("w_s")[0].transpose(0, 2, 1)),
        "rowsA": np.concatenate([f("dt_bias")[0].reshape(-1), f("a_log")[0].reshape(-1), f("d_skip")[0]]),
        "rowsB": np.concatenate([f("sgu_ln_w")[0], f("sgu_ln_b")[0], f("b_s")[0].reshape(-1)]),
    }
    for n in ("w_in_2", "w_out_2", "w_ffn_out_2"):
        g[n] = f(n)
    g["w_ffn_in_2"] = f("w_ffn_in_2").reshape(LAYERS, D, 2, KF, P).transpose(0, 1, 3, 2, 4).reshape(LAYERS, D, 2 * FF)
    g["w_branch_2"] = f("w_branch_2").reshape(LAYERS, 3 * BR, D)
    tiled = lambda w: w.reshape(LAYERS, -1, P, w.shape[2]).transpose(0, 2, 1, 3).reshape(LAYERS, P, -1)
    g["w_mla_2"] = np.concatenate([tiled(f("w_mla_qb_2")), tiled(f("w_mla_kvb_2"))], axis=2)
    rpb = f("na_rpb_2").reshape(LAYERS, -1)
    edge = np.zeros((LAYERS, RPB_PAD), np.float32)
    g["rpb"] = np.concatenate([edge, rpb, edge], axis=1)[:, ::-1]
    g["lam"] = f("diff_lambda_2").reshape(LAYERS, 256)
    lam_init = [0.8 - 0.6 * float(np.exp(-0.3 * l)) for l in range(LAYERS)]
    extra = {"lam_init": lam_init, "one_less": [1.0 - v for v in lam_init]}
    g["layer_vec"] = np.stack([np.concatenate(
        [np.full((P, 1), extra[n][l], np.float32) if n in extra else cols(f(n)[l]) for n, _ in _LAYER], axis=1)
        for l in range(LAYERS)])
    for n in ("router_w", "w_gate", "w_up", "w_down"):
        g[n] = f(n)[0]
    g["vec"] = np.concatenate([cols(f(n)) for n, _ in _VECS], axis=1)
    g["con"] = np.concatenate([np.asarray(v, np.float32) for v in _FIRST.values()], axis=1)
    g["con2"] = np.concatenate([np.asarray(v, np.float32) for v in _SECOND.values()], axis=1)
    return {k: np.ascontiguousarray(v, dtype=v.dtype) for k, v in g.items()}


def kernel(**inputs):
    import concourse.bacc as bacc
    from concourse.bass_utils import run_bass_kernel_spmd

    nc = bacc.Bacc("TRN2", target_bir_lowering=False, num_devices=1)
    arrays = {"in_" + n: a for n, a in lay_out(inputs).items()}
    ins = {n[3:]: nc.dram_tensor(n, list(a.shape), mybir.dt.from_np(a.dtype), kind="ExternalInput").ap()
           for n, a in arrays.items()}
    out = nc.dram_tensor("out", [D, T], F32, kind="ExternalOutput").ap()
    build_program(nc, ins, out)
    result = run_bass_kernel_spmd(nc, [arrays], core_ids=[0])
    y = np.empty((1, T, D), np.float32)
    y[0, _permuted_tokens()] = result.results[0]["out"].T
    return y
```
